# Optimizing a Trainium2 kernel written in Bass

```python
import math
import jax
import jax.numpy as jnp
from jax import lax
import numpy as np

D_MODEL = 1024
BATCH = 1
SEQ = 1024
DEPTH = 1
DEC_BATCH = 8
DEC_SEQ = 1
PAST_LEN = 512
PAGE_SIZE = 128

H_A = 4
DH_QK = 64
DV_A = 2 * DH_QK
Q_BLOCK = 128
H_B = 4
DK_B = 128
DV_B = 128
CHUNK_B = 64
N_KEYS = 128
N_EXPERTS = N_KEYS * N_KEYS
H_P = 8
DK_P = 128
DK_P_HALF = DK_P // 2
TOPK_P = 16
PEER_BLOCK = 256
EPS = 1e-6
POOL_NUM = 5
POOL_DEN = 4

IN_SIZES = (H_A * 2 * DH_QK, H_A * 2 * DH_QK, H_A * DV_A,
            H_B * DK_B, H_B * DK_B, H_B * DV_B, H_B * DV_B,
            D_MODEL, D_MODEL)
N_IN = sum(IN_SIZES)

kernel_name = 'hybrid_diffattn_hgrn2_peer_step'

def _rmsnorm(x, g):
    xf = x.astype(jnp.float32)
    y = xf * lax.rsqrt(jnp.mean(xf * xf, axis=-1, keepdims=True) + EPS)
    return (y * g.astype(jnp.float32)).astype(x.dtype)

def _split_in(proj):
    B, T = proj.shape[:2]
    offs = np.cumsum(IN_SIZES)[:-1].tolist()
    qa, ka, va, qb, fb, ib, gb, gate_a, gate_b = jnp.split(proj, offs, axis=-1)
    return (qa.reshape(B, T, H_A, 2, DH_QK), ka.reshape(B, T, H_A, 2, DH_QK),
            va.reshape(B, T, H_A, DV_A), qb.reshape(B, T, H_B, DK_B),
            fb.reshape(B, T, H_B, DK_B), ib.reshape(B, T, H_B, DV_B),
            gb.reshape(B, T, H_B, DV_B), gate_a, gate_b)

def _diff_lambda(lq1, lk1, lq2, lk2, lam_init):
    f = jnp.float32
    return (jnp.exp(jnp.sum(lq1.astype(f) * lk1.astype(f)))
            - jnp.exp(jnp.sum(lq2.astype(f) * lk2.astype(f))) + lam_init)

def _diff_attn_core(q, k, v, q_pos, k_pos, lam):
    s = jnp.einsum('bqhcd,bkhcd->bhcqk', q, k).astype(jnp.float32) * (DH_QK ** -0.5)
    s = jnp.where(k_pos[None, :] <= q_pos[:, None], s, -jnp.inf)
    p = jax.nn.softmax(s, axis=-1)
    a = p[:, :, 0] - lam * p[:, :, 1]
    return jnp.einsum('bhqk,bkhd->bqhd', a.astype(v.dtype), v)

def _diff_attn_prompt(q, k, v, lam):
    B, T = q.shape[:2]
    nb = T // Q_BLOCK
    qb = q.reshape(B, nb, Q_BLOCK, H_A, 2, DH_QK).swapaxes(0, 1)
    k_pos = jnp.arange(T)

    def one_block(args):
        qi, bi = args
        q_pos = bi * Q_BLOCK + jnp.arange(Q_BLOCK)
        return _diff_attn_core(qi, k, v, q_pos, k_pos, lam)

    out = lax.map(one_block, (qb, jnp.arange(nb)))
    return out.swapaxes(0, 1).reshape(B, T, H_A, DV_A)

def _diff_post(o, subln_w, lam_init):
    B, T = o.shape[:2]
    return (_rmsnorm(o, subln_w) * (1.0 - lam_init)).reshape(B, T, H_A * DV_A)

def _hgrn_inputs(qb, fb, lb):
    f32 = jnp.float32
    q = jax.nn.silu(qb.astype(f32)) * (DK_B ** -0.5)
    f = lb + (1.0 - lb) * jax.nn.sigmoid(fb.astype(f32))
    return q, 1.0 - f, jnp.log(f)

def _hgrn_prompt(q, k, v, logf):
    B, T = q.shape[:2]
    nc = T // CHUNK_B

    def chunks(a):
        return a.reshape(B, nc, CHUNK_B, H_B, a.shape[-1]).transpose(1, 0, 3, 2, 4)

    causal = jnp.tril(jnp.ones((CHUNK_B, CHUNK_B), dtype=bool))[None, None, :, :, None]

    def step(S, xs):
        qc, kc, vc, lc = xs
        g = jnp.cumsum(lc, axis=2)
        decay = jnp.exp(jnp.where(causal, g[:, :, :, None, :] - g[:, :, None, :, :], -jnp.inf))
        A = jnp.einsum('bhtk,bhsk,bhtsk->bhts', qc, kc, decay)
        o = (jnp.einsum('bhtk,bhkv->bhtv', qc * jnp.exp(g), S)
             + jnp.einsum('bhts,bhsv->bhtv', A, vc))
        g_end = g[:, :, -1:, :]
        S = (jnp.exp(g_end[:, :, 0, :])[..., None] * S
             + jnp.einsum('bhsk,bhsv->bhkv', kc * jnp.exp(g_end - g), vc))
        return S, o

    S0 = jnp.zeros((B, H_B, DK_B, DV_B), jnp.float32)
    S, o = lax.scan(step, S0, (chunks(q), chunks(k), chunks(v.astype(jnp.float32)), chunks(logf)))
    return o.transpose(1, 0, 3, 2, 4).reshape(B, T, H_B, DV_B), S

def _hgrn_sample(q, k, v, logf, S0):
    def step(S, xs):
        qt, kt, vt, lt = xs
        S = jnp.exp(lt)[..., None] * S + kt[..., None] * vt[..., None, :]
        return S, jnp.einsum('bhk,bhkv->bhv', qt, S)

    tm = lambda a: a.swapaxes(0, 1)
    S, o = lax.scan(step, S0.astype(jnp.float32),
                    (tm(q), tm(k), tm(v.astype(jnp.float32)), tm(logf)))
    return o.swapaxes(0, 1), S

def _hgrn_post(o, gb, gnorm_w, dtype):
    B, T = o.shape[:2]
    y = _rmsnorm(o, gnorm_w) * jax.nn.silu(gb.astype(jnp.float32))
    return y.reshape(B, T, H_B * DV_B).astype(dtype)

def _merge(oa, ob, gate_a, gate_b, w_branch_a, w_branch_b, w_out):
    m = jax.nn.sigmoid(gate_a) * (oa @ w_branch_a) + jax.nn.sigmoid(gate_b) * (ob @ w_branch_b)
    return m @ w_out

def _peer(x, w_query, sub_keys, expert_u, expert_v):
    shp = x.shape
    xt = x.reshape(-1, D_MODEL)
    n = xt.shape[0]
    nb = -(-n // PEER_BLOCK)
    xt = jnp.pad(xt, ((0, nb * PEER_BLOCK - n), (0, 0))).reshape(nb, PEER_BLOCK, D_MODEL)

    def one_block(xb):
        q = (xb @ w_query).reshape(PEER_BLOCK, H_P, 2, DK_P_HALF)
        s = jnp.einsum('thcd,hcnd->thcn', q, sub_keys).astype(jnp.float32)
        s1, i1 = lax.top_k(s[:, :, 0], TOPK_P)
        s2, i2 = lax.top_k(s[:, :, 1], TOPK_P)
        comb = (s1[..., :, None] + s2[..., None, :]).reshape(PEER_BLOCK, H_P, TOPK_P * TOPK_P)
        cs, ci = lax.top_k(comb, TOPK_P)
        e1 = jnp.take_along_axis(i1, ci // TOPK_P, axis=-1)
        e2 = jnp.take_along_axis(i2, ci % TOPK_P, axis=-1)
        idx = e1 * N_KEYS + e2
        w = jax.nn.softmax(cs, axis=-1)
        u = expert_u[idx]
        a = jax.nn.gelu(jnp.einsum('td,thkd->thk', xb, u).astype(jnp.float32), approximate=False)
        v = expert_v[idx]
        return jnp.einsum('thk,thkd->td', (w * a).astype(xb.dtype), v)

    out = lax.map(one_block, xt).reshape(-1, D_MODEL)[:n]
    return out.reshape(shp)

def setup_inputs(seed: int = 0) -> dict:
    key = jax.random.key(seed)
    ks = jax.random.split(key, 24)

    def nrm(k, shape, scale):
        return jax.random.normal(k, shape, jnp.float32) * scale

    n_pages = PAST_LEN // PAGE_SIZE
    n_used = DEC_BATCH * n_pages
    n_phys = (n_used * POOL_NUM + POOL_DEN - 1) // POOL_DEN
    perm = jax.random.permutation(ks[5], n_phys)
    page_table = perm[:n_used].reshape(DEC_BATCH, n_pages).astype(jnp.int32)
    return {
        'x_prompt': nrm(ks[0], (BATCH, SEQ, D_MODEL), 1.0),
        'x_sample': nrm(ks[1], (DEC_BATCH, DEC_SEQ, D_MODEL), 1.0),
        'cache_k': nrm(ks[2], (DEPTH, n_phys, PAGE_SIZE, H_A, 2, DH_QK), 1.0),
        'cache_v': nrm(ks[3], (DEPTH, n_phys, PAGE_SIZE, H_A, DV_A), 1.0),
        'state_hgrn': nrm(ks[4], (DEPTH, DEC_BATCH, H_B, DK_B, DV_B), 0.3),
        'page_table': page_table,
        'norm1_w': 1.0 + nrm(ks[6], (DEPTH, D_MODEL), 0.02),
        'w_in': nrm(ks[7], (DEPTH, D_MODEL, N_IN), D_MODEL ** -0.5),
        'lambda_q1': nrm(ks[8], (DEPTH, DH_QK), 0.1),
        'lambda_k1': nrm(ks[9], (DEPTH, DH_QK), 0.1),
        'lambda_q2': nrm(ks[10], (DEPTH, DH_QK), 0.1),
        'lambda_k2': nrm(ks[11], (DEPTH, DH_QK), 0.1),
        'subln_w': 1.0 + nrm(ks[12], (DEPTH, DV_A), 0.02),
        'lb_param': nrm(ks[13], (DEPTH + 1, H_B * DK_B), 0.1),
        'gnorm_w': 1.0 + nrm(ks[14], (DEPTH, DV_B), 0.02),
        'w_branch_a': nrm(ks[15], (DEPTH, H_A * DV_A, D_MODEL), (H_A * DV_A) ** -0.5),
        'w_branch_b': nrm(ks[16], (DEPTH, H_B * DV_B, D_MODEL), (H_B * DV_B) ** -0.5),
        'w_out': nrm(ks[17], (DEPTH, D_MODEL, D_MODEL), D_MODEL ** -0.5),
        'norm2_w': 1.0 + nrm(ks[18], (DEPTH, D_MODEL), 0.02),
        'w_query': nrm(ks[19], (DEPTH, D_MODEL, H_P * DK_P), D_MODEL ** -0.5),
        'sub_keys': nrm(ks[20], (DEPTH, H_P, 2, N_KEYS, DK_P_HALF), DK_P_HALF ** -0.5),
        'expert_u': nrm(ks[21], (DEPTH, N_EXPERTS, D_MODEL), D_MODEL ** -0.5),
        'expert_v': nrm(ks[22], (DEPTH, N_EXPERTS, D_MODEL), 0.5),
        'norm_f_w': 1.0 + nrm(ks[23], (D_MODEL,), 0.02),
    }

def reference(x_prompt, x_sample, cache_k, cache_v, state_hgrn, page_table,
              norm1_w, w_in, lambda_q1, lambda_k1, lambda_q2, lambda_k2, subln_w,
              lb_param, gnorm_w, w_branch_a, w_branch_b, w_out, norm2_w,
              w_query, sub_keys, expert_u, expert_v, norm_f_w):
    n_dec, n_pages = page_table.shape
    past = n_pages * cache_k.shape[2]
    dec_len = x_sample.shape[1]
    lb_all = jnp.cumsum(jax.nn.softmax(lb_param.astype(jnp.float32), axis=0), axis=0)
    hp, hs = x_prompt, x_sample
    kp_l, vp_l, sp_l, ks_l, vs_l, ss_l = [], [], [], [], [], []
    for l in range(DEPTH):
        lam_init = 0.8 - 0.6 * math.exp(-0.3 * l)
        lam = _diff_lambda(lambda_q1[l], lambda_k1[l], lambda_q2[l], lambda_k2[l], lam_init)
        lb = lb_all[l].reshape(H_B, DK_B)

        qa, ka, va, qb, fb, ib, gb, ga, gbr = _split_in(_rmsnorm(hp, norm1_w[l]) @ w_in[l])
        oa = _diff_post(_diff_attn_prompt(qa, ka, va, lam), subln_w[l], lam_init)
        hq, hk, hlf = _hgrn_inputs(qb, fb, lb)
        ob, s_p = _hgrn_prompt(hq, hk, ib, hlf)
        ob = _hgrn_post(ob, gb, gnorm_w[l], hp.dtype)
        hp = hp + _merge(oa, ob, ga, gbr, w_branch_a[l], w_branch_b[l], w_out[l])
        hp = hp + _peer(_rmsnorm(hp, norm2_w[l]), w_query[l], sub_keys[l], expert_u[l], expert_v[l])
        kp_l.append(ka)
        vp_l.append(va)
        sp_l.append(s_p.astype(state_hgrn.dtype))

        qa_s, ka_s, va_s, qb_s, fb_s, ib_s, gb_s, ga_s, gbr_s = _split_in(_rmsnorm(hs, norm1_w[l]) @ w_in[l])
        k_past = cache_k[l, page_table].reshape(n_dec, past, H_A, 2, DH_QK)
        v_past = cache_v[l, page_table].reshape(n_dec, past, H_A, DV_A)
        k_all = jnp.concatenate([k_past, ka_s.astype(k_past.dtype)], axis=1)
        v_all = jnp.concatenate([v_past, va_s.astype(v_past.dtype)], axis=1)
        q_pos = past + jnp.arange(dec_len)
        k_pos = jnp.arange(past + dec_len)
        oa_s = _diff_post(_diff_attn_core(qa_s, k_all, v_all, q_pos, k_pos, lam), subln_w[l], lam_init)
        hq_s, hk_s, hlf_s = _hgrn_inputs(qb_s, fb_s, lb)
        ob_s, s_s = _hgrn_sample(hq_s, hk_s, ib_s, hlf_s, state_hgrn[l])
        ob_s = _hgrn_post(ob_s, gb_s, gnorm_w[l], hs.dtype)
        hs = hs + _merge(oa_s, ob_s, ga_s, gbr_s, w_branch_a[l], w_branch_b[l], w_out[l])
        hs = hs + _peer(_rmsnorm(hs, norm2_w[l]), w_query[l], sub_keys[l], expert_u[l], expert_v[l])
        ks_l.append(ka_s)
        vs_l.append(va_s)
        ss_l.append(s_s.astype(state_hgrn.dtype))

    y_prompt = _rmsnorm(hp, norm_f_w)
    y_sample = _rmsnorm(hs, norm_f_w)
    return (y_prompt, y_sample, jnp.stack(kp_l), jnp.stack(vp_l), jnp.stack(sp_l),
            jnp.stack(ks_l), jnp.stack(vs_l), jnp.stack(ss_l))


_drawn_inputs = setup_inputs


def setup_inputs(seed=0):
    import zlib

    import numpy as np

    out = dict(_drawn_inputs(seed))
    spreads = {}
    factors = {'lambda_k1': 4.538, 'lambda_q2': 4.932, 'gnorm_w': 2.967, 'norm_f_w': 2.904}
    for name, (base, spread) in spreads.items():
        noise = np.random.default_rng([zlib.crc32(name.encode()), seed]).standard_normal(out[name].shape)
        drawn = base * np.exp(spread * noise) if base else spread * noise
        out[name] = jnp.asarray(drawn.astype(out[name].dtype))
    for name, factor in factors.items():
        out[name] = (out[name] * factor).astype(out[name].dtype)
    return out
```

```python
import math
from contextlib import ExitStack

import concourse.bass as bass
from concourse import mybir

ALU = mybir.AluOpType
ACT = mybir.ActivationFunctionType
AX_X = mybir.AxisListType.X
F32 = mybir.dt.float32
I32 = mybir.dt.int32
U32 = mybir.dt.uint32

P = 128
D = 1024
SEQ = 1024
NS = 8
T = SEQ + NS
NP = SEQ // P
NT = NP + 1
KD = D // P
H = 4
DH = 64
DV = 128
PAGE = 128
PAGES = 4
EPS = 1e-6
LAM_INIT = 0.8 - 0.6 * math.exp(-0.3 * 0)
QK_SCALE = DH ** -0.5
HG_SCALE = 128 ** -0.5
CH = 32
NCH = SEQ // CH
HP = 8
NK = 128
TOPK = 16
SLOTS = HP * TOPK
RING = 8
NEG = -1e30
LOWEST = -3.0e38
CQ, CK, CHQ, CHF, CGA, CGB = 0, 4, 8, 12, 16, 24
N_QKF = 16
SLICES = ((0, 512), (512, 512), (SEQ, NS))


def rows(i):
    return P if i < NP else NS


class Chain:

    def __init__(self, eng, sem, base=0):
        self.eng, self.sem, self.base, self.n = eng, sem, base, 0

    def mark(self, ins):
        self.n += 1
        ins.then_inc(self.sem, 1)

    def wait(self):
        self.eng.wait_ge(self.sem, self.base + self.n)

    def __call__(self, ins):
        self.mark(ins)
        self.wait()


def hold(eng, sem, value, carrier):
    eng.wait_ge(sem, value)
    eng.sem_inc(carrier, 1)


class Memory:

    def __init__(self, nc, stack):
        self.nc, self.stack = nc, stack

    def sb(self, name, shape, dt=F32):
        return self.stack.enter_context(self.nc.sbuf_tensor(name, shape, dt))

    def ps(self, name, shape):
        return self.stack.enter_context(self.nc.psum_tensor(name, shape, F32))

    def sem(self, name):
        return self.stack.enter_context(self.nc.semaphore(name))


def bcast(ap, shape, axis):
    return ap.unsqueeze(axis).to_broadcast(shape)


def normalise(nc, mem, top, io, c):
    with ExitStack() as st:
        m = Memory(nc, st)
        xs = m.sb("xs", [P, NT, D])
        xn = m.sb("xn", [P, NT, D])
        ss = m.sb("ss", [P, NT])
        rstd = m.sb("rstd", [P, NT])
        norm1 = m.sb("norm1", [P, KD])
        lam_w = m.sb("lam_w", [P, 2, 2, DH])
        lam_p = m.sb("lam_p", [P, 2, DH])
        lam_s = m.sb("lam_s", [P, 2])
        lb_w = m.sb("lb_w", [P, 2, H])
        lb_m = m.sb("lb_m", [P, H])
        pages = m.sb("pages", [P, NS * PAGES], I32)
        pidx_i = m.sb("pidx_i", [P, 1], I32)
        pidx = m.sb("pidx", [P, 1])
        iota_i = m.sb("iota_i", [P, TOPK], I32)
        halves = m.sb("halves", [64, 2, NS])
        heads = m.sb("heads", [32, H, NS])
        tp = [m.ps(f"n_tp{b}", [P, KD, P]) for b in range(2)]

        tail_zeroed = top.sem("tail_zeroed")
        x_landed = top.sem("x_landed")
        small_landed = top.sem("small_landed")
        squares = top.sem("squares")
        mean_ready = top.sem("mean_ready")
        root_ready = top.sem("root_ready")
        xn_ready = top.sem("xn_ready")
        xn_turned = top.sem("xn_turned")
        xnt_stored = top.sem("xnt_stored")
        lam_sum = top.sem("lam_sum")
        lam_exp = top.sem("lam_exp")
        pool_chain = top.sem("norm_pool_chain")
        dve_chain = top.sem("norm_dve_chain")
        ident_ready = top.sem("ident_ready")
        masks_ready = top.sem("masks_ready")
        block = st.enter_context(nc.Block())

        @block.sync
        def _(sp):
            sp.dma_start(norm1[:], io["norm1"]).then_inc(small_landed, 16)
            sp.dma_start(lam_w[:].rearrange("p a b d -> p (a b d)"),
                         io["lam_w"].to_broadcast([P, 4 * DH])).then_inc(small_landed, 16)
            sp.dma_start(lb_w[:], io["lb_w"]).then_inc(small_landed, 16)
            sp.dma_start(c["subln"][:], io["subln"]).then_inc(small_landed, 16)
            sp.dma_start(c["gnorm"][:], io["gnorm"]).then_inc(small_landed, 16)
            sp.dma_start(pages[:], io["pages"].to_broadcast([P, NS * PAGES])).then_inc(small_landed, 16)
            sp.wait_ge(tail_zeroed, 1)
            sp.dma_start(xs[0:NS, NP, :], io["x"][SEQ:T, :]).then_inc(x_landed, 16)
            sp.dma_start(xs[:, 0:NP, :], io["x"][0:SEQ, :].rearrange("(t p) d -> p t d", p=P)
                         ).then_inc(x_landed, 16)

        @block.gpsimd
        def _(pool):
            link = Chain(pool, pool_chain)
            g = nc.gpsimd
            ident, cmask, bmask = c["ident"], c["cmask"], c["bmask"]
            link(g.memset(ident[:], 0.0))
            g.affine_select(out=ident[:], in_=ident[:], compare_op=ALU.not_equal, fill=1.0, base=0,
                            pattern=[[-1, P]], channel_multiplier=1).then_inc(ident_ready, 1)
            link(g.memset(cmask[:], 0.0))
            link(g.affine_select(out=cmask[:], in_=cmask[:], compare_op=ALU.is_ge, fill=NEG, base=0,
                                 pattern=[[-1, P]], channel_multiplier=1))
            link(g.memset(bmask[:], 1.0))
            link(g.affine_select(out=bmask[:], in_=bmask[:], compare_op=ALU.is_ge, fill=0.0, base=0,
                                 pattern=[[1, P]], channel_multiplier=-1))
            b3 = bmask[:].rearrange("p (a b) -> p a b", b=CH)
            link(g.affine_select(out=b3, in_=b3, compare_op=ALU.is_ge, fill=0.0, base=0,
                                 pattern=[[-CH, P // CH], [0, CH]], channel_multiplier=1))
            link(g.iota(iota_i[:], pattern=[[1, TOPK]], base=0, channel_multiplier=0))
            link(g.tensor_copy(c["iota"][:], iota_i[:]))
            link(g.iota(pidx_i[:], pattern=[[0, 1]], base=0, channel_multiplier=1))
            link(g.tensor_copy(pidx[:], pidx_i[:]))
            link(g.memset(c["pick"][:], 0.0))
            link(g.affine_select(out=c["pick"][:], in_=c["pick"][:], compare_op=ALU.not_equal, fill=1.0,
                                 base=0, pattern=[[-1, NS], [0, P]], channel_multiplier=1))
            link(g.memset(halves[:], 1.0))
            link(g.affine_select(out=halves[:], in_=halves[:], compare_op=ALU.is_ge, fill=0.0, base=0,
                                 pattern=[[-32, 2], [-H, NS]], channel_multiplier=1))
            link(g.affine_select(out=halves[:], in_=halves[:], compare_op=ALU.is_ge, fill=0.0, base=H - 1,
                                 pattern=[[32, 2], [H, NS]], channel_multiplier=-1))
            link(g.tensor_tensor(c["own_token"][:], halves[:, 0, :], halves[:, 1, :], ALU.add))
            link(g.memset(heads[:], 0.0))
            link(g.affine_select(out=heads[:], in_=heads[:], compare_op=ALU.not_equal, fill=1.0, base=0,
                                 pattern=[[-1, H], [-H, NS]], channel_multiplier=1))
            g.memset(c["zeros_i"][:], 0.0).then_inc(masks_ready, 1)

        @block.scalar
        def _(act):
            act.wait_ge(x_landed, 32)
            for i in range(NT):
                nc.scalar.activation(xn[:, i, :], xs[:, i, :], ACT.Square,
                                     accum_out=ss[:, i:i + 1]).then_inc(squares, 1)
            act.wait_ge(mean_ready, 1)
            nc.scalar.activation(rstd[:], ss[:], ACT.Sqrt).then_inc(root_ready, 1)
            act.wait_ge(lam_sum, 1)
            nc.scalar.activation(lam_s[:], lam_s[:], ACT.Exp).then_inc(lam_exp, 1)
            act.wait_ge(lam_sum, 2)
            nc.scalar.activation(lb_w[:], lb_w[:], ACT.Exp).then_inc(lam_exp, 1)

        @block.vector
        def _(dve):
            link = Chain(dve, dve_chain)
            v = nc.vector
            v.memset(xs[:, NP, :], 0.0).then_inc(tail_zeroed, 1)
            dve.wait_ge(small_landed, 6 * 16)
            link(v.tensor_tensor(lam_p[:], lam_w[:, 0], lam_w[:, 1], ALU.mult))
            v.tensor_reduce(lam_s[:], lam_p[:], AX_X, ALU.add).then_inc(lam_sum, 1)
            link(v.tensor_tensor(lb_m[:], lb_w[:, 0, :], lb_w[:, 1, :], ALU.max))
            v.tensor_tensor(lb_w[:], lb_w[:], bcast(lb_m[:], [P, 2, H], 1), ALU.subtract).then_inc(lam_sum, 1)
            link(v.tensor_scalar(c["subln"][:], c["subln"][:], 1.0 - LAM_INIT, None, ALU.mult))
            dve.wait_ge(squares, NT)
            link(v.tensor_scalar(ss[:], ss[:], 1.0 / D, EPS, ALU.mult, ALU.add))
            v.memset(c["zero1"][:], 0.0).then_inc(mean_ready, 1)
            dve.wait_ge(root_ready, 1)
            link(v.reciprocal(rstd[:], rstd[:]))
            v.tensor_tensor(xn[:], xs[:], bcast(rstd[:], [P, NT, D], 2), ALU.mult).then_inc(xn_ready, 1)
            for i in range(NT):
                dve.wait_ge(xn_turned, i + 1)
                v.tensor_tensor(c["xnt"][:, :, i * P:i * P + rows(i)], tp[i % 2][:, :, 0:rows(i)],
                                bcast(norm1[:], [P, KD, rows(i)], 2), ALU.mult).then_inc(xnt_stored, 1)
            dve.wait_ge(lam_exp, 1)
            link(v.tensor_tensor(c["neg_lam"][:], lam_s[:, 1:2], lam_s[:, 0:1], ALU.subtract))
            link(v.tensor_scalar(c["neg_lam"][:], c["neg_lam"][:], -LAM_INIT, None, ALU.add))
            link(v.memset(c["map_coef"][:], 1.0))
            link(v.tensor_copy(c["map_coef"][32:64, :], c["neg_lam"][32:64, :]))
            dve.wait_ge(lam_exp, 2)
            link(v.tensor_tensor(lb_m[:], lb_w[:, 0, :], lb_w[:, 1, :], ALU.add))
            link(v.reciprocal(lb_m[:], lb_m[:]))
            link(v.tensor_tensor(c["lb"][:], lb_w[:, 0, :], lb_m[:], ALU.mult))
            link(v.tensor_scalar(c["one_lb"][:], c["lb"][:], -1.0, 1.0, ALU.mult, ALU.add))
            dve.wait_ge(masks_ready, 1)
            link(v.tensor_scalar(c["cache_rows"][:], pages[:], float(PAGE), pidx[:, 0:1], ALU.mult, ALU.add))
            link(v.tensor_reduce(c["own_head"][:], heads[:], AX_X, ALU.add))
            link(v.tensor_tensor(c["sum_maps"][:], c["ident"][0:64, 0:32], c["ident"][0:64, 32:64], ALU.add))

        @block.tensor
        def _(pe):
            pe.wait_ge(ident_ready, 1)
            pe.wait_ge(xn_ready, 1)
            for i in range(NT):
                if i >= 2:
                    pe.wait_ge(xnt_stored, i - 1)
                for k in range(KD):
                    last = nc.tensor.transpose(tp[i % 2][:, k, :], xn[:, i, k * P:(k + 1) * P], c["ident"][:])
                last.then_inc(xn_turned, 1)


def project(nc, mem, top, io, c):
    qkf, vig, xnt, ident = c["qkf"], c["vig"], c["xnt"], c["ident"]
    with ExitStack() as st:
        m = Memory(nc, st)
        wt = [m.sb(f"wt{u}", [P, KD, P]) for u in range(2)]
        wn = m.sb("wn", [P, KD, 512])
        kst = [m.sb(f"kst{u}", [P, 512]) for u in range(2)]
        pt = [[m.ps(f"pt{u}_{s}", [P, 512]) for s in range(3)] for u in range(2)]
        pn = [m.ps(f"pn{u}", [P, 512]) for u in range(2)]

        wt_landed = [top.sem(f"wt_landed{u}") for u in range(2)]
        wt_used = [top.sem(f"wt_used{u}") for u in range(2)]
        cols_stored = [top.sem(f"cols_stored{u}") for u in range(2)]
        wn_landed = top.sem("wn_landed")
        rows_done = [top.sem(f"rows_done{u}") for u in range(2)]
        rows_stored = [top.sem(f"rows_stored{u}") for u in range(2)]
        tail_clear = top.sem("vig_tail_clear")
        k_saved = [top.sem(f"k_saved{u}") for u in range(2)]
        v_saved = top.sem("v_saved")
        sp_held = top.sem("p_sp_held")
        block = st.enter_context(nc.Block())
        n_rows = 3 * NT

        @block.sync
        def _(sp):
            for u in range(2):
                sp.dma_start(wt[u][:], io["w_t"][u]).then_inc(wt_landed[u], 16)
            sp.dma_start(wn[:], io["w_n"][0]).then_inc(wn_landed, 16)
            with sp.Fori(1, N_QKF // 2) as j:
                for u in range(2):
                    hold(sp, wt_used[u], j, sp_held)
                    sp.dma_start(wt[u][:], io["w_t"][bass.ds(2 * j + u, 1)].rearrange(
                        "a p k n -> (a p) k n")).then_inc(wt_landed[u], 16)
            for b in range(1, 3):
                for u in range(2):
                    sp.wait_ge(rows_done[u], (NT * b + 1 - u) // 2)
                sp.dma_start(wn[:], io["w_n"][b]).then_inc(wn_landed, 16)
            for u in range(2):
                sp.wait_ge(rows_stored[u], (NT + 1 - u) // 2)
            sp.dma_start(io["v_out"][0:SEQ, :].rearrange("(t p) n -> p t n", p=P), vig[:, 0, 0:NP, :]
                         ).then_inc(v_saved, 16)
            sp.dma_start(io["v_out"][SEQ:T, :], vig[0:NS, 0, NP, :]).then_inc(v_saved, 16)
            for i in range(NT):
                n = n_rows + i
                sp.wait_ge(rows_stored[n % 2], n // 2 + 1)
                src = kst[n % 2][:] if i < NP else c["k_new"][:]
                sp.dma_start(io["k_out"][i * P:i * P + rows(i), :], src).then_inc(k_saved[n % 2], 16)
            sp.wait_ge(v_saved, 32)
            for u in range(2):
                sp.wait_ge(k_saved[u], 16 * len([i for i in range(NT) if (n_rows + i) % 2 == u]))

        def store_cols(eng, copy, u):
            def one(j, first):
                eng.wait_ge(wt_used[u], j + 1)
                for s, (t0, n) in enumerate(SLICES):
                    last = copy(qkf[:, 0 + u, t0:t0 + n] if first else
                                qkf[:, bass.ds(2 * j + u, 1), t0:t0 + n].rearrange("p a t -> p (a t)"),
                                pt[u][s][:, 0:n])
                    last.then_inc(cols_stored[u], 1)
            one(0, True)
            with eng.Fori(1, N_QKF // 2) as j:
                one(j, False)

        def store_rows(eng, copy, u):
            if u == 0:
                eng.wait_ge(tail_clear, 1)
            else:
                eng.wait_ge(tail_clear, 1)
            for n in range(n_rows + NT + 1):
                if n % 2 != u:
                    continue
                i = n - n_rows
                eng.wait_ge(rows_done[u], n // 2 + 1)
                if i < 0:
                    dst = vig[0:rows(n % NT), n // NT, n % NT, :]
                elif i < NP:
                    dst = kst[u][:]
                    if i >= 2:
                        eng.wait_ge(k_saved[u], 16 * (i // 2))
                elif i == NP:
                    dst = c["k_new"][:]
                else:
                    dst = c["q_new"][:]
                copy(dst, pn[u][0:dst.shape[0], :]).then_inc(rows_stored[u], 1)

        @block.scalar
        def _(act):
            store_cols(act, nc.scalar.copy, 1)
            store_rows(act, nc.scalar.copy, 1)

        @block.vector
        def _(dve):
            nc.vector.memset(vig[:, :, NP, :], 0.0).then_inc(tail_clear, 1)
            store_cols(dve, nc.vector.tensor_copy, 0)
            store_rows(dve, nc.vector.tensor_copy, 0)

        @block.tensor
        def _(pe):
            def chunk(u, j, first):
                if not first:
                    pe.wait_ge(cols_stored[u], 3 * j)
                pe.wait_ge(wt_landed[u], 16 * (j + 1))
                for k in range(KD):
                    for s, (t0, n) in enumerate(SLICES):
                        last = nc.tensor.matmul(pt[u][s][:, 0:n], wt[u][:, k, :], xnt[:, k, t0:t0 + n],
                                                start=(k == 0), stop=(k == KD - 1))
                last.then_inc(wt_used[u], 1)
            for u in range(2):
                chunk(u, 0, True)
            with pe.Fori(1, N_QKF // 2) as j:
                for u in range(2):
                    chunk(u, j, False)
            for n in range(n_rows + NT + 1):
                u, i = n % 2, n - n_rows
                if n >= 2:
                    pe.wait_ge(rows_stored[u], n // 2)
                if i < 0:
                    pe.wait_ge(wn_landed, 16 * (n // NT + 1))
                    t = n % NT
                    for k in range(KD):
                        last = nc.tensor.matmul(pn[u][0:rows(t), :], xnt[:, k, t * P:t * P + rows(t)],
                                                wn[:, k, :], start=(k == 0), stop=(k == KD - 1))
                else:
                    if n == n_rows:
                        for w in range(2):
                            pe.wait_ge(cols_stored[w], 3 * N_QKF // 2)
                    t, c0 = (i, CK) if i < NT else (NP, CQ)
                    for h in range(H):
                        last = nc.tensor.transpose(pn[u][0:rows(t), h * P:(h + 1) * P],
                                                   qkf[:, c0 + h, t * P:t * P + rows(t)], ident[:])
                last.then_inc(rows_done[u], 1)


def attend_prompt(nc, mem, top, io, c):
    qkf, vig, ident, oat = c["qkf"], c["vig"], c["ident"], c["oat"]
    units = [(i, h) for i in range(NP) for h in range(H)]
    with ExitStack() as st:
        m = Memory(nc, st)
        prob = [[m.sb(f"prob{b}{k}", [P, SEQ]) for k in range(2)] for b in range(2)]
        probt = m.sb("probt", [P, SEQ])
        stat = {n: m.sb(f"at_{n}", [P, 2 * len(units)]) for n in ("top", "neg", "sum", "inv")}
        o_sb = m.sb("o_sb", [P, H, DV])
        o_sq = m.sb("o_sq", [P, H, DV])
        o_ss = m.sb("o_ss", [P, NP, H])
        sc = [m.ps(f"sc{k}", [P, SEQ]) for k in range(2)]
        pt = m.ps("at_pt", [P, SEQ])
        o_ps = m.ps("o_ps", [P, H, DV])
        ot_ps = m.ps("ot_ps", [P, H, P])

        scores_done = top.sem("at_scores_done")
        neg_ready = top.sem("at_neg_ready")
        exp_done = top.sem("at_exp_done")
        diff_ready = top.sem("at_diff_ready")
        turned = top.sem("at_turned")
        probt_ready = top.sem("at_probt_ready")
        pv_done = top.sem("at_pv_done")
        o_taken = top.sem("at_o_taken")
        ms_ready = top.sem("at_ms_ready")
        rms_ready = top.sem("at_rms_ready")
        on_ready = top.sem("at_on_ready")
        on_turned = top.sem("at_on_turned")
        oat_stored = top.sem("at_oat_stored")
        chain = top.sem("at_chain")
        block = st.enter_context(nc.Block())

        @block.tensor
        def _(pe):
            def scores(u):
                i, h = units[u]
                w = (i + 1) * P
                for k in range(2):
                    if u >= 1:
                        pe.wait_ge(exp_done, 2 * (u - 1) + k + 1)
                    for k0 in range(0, w, 512):
                        n = min(512, w - k0)
                        last = nc.tensor.matmul(sc[k][:, k0:k0 + n],
                                                qkf[k * DH:(k + 1) * DH, CQ + h, i * P:(i + 1) * P],
                                                qkf[k * DH:(k + 1) * DH, CK + h, k0:k0 + n],
                                                start=True, stop=True)
                    last.then_inc(scores_done, 1)

            def turn(u):
                i, h = units[u]
                pe.wait_ge(diff_ready, u + 1)
                if u >= 1:
                    pe.wait_ge(probt_ready, u)
                for b in range(i + 1):
                    last = nc.tensor.transpose(pt[:, b * P:(b + 1) * P], prob[u % 2][0][:, b * P:(b + 1) * P],
                                               ident[:])
                last.then_inc(turned, 1)

            def pv(u):
                i, h = units[u]
                pe.wait_ge(probt_ready, u + 1)
                if h == 0 and i >= 1:
                    pe.wait_ge(o_taken, i)
                for b in range(i + 1):
                    last = nc.tensor.matmul(o_ps[:, h, :], probt[:, b * P:(b + 1) * P],
                                            vig[:, 0, b, h * DV:(h + 1) * DV], start=(b == 0), stop=(b == i))
                last.then_inc(pv_done, 1)

            def turn_out(i):
                pe.wait_ge(on_ready, i + 1)
                if i >= 1:
                    pe.wait_ge(oat_stored, i)
                for h in range(H):
                    last = nc.tensor.transpose(ot_ps[:, h, :], o_sb[:, h, :], ident[:])
                last.then_inc(on_turned, 1)

            scores(0)
            for u in range(len(units)):
                if u + 1 < len(units):
                    scores(u + 1)
                turn(u)
                pv(u)
                if u % H == 0 and u:
                    turn_out(u // H - 1)
            turn_out(NP - 1)

        @block.scalar
        def _(act):
            def exps(u):
                w = (units[u][0] + 1) * P
                for k in range(2):
                    q = 2 * u + k
                    act.wait_ge(neg_ready, q + 1)
                    if u >= 2:
                        act.wait_ge(turned, u - 1)
                    nc.scalar.activation(prob[u % 2][k][:, 0:w], sc[k][:, 0:w], ACT.Exp, scale=QK_SCALE,
                                         bias=stat["neg"][:, q:q + 1],
                                         accum_out=stat["sum"][:, q:q + 1]).then_inc(exp_done, 1)

            def store(u):
                w = (units[u][0] + 1) * P
                act.wait_ge(turned, u + 1)
                if u >= 1:
                    act.wait_ge(pv_done, u)
                nc.scalar.copy(probt[:, 0:w], pt[:, 0:w]).then_inc(probt_ready, 1)

            def post(i):
                act.wait_ge(ms_ready, i + 1)
                nc.scalar.activation(o_ss[:, i, :], o_ss[:, i, :], ACT.Sqrt).then_inc(rms_ready, 1)
                act.wait_ge(on_turned, i + 1)
                nc.scalar.activation(oat[:, :, i * P:(i + 1) * P], ot_ps[:], ACT.Copy,
                                     scale=c["subln"][:, 0:1]).then_inc(oat_stored, 1)

            exps(0)
            for u in range(len(units)):
                if u + 1 < len(units):
                    exps(u + 1)
                store(u)
                if u % H == 0 and u:
                    post(u // H - 1)
            post(NP - 1)

        @block.vector
        def _(dve):
            link = Chain(dve, chain)
            v = nc.vector

            def tops(u):
                i, h = units[u]
                w = (i + 1) * P
                for k in range(2):
                    q = 2 * u + k
                    dve.wait_ge(scores_done, q + 1)
                    link(v.tensor_tensor(sc[k][:, i * P:w], sc[k][:, i * P:w], c["cmask"][:], ALU.add))
                    link(v.reduce_max(stat["top"][:, q:q + 1], sc[k][:, 0:w], AX_X))
                    v.tensor_scalar(stat["neg"][:, q:q + 1], stat["top"][:, q:q + 1], -QK_SCALE, None,
                                    ALU.mult).then_inc(neg_ready, 1)

            def differ(u):
                w = (units[u][0] + 1) * P
                a, b = prob[u % 2][0][:, 0:w], prob[u % 2][1][:, 0:w]
                q = 2 * u
                dve.wait_ge(exp_done, q + 2)
                link(v.reciprocal(stat["inv"][:, q:q + 2], stat["sum"][:, q:q + 2]))
                link(v.tensor_scalar(stat["inv"][:, q + 1:q + 2], stat["inv"][:, q + 1:q + 2],
                                     c["neg_lam"][:, 0:1], None, ALU.mult))
                link(v.tensor_scalar(a, a, stat["inv"][:, q:q + 1], None, ALU.mult))
                v.scalar_tensor_tensor(out=a, in0=b, scalar=stat["inv"][:, q + 1:q + 2], in1=a,
                                       op0=ALU.mult, op1=ALU.add).then_inc(diff_ready, 1)

            def post(i):
                dve.wait_ge(pv_done, H * (i + 1))
                if i >= 1:
                    dve.wait_ge(on_turned, i)
                v.tensor_copy(o_sb[:], o_ps[:]).then_inc(o_taken, 1)
                dve.wait_ge(o_taken, i + 1)
                link(v.tensor_tensor(o_sq[:], o_sb[:], o_sb[:], ALU.mult))
                link(v.tensor_reduce(o_ss[:, i, :], o_sq[:], AX_X, ALU.add))
                v.tensor_scalar(o_ss[:, i, :], o_ss[:, i, :], 1.0 / DV, EPS, ALU.mult, ALU.add
                                ).then_inc(ms_ready, 1)
                dve.wait_ge(rms_ready, i + 1)
                link(v.reciprocal(o_ss[:, i, :], o_ss[:, i, :]))
                v.tensor_tensor(o_sb[:], o_sb[:], bcast(o_ss[:, i, :], [P, H, DV], 2), ALU.mult
                                ).then_inc(on_ready, 1)

            tops(0)
            for u in range(len(units)):
                if u + 1 < len(units):
                    tops(u + 1)
                differ(u)
                if u % H == 0 and u:
                    post(u // H - 1)
            post(NP - 1)


def attend_sample(nc, mem, top, io, c):
    qkf, vig, ident = c["qkf"], c["vig"], c["ident"]
    G = PAGES + 1
    NR = 2 * NS * H
    with ExitStack() as st:
        m = Memory(nc, st)
        ring = qkf[:, 0:8, :].rearrange("p a t -> p (a t)")[:, 0:4 * PAGES * 512].rearrange(
            "p (r g n) -> p r g n", r=4, g=PAGES)
        q_b = m.sb("q_b", [P, 512])
        own = m.sb("own", [P, 512])
        sco = m.sb("sco", [P, G, 2, NS, H])
        pr = m.sb("pr", [NR, G * PAGE])
        mx = m.sb("as_mx", [NR, 4])
        pown = m.sb("pown", [NR, NS])
        own_w = m.sb("own_w", [NS, NS * H])
        wz = m.sb("wz", [P, NS, PAGES, NS * H])
        osel = m.sb("osel", [NS * H, H, DV])
        o_sb = m.sb("as_o", [NS, H, DV])
        o_sq = m.sb("as_sq", [NS, H, DV])
        o_ss = m.sb("as_ss", [NS, H])
        qb_ps = m.ps("qb_ps", [P, 512])
        kb_ps = m.ps("kb_ps", [P, 512])
        s_ps = m.ps("s_ps", [NR, 2, 512])
        w_ps = m.ps("w_ps", [P, PAGES, NS * H])
        ow_ps = m.ps("ow_ps", [NS, NS * H])
        o_ps = m.ps("as_o_ps", [NS * H, H, DV])
        f_ps = m.ps("as_f_ps", [P, 512])

        row_landed = [top.sem(f"as_landed{r}") for r in range(4)]
        ring_free = top.sem("as_ring_free")
        q_spread = top.sem("as_q_spread")
        q_copied = top.sem("as_q_copied")
        q_used = top.sem("as_q_used")
        s_ready = top.sem("as_s_ready")
        s_turned = top.sem("as_s_turned")
        neg_ready = top.sem("as_neg_ready")
        exp_done = top.sem("as_exp_done")
        pr_ready = top.sem("as_pr_ready")
        w_done = top.sem("as_w_done")
        wz_ready = top.sem("as_wz_ready")
        v_used = top.sem("as_v_used")
        osel_ready = top.sem("as_osel_ready")
        o_done = top.sem("as_o_done")
        ms_ready = top.sem("as_ms_ready")
        rms_ready = top.sem("as_rms_ready")
        on_ready = top.sem("as_on_ready")
        on_turned = top.sem("as_on_turned")
        chain = top.sem("as_chain")
        pr_scores = s_ps[:].rearrange("p a b -> p (a b)")
        block = st.enter_context(nc.Block())

        @block.gpsimd
        def _(pool):
            for n in range(2 * NS):
                cache, b, r = io["cache_k"] if n < NS else io["cache_v"], n % NS, n % 4
                if 4 <= n:
                    if n - 4 < NS:
                        pool.wait_ge(ring_free, n - 3)
                    else:
                        pool.wait_ge(v_used, n - 3 - NS)
                for g in range(PAGES):
                    nc.gpsimd.indirect_dma_start(
                        out=ring[:, r, g, :], out_offset=None, in_=cache,
                        in_offset=bass.IndirectOffsetOnAxis(
                            ap=c["cache_rows"][:, b * PAGES + g:b * PAGES + g + 1], axis=0),
                    ).then_inc(row_landed[r], 16)

        @block.tensor
        def _(pe):
            for b in range(NS):
                if b >= 1:
                    pe.wait_ge(q_used, b)
                nc.tensor.matmul(qb_ps[:], c["pick"][:, b, :], c["q_new"][:], start=True, stop=True)
                nc.tensor.matmul(kb_ps[:], c["pick"][:, b, :], c["k_new"][:], start=True, stop=True
                                 ).then_inc(q_spread, 1)
            pe.wait_ge(s_ready, 1)
            for g in range(G):
                last = nc.tensor.transpose(pr_scores[:, g * P:(g + 1) * P],
                                           sco[:, g].rearrange("p c b h -> p (c b h)"), ident[:])
            last.then_inc(s_turned, 1)
            pe.wait_ge(pr_ready, 1)
            for g in range(PAGES):
                nc.tensor.matmul(w_ps[:, g, :], pr[:, g * P:(g + 1) * P], c["sum_maps"][:],
                                 start=True, stop=True)
            nc.tensor.matmul(ow_ps[:], pown[:], c["sum_maps"][:], start=True, stop=True).then_inc(w_done, 1)
            pe.wait_ge(wz_ready, 1)
            nc.tensor.matmul(o_ps[:].rearrange("p h d -> p (h d)"), own_w[:], vig[0:NS, 0, NP, :],
                             start=True, stop=False)
            for b in range(NS):
                pe.wait_ge(row_landed[b % 4], 16 * PAGES * ((NS + b) // 4 + 1))
                for g in range(PAGES):
                    last = nc.tensor.matmul(o_ps[:].rearrange("p h d -> p (h d)"), wz[:, b, g, :],
                                            ring[:, b % 4, g, :], start=False,
                                            stop=(b == NS - 1 and g == PAGES - 1))
                last.then_inc(v_used, 1)
            pe.wait_ge(osel_ready, 1)
            nc.tensor.matmul(f_ps[0:NS, :], c["own_token"][0:NS * H, :],
                             osel[:].rearrange("p h d -> p (h d)"), start=True, stop=True).then_inc(o_done, 1)
            pe.wait_ge(on_ready, 1)
            for h in range(H):
                last = nc.tensor.transpose(qb_ps[:, h * NS:(h + 1) * NS], o_sb[:, h, :], ident[0:NS, 0:NS])
            last.then_inc(on_turned, 1)

        @block.scalar
        def _(act):
            for b in range(NS):
                act.wait_ge(q_spread, b + 1)
                if b >= 1:
                    act.wait_ge(q_used, b)
                nc.scalar.copy(q_b[:], qb_ps[:]).then_inc(q_copied, 1)
            act.wait_ge(neg_ready, 1)
            nc.scalar.activation(pr[:, 0:PAGES * PAGE + 1], pr_scores[:, 0:PAGES * PAGE + 1], ACT.Exp,
                                 scale=QK_SCALE, bias=mx[:, 1:2], accum_out=mx[:, 2:3]).then_inc(exp_done, 1)
            act.wait_ge(ms_ready, 1)
            nc.scalar.activation(o_ss[:], o_ss[:], ACT.Sqrt).then_inc(rms_ready, 1)
            act.wait_ge(on_turned, 1)
            nc.scalar.activation(c["oat"][:, :, SEQ:T], qb_ps[:, 0:H * NS].rearrange("p (h b) -> p h b", h=H),
                                 ACT.Copy, scale=c["subln"][:, 0:1])

        @block.vector
        def _(dve):
            link = Chain(dve, chain)
            v = nc.vector
            link(v.memset(wz[:], 0.0))
            for b in range(NS):
                r = b % 4
                k_rows = ring[:, r]
                dve.wait_ge(q_copied, b + 1)
                dve.wait_ge(row_landed[r], 16 * PAGES * (b // 4 + 1))
                link(v.tensor_tensor(k_rows, k_rows, bcast(q_b[:], [P, PAGES, 512], 1), ALU.mult))
                for k in range(2):
                    last = v.tensor_reduce(
                        sco[:, 0:PAGES, k, b, :],
                        k_rows.rearrange("p g (h c d) -> p g h c d", h=H, c=2)[:, :, :, k, :], AX_X, ALU.add)
                    last.then_inc(ring_free, 1) if k else link(last)
                link(v.tensor_tensor(own[:], kb_ps[:], q_b[:], ALU.mult))
                last = v.tensor_reduce(sco[:, PAGES, :, b, :].rearrange("p c h -> p h c"),
                                       own[:].rearrange("p (h c d) -> p h c d", h=H, c=2), AX_X, ALU.add)
                last.then_inc(q_used, 1)
                dve.wait_ge(q_used, b + 1)
            dve.wait_ge(ring_free, NS)
            v.memset(mx[:], 0.0).then_inc(s_ready, 1)
            dve.wait_ge(s_ready, 1)
            dve.wait_ge(s_turned, 1)
            link(v.reduce_max(mx[:, 0:1], pr_scores[:, 0:PAGES * PAGE + 1], AX_X))
            v.tensor_scalar(mx[:, 1:2], mx[:, 0:1], -QK_SCALE, None, ALU.mult).then_inc(neg_ready, 1)
            dve.wait_ge(exp_done, 1)
            link(v.reciprocal(mx[:, 3:4], mx[:, 2:3]))
            link(v.tensor_tensor(mx[:, 3:4], mx[:, 3:4], c["map_coef"][:], ALU.mult))
            link(v.tensor_scalar(pr[:, 0:PAGES * PAGE + 1], pr[:, 0:PAGES * PAGE + 1], mx[:, 3:4], None, ALU.mult))
            v.tensor_scalar(pown[:], c["own_token"][:], pr[:, PAGES * PAGE:PAGES * PAGE + 1], None,
                            ALU.mult).then_inc(pr_ready, 1)
            dve.wait_ge(w_done, 1)
            link(v.tensor_copy(own_w[:], ow_ps[:]))
            for b in range(NS):
                last = v.tensor_copy(wz[:, b, :, b * H:(b + 1) * H], w_ps[:, :, b * H:(b + 1) * H])
                last.then_inc(wz_ready, 1) if b == NS - 1 else link(last)
            dve.wait_ge(v_used, NS)
            v.tensor_tensor(osel[:], o_ps[:], bcast(c["own_head"][:], [NS * H, H, DV], 2), ALU.mult
                            ).then_inc(osel_ready, 1)
            dve.wait_ge(o_done, 1)
            link(v.tensor_copy(o_sb[:], f_ps[0:NS, :].rearrange("p (h d) -> p h d", h=H)))
            link(v.tensor_tensor(o_sq[:], o_sb[:], o_sb[:], ALU.mult))
            link(v.tensor_reduce(o_ss[:], o_sq[:], AX_X, ALU.add))
            v.tensor_scalar(o_ss[:], o_ss[:], 1.0 / DV, EPS, ALU.mult, ALU.add).then_inc(ms_ready, 1)
            dve.wait_ge(rms_ready, 1)
            link(v.reciprocal(o_ss[:], o_ss[:]))
            v.tensor_tensor(o_sb[:], o_sb[:], bcast(o_ss[:], [NS, H, DV], 2), ALU.mult).then_inc(on_ready, 1)


def hgrn(nc, mem, top, io, c):
    qkf, vig, ident, obt = c["qkf"], c["vig"], c["ident"], c["obt"]
    MID = CH // 2 - 1
    NB = P // CH
    with ExitStack() as st:
        m = Memory(nc, st)
        r = lambda n: qkf[:, n, 0:SEQ]
        KM, KK, GG, QM, G2, QE, KDN = range(7)
        kdn = qkf[:, KDN, 0:SEQ].rearrange("p (t n) -> p t n", t=NP)
        restart = m.sb("restart", [P, SEQ])
        apart = [m.sb(f"apart{b}", [P, NB, DV]) for b in range(2)]
        atm = [m.sb(f"atm{b}", [P, P]) for b in range(2)]
        state = [m.sb(f"state{b}", [P, DV]) for b in range(4)]
        tp = [m.ps(f"hg_tp{b}", [P, 4, P]) for b in range(2)]
        a_ps = [m.ps(f"hg_a{b}", [P, P]) for b in range(2)]
        o_ps = [m.ps(f"hg_o{b}", [P, DV]) for b in range(2)]
        u_ps = [m.ps(f"hg_u{b}", [P, NB, DV]) for b in range(2)]

        gates = top.sem("hg_gates")
        f_ready = top.sem("hg_f_ready")
        log_ready = top.sem("hg_log_ready")
        rel_ready = top.sem("hg_rel_ready")
        exps_done = top.sem("hg_exps_done")
        ops_ready = top.sem("hg_ops_ready")
        kd_turned = top.sem("hg_kd_turned")
        kd_stored = top.sem("hg_kd_stored")
        a_done = top.sem("hg_a_done")
        a_masked = top.sem("hg_a_masked")
        u_done = top.sem("hg_u_done")
        inter_done = top.sem("hg_inter_done")
        state_ready = top.sem("hg_state_ready")
        o_stored = top.sem("hg_o_stored")
        state_saved = top.sem("hg_state_saved")
        chain = top.sem("hg_chain")
        apart_zeroed = top.sem("hg_apart_zeroed")
        apart_ready = top.sem("hg_apart_ready")
        block = st.enter_context(nc.Block())

        @block.gpsimd
        def _(pool):
            for b in range(2):
                nc.gpsimd.memset(apart[b][:], 0.0).then_inc(apart_zeroed, 1)
            pool.wait_ge(apart_zeroed, 2)
            for n_tile in range(H * NP):
                h, i = divmod(n_tile, NP)
                if n_tile >= 2:
                    pool.wait_ge(u_done, n_tile - 1)
                for j in range(NB):
                    s = slice(j * CH, (j + 1) * CH)
                    nc.gpsimd.tensor_copy(apart[i % 2][s, j, :], vig[s, 1, i, h * DV:(h + 1) * DV]
                                          ).then_inc(apart_ready, 1)

        def state_count(h, n):
            return h * (NCH + 1) + n + 1

        @block.scalar
        def _(act):
            for h in range(H):
                q, f = qkf[:, CHQ + h, :], qkf[:, CHF + h, :]
                nc.scalar.activation(q, q, ACT.Silu).then_inc(gates, 1)
                nc.scalar.activation(f, f, ACT.Sigmoid).then_inc(gates, 1)
                act.wait_ge(f_ready, h + 1)
                nc.scalar.activation(r(KM), f[:, 0:SEQ], ACT.Ln).then_inc(log_ready, 1)
                act.wait_ge(rel_ready, h + 1)
                nc.scalar.activation(r(QM), r(KM), ACT.Exp).then_inc(exps_done, 1)
                act.wait_ge(exps_done, 4 * h + 1)
                nc.scalar.activation(r(KM), r(KM), ACT.Exp, scale=-1.0).then_inc(exps_done, 1)
                nc.scalar.activation(r(GG), r(GG), ACT.Exp).then_inc(exps_done, 1)
                nc.scalar.activation(r(G2), r(G2), ACT.Exp).then_inc(exps_done, 1)
                for half in range(2):
                    act.wait_ge(kd_turned, 2 * h + half + 1)
                    nc.scalar.copy(kdn[:, 4 * half:4 * half + 4, :], tp[half][:]).then_inc(kd_stored, 1)
                for i in range(NP):
                    act.wait_ge(inter_done, NB * (h * NP + i + 1))
                    nc.scalar.copy(vig[:, 0, i, h * DV:(h + 1) * DV], o_ps[i % 2][:]).then_inc(o_stored, 1)

        @block.vector
        def _(dve):
            link = Chain(dve, chain)
            v = nc.vector
            link(v.memset(restart[:], 1.0))
            link(v.memset(restart[:].rearrange("p (a b) -> p a b", b=CH)[:, :, 0:1], 0.0))
            for b in range(2):
                link(v.memset(atm[b][:], 0.0))
            for h in range(H):
                q, f = qkf[:, CHQ + h, :], qkf[:, CHF + h, :]
                lb, one_lb = c["lb"][:, h:h + 1], c["one_lb"][:, h:h + 1]
                dve.wait_ge(gates, 2 * h + 2)
                v.tensor_scalar(f, f, one_lb, lb, ALU.mult, ALU.add).then_inc(f_ready, 1)
                dve.wait_ge(f_ready, h + 1)
                link(v.tensor_scalar(r(KK), f[:, 0:SEQ], -1.0, 1.0, ALU.mult, ALU.add))
                dve.wait_ge(log_ready, h + 1)
                link(v.tensor_tensor_scan(r(GG), restart[:], r(KM), 0.0, ALU.mult, ALU.add))
                g3 = r(GG).rearrange("p (a b) -> p a b", b=CH)
                shape = [P, NCH, CH]
                link(v.tensor_tensor(r(KM).rearrange("p (a b) -> p a b", b=CH), g3,
                                     g3[:, :, MID:MID + 1].to_broadcast(shape), ALU.subtract))
                v.tensor_tensor(r(G2).rearrange("p (a b) -> p a b", b=CH),
                                g3[:, :, CH - 1:CH].to_broadcast(shape), g3, ALU.subtract).then_inc(rel_ready, 1)
                dve.wait_ge(exps_done, 4 * h + 4)
                sc = q[:, 0:SEQ]
                v.scalar_tensor_tensor(out=r(QM), in0=sc, scalar=HG_SCALE, in1=r(QM), op0=ALU.mult,
                                       op1=ALU.mult).then_inc(ops_ready, 1)
                v.tensor_tensor(r(KM), r(KK), r(KM), ALU.mult).then_inc(ops_ready, 1)
                v.scalar_tensor_tensor(out=r(QE), in0=sc, scalar=HG_SCALE, in1=r(GG), op0=ALU.mult,
                                       op1=ALU.mult).then_inc(ops_ready, 1)
                v.tensor_tensor(r(G2), r(KK), r(G2), ALU.mult).then_inc(ops_ready, 1)
                if h >= 1:
                    dve.wait_ge(state_saved, 16 * h)
                v.memset(state[0][:], 0.0).then_inc(state_ready, 1)
                for i in range(NP):
                    n_tile = h * NP + i
                    dve.wait_ge(a_done, n_tile + 1)
                    if n_tile >= 2:
                        dve.wait_ge(inter_done, NB * (n_tile - 1))
                    v.copy_predicated(atm[i % 2][:], c["bmask"][:].bitcast(U32), a_ps[i % 2][:]
                                      ).then_inc(a_masked, 1)
                    dve.wait_ge(u_done, n_tile + 1)
                    for j in range(NB):
                        n = i * NB + j
                        dve.wait_ge(state_ready, state_count(h, n))
                        if h * NCH + n >= 3:
                            dve.wait_ge(inter_done, h * NCH + n - 2)
                        v.scalar_tensor_tensor(out=state[(n + 1) % 4][:], in0=state[n % 4][:],
                                               scalar=r(GG)[:, n * CH + CH - 1:n * CH + CH],
                                               in1=u_ps[i % 2][:, j, :], op0=ALU.mult, op1=ALU.add
                                               ).then_inc(state_ready, 1)
                dve.wait_ge(state_ready, state_count(h, NCH))

        @block.tensor
        def _(pe):
            for h in range(H):
                pe.wait_ge(ops_ready, 4 * h + 4)
                for half in range(2):
                    if h >= 1:
                        pe.wait_ge(kd_stored, 2 * h)
                    for t in range(4):
                        i = 4 * half + t
                        last = nc.tensor.transpose(tp[half][:, t, :], r(G2)[:, i * P:(i + 1) * P], ident[:])
                    last.then_inc(kd_turned, 1)
                for i in range(NP):
                    n_tile = h * NP + i
                    tok = slice(i * P, (i + 1) * P)
                    if n_tile >= 2:
                        pe.wait_ge(a_masked, n_tile - 1)
                    nc.tensor.matmul(a_ps[i % 2][:], r(KM)[:, tok], r(QM)[:, tok], start=True, stop=True
                                     ).then_inc(a_done, 1)
                    pe.wait_ge(kd_stored, 2 * h + 1 + (i >= 4))
                    if n_tile >= 2:
                        pe.wait_ge(state_ready, state_count((n_tile - 2) // NP, ((n_tile - 2) % NP + 1) * NB))
                    pe.wait_ge(apart_ready, NB * (n_tile + 1))
                    last = nc.tensor.matmul(u_ps[i % 2][:].rearrange("p j d -> p (j d)"), kdn[:, i, :],
                                            apart[i % 2][:].rearrange("p j d -> p (j d)"),
                                            start=True, stop=True)
                    last.then_inc(u_done, 1)
                    pe.wait_ge(a_masked, n_tile + 1)
                    if n_tile >= 2:
                        pe.wait_ge(o_stored, n_tile - 1)
                    nc.tensor.matmul(o_ps[i % 2][:], atm[i % 2][:], vig[:, 1, i, h * DV:(h + 1) * DV],
                                     start=True, stop=False, skip_group_check=True)
                    for j in range(NB):
                        n = i * NB + j
                        pe.wait_ge(state_ready, state_count(h, n))
                        nc.tensor.matmul(o_ps[i % 2][j * CH:(j + 1) * CH, :],
                                         r(QE)[:, n * CH:(n + 1) * CH], state[n % 4][:], start=False,
                                         stop=True, skip_group_check=True, tile_position=(0, j * CH)
                                         ).then_inc(inter_done, 1)

        @block.sync
        def _(sp):
            for h in range(H):
                sp.wait_ge(state_ready, state_count(h, NCH))
                sp.dma_start(io["state_prompt"][h], state[NCH % 4][:]).then_inc(state_saved, 16)
            sp.wait_ge(state_saved, 16 * H)

    with ExitStack() as st:
        m = Memory(nc, st)
        s0 = qkf[:, 0:4, :].rearrange("p a t -> p (a t)")[:, 0:NS * H * DV].rearrange(
            "p (b h d) -> p b h d", b=NS, h=H)
        kv = m.sb("kv", [P, H, DV])
        v_sb = m.sb("v_sb", [P, H, DV])
        k_s = m.sb("k_s2", [P, H, NS])
        q_z = m.sb("q_z2", [P, H, NS, NS])
        ss = m.sb("hp_ss", [P, NT, H])
        v_ps = m.ps("v_ps", [P, H, DV])
        o_ps = m.ps("hs_o_ps", [NS, H, DV])
        t_ps = [m.ps(f"hp_t{b}", [P, H, P]) for b in range(2)]
        s_landed = top.sem("hs_landed")
        v_spread = top.sem("hs_v_spread")
        v_copied = top.sem("hs_v_copied")
        kv_ready = top.sem("hs_kv_ready")
        new_ready = top.sem("hs_new_ready")
        qz_ready = top.sem("hs_qz_ready")
        o_done = top.sem("hs_o_done")
        s_saved = top.sem("hs_saved")
        silu_done = top.sem("hp_silu_done")
        ms_ready = top.sem("hp_ms_ready")
        rms_ready = top.sem("hp_rms_ready")
        y_ready = top.sem("hp_y_ready")
        turned = top.sem("hp_turned")
        stored = top.sem("hp_stored")
        chain = top.sem("hs_chain")
        squares = vig[:, 1].rearrange("p t (h d) -> p t h d", h=H)
        o_all = vig[:, 0].rearrange("p t (h d) -> p t h d", h=H)
        gate = vig[:, 2].rearrange("p t (h d) -> p t h d", h=H)
        block = st.enter_context(nc.Block())

        @block.sync
        def _(sp):
            sp.dma_start(s0.rearrange("p b h d -> p (b h d)"), io["state"].rearrange("p b h d -> p (b h d)")
                         ).then_inc(s_landed, 16)
            for b in range(NS):
                sp.wait_ge(new_ready, b + 1)
                sp.dma_start(io["state_sample"][:, b], s0[:, b]).then_inc(s_saved, 16)
            sp.wait_ge(s_saved, 16 * NS)

        @block.scalar
        def _(act):
            for b in range(NS):
                act.wait_ge(v_spread, b + 1)
                if b >= 1:
                    act.wait_ge(kv_ready, b)
                nc.scalar.copy(v_sb[:], v_ps[:]).then_inc(v_copied, 1)
            nc.scalar.activation(vig[:, 2], vig[:, 2], ACT.Silu).then_inc(silu_done, 1)
            act.wait_ge(ms_ready, 1)
            nc.scalar.activation(ss[:], ss[:], ACT.Sqrt).then_inc(rms_ready, 1)
            for i in range(NT):
                act.wait_ge(turned, i + 1)
                nc.scalar.activation(obt[:, :, i * P:i * P + rows(i)], t_ps[i % 2][:, :, 0:rows(i)], ACT.Copy,
                                     scale=c["gnorm"][:, 0:1]).then_inc(stored, 1)

        @block.vector
        def _(dve):
            link = Chain(dve, chain)
            v = nc.vector
            q_s, f_s = qkf[:, CHQ:CHQ + H, SEQ:T], qkf[:, CHF:CHF + H, SEQ:T]
            link(v.tensor_scalar(k_s[:], f_s, -1.0, 1.0, ALU.mult, ALU.add))
            link(v.memset(q_z[:], 0.0))
            for b in range(NS):
                last = v.tensor_scalar(q_z[:, :, b, b], q_s[:, :, b], HG_SCALE, None, ALU.mult)
                last.then_inc(qz_ready, 1)
            dve.wait_ge(s_landed, 16)
            for b in range(NS):
                dve.wait_ge(v_copied, b + 1)
                v.tensor_tensor(kv[:], v_sb[:], bcast(k_s[:, :, b], [P, H, DV], 2), ALU.mult).then_inc(kv_ready, 1)
                link(v.tensor_tensor(s0[:, b], s0[:, b], bcast(f_s[:, :, b], [P, H, DV], 2), ALU.mult))
                dve.wait_ge(kv_ready, b + 1)
                v.tensor_tensor(s0[:, b], s0[:, b], kv[:], ALU.add).then_inc(new_ready, 1)
                dve.wait_ge(new_ready, b + 1)
            dve.wait_ge(o_done, 1)
            link(v.memset(vig[:, 0, NP, :], 0.0))
            link(v.tensor_copy(o_all[0:NS, NP], o_ps[:]))
            link(v.tensor_tensor(squares, o_all, o_all, ALU.mult))
            link(v.tensor_reduce(ss[:], squares, AX_X, ALU.add))
            v.tensor_scalar(ss[:], ss[:], 1.0 / DV, EPS, ALU.mult, ALU.add).then_inc(ms_ready, 1)
            dve.wait_ge(rms_ready, 1)
            link(v.reciprocal(ss[:], ss[:]))
            link(v.tensor_tensor(o_all.rearrange("p t h d -> p (t h) d"), o_all.rearrange("p t h d -> p (t h) d"),
                                 bcast(ss[:].rearrange("p t h -> p (t h)"), [P, NT * H, DV], 2), ALU.mult))
            dve.wait_ge(silu_done, 1)
            v.tensor_tensor(vig[:, 0], vig[:, 0], vig[:, 2], ALU.mult).then_inc(y_ready, 1)

        @block.tensor
        def _(pe):
            for b in range(NS):
                if b >= 1:
                    pe.wait_ge(v_copied, b)
                nc.tensor.matmul(v_ps[:].rearrange("p h d -> p (h d)"), c["pick"][:, b, :], vig[0:NS, 1, NP, :],
                                 start=True, stop=True).then_inc(v_spread, 1)
            pe.wait_ge(qz_ready, NS)
            pe.wait_ge(new_ready, NS)
            for h in range(H):
                for b in range(NS):
                    last = nc.tensor.matmul(o_ps[:, h, :], q_z[:, h, b, :], s0[:, b, h, :],
                                            start=(b == 0), stop=(b == NS - 1))
            last.then_inc(o_done, 1)
            pe.wait_ge(y_ready, 1)
            for i in range(NT):
                if i >= 2:
                    pe.wait_ge(stored, i - 1)
                for h in range(H):
                    last = nc.tensor.transpose(t_ps[i % 2][:, h, :], vig[:, 0, i, h * DV:(h + 1) * DV], ident[:])
                last.then_inc(turned, 1)


def merge(nc, mem, top, io, c):
    xnt, branch = c["xnt"], (c["oat"], c["obt"])
    NSL = len(SLICES)
    with ExitStack() as st:
        m = Memory(nc, st)
        wg = [[m.sb(f"wg{u}{x}", [P, KD, P]) for x in range(2)] for u in range(2)]
        wb = [[m.sb(f"wb{u}{x}", [P, H, P]) for x in range(2)] for u in range(2)]
        gate = [[m.sb(f"mg{z}{x}", [P, 512]) for x in range(2)] for z in range(2)]
        mt = [m.sb(f"mt{u}", [P, T]) for u in range(2)]
        g_ps = [[m.ps(f"mg_ps{z}{x}", [P, 512]) for x in range(2)] for z in range(2)]
        b_ps = [[m.ps(f"mb_ps{z}{x}", [P, 512]) for x in range(2)] for z in range(2)]
        w_landed = [top.sem(f"mw_landed{u}") for u in range(2)]
        chunk_done = top.sem("m_chunk_done")
        slice_done = top.sem("m_slice_done")
        gates_done = top.sem("m_gates_done")
        sums_done = top.sem("m_sums_done")
        m_saved = [top.sem(f"m_saved{u}") for u in range(2)]
        chain = top.sem("m_chain")
        block = st.enter_context(nc.Block())

        @block.sync
        def _(sp):
            for k in range(KD):
                u = k % 2
                if k >= 2:
                    sp.wait_ge(slice_done, NSL * (k - 1))
                sp.dma_start(wg[u][0][:], io["w_t"][CGA + k]).then_inc(w_landed[u], 16)
                sp.dma_start(wg[u][1][:], io["w_t"][CGB + k]).then_inc(w_landed[u], 16)
                sp.dma_start(wb[u][0][:], io["wa"][k]).then_inc(w_landed[u], 16)
                sp.dma_start(wb[u][1][:], io["wb"][k]).then_inc(w_landed[u], 16)
                if k >= 1:
                    sp.wait_ge(sums_done, NSL * k)
                    sp.dma_start(io["mt"][k - 1], mt[(k - 1) % 2][:]).then_inc(m_saved[(k - 1) % 2], 16)
            sp.wait_ge(sums_done, NSL * KD)
            sp.dma_start(io["mt"][KD - 1], mt[(KD - 1) % 2][:]).then_inc(m_saved[(KD - 1) % 2], 16)
            for u in range(2):
                sp.wait_ge(m_saved[u], 16 * KD // 2)

        @block.tensor
        def _(pe):
            for k in range(KD):
                u = k % 2
                pe.wait_ge(w_landed[u], 64 * (k // 2 + 1))
                for s, (t0, n) in enumerate(SLICES):
                    q = NSL * k + s
                    if q >= 2:
                        pe.wait_ge(sums_done, q - 1)
                    for x in range(2):
                        for d in range(KD):
                            nc.tensor.matmul(g_ps[q % 2][x][:, 0:n], wg[u][x][:, d, :], xnt[:, d, t0:t0 + n],
                                             start=(d == 0), stop=(d == KD - 1))
                        for d in range(H):
                            last = nc.tensor.matmul(b_ps[q % 2][x][:, 0:n], wb[u][x][:, d, :],
                                                    branch[x][:, d, t0:t0 + n], start=(d == 0), stop=(d == H - 1))
                    last.then_inc(slice_done, 1)

        @block.scalar
        def _(act):
            for q in range(NSL * KD):
                n = SLICES[q % NSL][1]
                act.wait_ge(slice_done, q + 1)
                if q >= 2:
                    act.wait_ge(sums_done, q - 1)
                for x in range(2):
                    nc.scalar.activation(gate[q % 2][x][:, 0:n], g_ps[q % 2][x][:, 0:n], ACT.Sigmoid
                                         ).then_inc(gates_done, 1)

        @block.vector
        def _(dve):
            link = Chain(dve, chain)
            v = nc.vector
            for k in range(KD):
                if k >= 2:
                    dve.wait_ge(m_saved[k % 2], 16 * (k // 2))
                for s, (t0, n) in enumerate(SLICES):
                    q = NSL * k + s
                    dve.wait_ge(gates_done, 2 * q + 2)
                    ga, gb = gate[q % 2][0][:, 0:n], gate[q % 2][1][:, 0:n]
                    link.mark(v.tensor_tensor(ga, ga, b_ps[q % 2][0][:, 0:n], ALU.mult))
                    link(v.tensor_tensor(gb, gb, b_ps[q % 2][1][:, 0:n], ALU.mult))
                    v.tensor_tensor(mt[k % 2][:, t0:t0 + n], ga, gb, ALU.add).then_inc(sums_done, 1)


def experts(nc, mem, top, io, c):
    ident = c["ident"]
    with ExitStack() as st:
        m = Memory(nc, st)
        w_out = m.sb("w_out", [P, KD, D])
        w_q = m.sb("w_q", [P, KD, D])
        keys = m.sb("keys", [P, HP, NK])
        norm2 = m.sb("norm2", [P, D])
        norm_f = m.sb("norm_f", [P, D])
        xt = m.sb("xt", [P, D])
        mts = m.sb("mts", [P, KD, P])
        hs = m.sb("hs", [P, D])
        n2 = m.sb("n2", [P, D])
        n2t = m.sb("n2t", [P, KD, P])
        qn = m.sb("qn", [P, D])
        qt = m.sb("qt", [P, HP, P])
        work = m.sb("work", [P, 2 * HP * NK])
        comb = m.sb("comb", [P, HP, TOPK * TOPK])
        s16 = m.sb("s16", [P, HP, 2, TOPK])
        i16 = m.sb("i16", [P, HP, 2, TOPK], U32)
        i16f = m.sb("i16f", [P, HP, 2, TOPK])
        cs = m.sb("cs", [P, HP, TOPK])
        ci = m.sb("ci", [P, HP, TOPK], U32)
        cd = m.sb("cd", [P, HP, TOPK], U32)
        cf = [m.sb(f"cf{x}", [P, HP, TOPK]) for x in range(2)]
        ee = [m.sb(f"ee{x}", [P, SLOTS]) for x in range(2)]
        idx = m.sb("idx", [P, SLOTS], U32)
        cur = m.sb("cur", [P, 2, RING], U32)
        wgt = m.sb("wgt", [P, HP, TOPK])
        zz = m.sb("zz", [P, HP])
        sm = m.sb("sm", [P, 4])
        dots = m.sb("dots", [P, 2, RING])
        gel = m.sb("gel", [P, 2, RING])
        coef = m.sb("coef", [P, 2, RING])
        ring = m.sb("ring", [P, RING, 2 * D])
        a_ps = m.ps("xa_ps", [P, D])
        b_ps = m.ps("xb_ps", [P, KD, P])
        s_ps = m.ps("xs_ps", [P, 2, HP, NK])

        w_landed = top.sem("xw_landed")
        in_landed = top.sem("xin_landed")
        out_done = top.sem("x_out_done")
        h_ready = top.sem("x_h_ready")
        sq_done = top.sem("x_sq_done")
        ms_ready = top.sem("x_ms_ready")
        rms_ready = top.sem("x_rms_ready")
        n2_ready = top.sem("x_n2_ready")
        n2_turned = top.sem("x_n2_turned")
        n2t_ready = top.sem("x_n2t_ready")
        q_done = top.sem("x_q_done")
        q_ready = top.sem("x_q_ready")
        q_turned = top.sem("x_q_turned")
        qt_ready = top.sem("x_qt_ready")
        s_done = top.sem("x_s_done")
        e_ready = top.sem("x_e_ready")
        e_done = top.sem("x_e_done")
        idx_ready = top.sem("x_idx_ready")
        cur_ready = top.sem("x_cur_ready")
        landed = [top.sem(f"x_landed{j}") for j in range(RING)]
        dots_ready = top.sem("x_dots_ready")
        gel_ready = top.sem("x_gel_ready")
        coef_ready = top.sem("x_coef_ready")
        slot_used = top.sem("x_slot_used")
        sum_ready = top.sem("x_sum_ready")
        y_ready = top.sem("x_y_ready")
        y_saved = top.sem("x_y_saved")
        chain = top.sem("x_chain")
        coef_final = top.sem("x_coef_final")
        sp_held = top.sem("x_sp_held")
        pool_held = top.sem("x_pool_held")
        dve_held = top.sem("x_dve_held")
        block = st.enter_context(nc.Block())
        HALVES = TOPK // RING

        @block.sync
        def _(sp):
            sp.dma_start(w_out[:], io["w_out"]).then_inc(w_landed, 16)
            sp.dma_start(norm2[:], io["norm2"].to_broadcast([P, D])).then_inc(w_landed, 16)
            sp.dma_start(norm_f[:], io["norm_f"].to_broadcast([P, D])).then_inc(w_landed, 16)
            sp.dma_start(keys[:], io["keys"]).then_inc(w_landed, 16)
            sp.dma_start(w_q[:], io["w_query"]).then_inc(w_landed, 16)

            def tile(i, R, first):
                if not first:
                    hold(sp, h_ready, i, sp_held)
                tok = bass.ds(i * P, R)
                sp.dma_start(xt[0:R, :], io["x"][tok, :]).then_inc(in_landed, 16)
                sp.dma_start(mts[:, :, 0:R], io["mt"][:, :, tok].rearrange("k p t -> p k t")).then_inc(in_landed, 16)
                hold(sp, y_ready, i + 1, sp_held)
                sp.dma_start(io["y"][tok, :], hs[0:R, :]).then_inc(y_saved, 16)
                hold(sp, y_saved, 16 * (i + 1), sp_held)

            tile(0, P, True)
            with sp.Fori(1, NP) as i:
                tile(i, P, False)
            tile(NP, NS, False)

        @block.gpsimd
        def _(pool):
            def tile(i, R, first):
                hold(pool, idx_ready, i + 1, pool_held)

                def head(h, slots0):
                    for half in range(HALVES):
                        s0 = h * TOPK + half * RING
                        n0 = slots0 + s0
                        nc.gpsimd.tensor_copy(cur[0:R, half, :], idx[0:R, bass.ds(s0, RING)]).then_inc(cur_ready, 1)
                        hold(pool, cur_ready, i * (SLOTS // RING) + h * HALVES + half + 1, pool_held)
                        for j in range(RING):
                            if not (first and isinstance(h, int) and h == 0 and half == 0):
                                hold(pool, slot_used, n0 + j + 1 - RING, pool_held)
                            nc.gpsimd.indirect_dma_start(
                                out=ring[0:R, j, :], out_offset=None, in_=io["experts"],
                                in_offset=bass.IndirectOffsetOnAxis(ap=cur[0:R, half, j:j + 1], axis=0),
                            ).then_inc(landed[j], 16)

                if first:
                    head(0, 0)
                with pool.Fori(1 if first else 0, HP) as h:
                    head(h, i * SLOTS)

            tile(0, P, True)
            with pool.Fori(1, NP) as i:
                tile(i, P, False)
            tile(NP, NS, False)

        @block.tensor
        def _(pe):
            pe.wait_ge(w_landed, 16 * 5)

            def tile(i, R, first):
                pe.wait_ge(in_landed, 32 * (i + 1))
                for k in range(KD):
                    for n in range(2):
                        last = nc.tensor.matmul(a_ps[0:R, n * 512:(n + 1) * 512], mts[:, k, 0:R],
                                                w_out[:, k, n * 512:(n + 1) * 512],
                                                start=(k == 0), stop=(k == KD - 1))
                last.then_inc(q_done, 1)
                pe.wait_ge(n2_ready, i + 1)
                for k in range(KD):
                    last = nc.tensor.transpose(b_ps[:, k, 0:R], n2[0:R, k * P:(k + 1) * P], ident[0:R, 0:R])
                last.then_inc(n2_turned, 1)
                pe.wait_ge(n2t_ready, i + 1)
                for k in range(KD):
                    for n in range(2):
                        last = nc.tensor.matmul(a_ps[0:R, n * 512:(n + 1) * 512], n2t[:, k, 0:R],
                                                w_q[:, k, n * 512:(n + 1) * 512],
                                                start=(k == 0), stop=(k == KD - 1))
                last.then_inc(q_done, 1)
                pe.wait_ge(q_ready, i + 1)
                for k in range(HP):
                    last = nc.tensor.transpose(b_ps[:, k, 0:R], qn[0:R, k * P:(k + 1) * P], ident[0:R, 0:R])
                last.then_inc(q_turned, 1)
                pe.wait_ge(qt_ready, i + 1)
                for k in range(HP):
                    for x in range(2):
                        s = slice(x * DH, (x + 1) * DH)
                        last = nc.tensor.matmul(s_ps[0:R, x, k, :], qt[s, k, 0:R], keys[s, k, :],
                                                start=True, stop=True)
                last.then_inc(s_done, 1)

            tile(0, P, True)
            with pe.Fori(1, NP) as i:
                tile(i, P, False)
            tile(NP, NS, False)

        @block.scalar
        def _(act):
            def tile(i, R, first):
                act.wait_ge(h_ready, i + 1)
                nc.scalar.activation(n2[0:R, :], hs[0:R, :], ACT.Square, accum_out=sm[0:R, 0:1]
                                     ).then_inc(sq_done, 1)
                act.wait_ge(ms_ready, 2 * i + 1)
                nc.scalar.activation(sm[0:R, 1:2], sm[0:R, 1:2], ACT.Sqrt).then_inc(rms_ready, 1)
                act.wait_ge(n2_turned, i + 1)
                nc.scalar.copy(n2t[:, :, 0:R], b_ps[:, :, 0:R]).then_inc(n2t_ready, 1)
                act.wait_ge(q_done, 2 * i + 2)
                nc.scalar.copy(qn[0:R, :], a_ps[0:R, :]).then_inc(q_ready, 1)
                act.wait_ge(q_turned, i + 1)
                nc.scalar.copy(qt[:, :, 0:R], b_ps[:, :, 0:R]).then_inc(qt_ready, 1)
                act.wait_ge(e_ready, i + 1)
                nc.scalar.activation(wgt[0:R], wgt[0:R], ACT.Exp).then_inc(e_done, 1)
                with act.Fori(0, HP) as h:
                    for half in range(HALVES):
                        act.wait_ge(dots_ready, i * (SLOTS // RING) + h * HALVES + half + 1)
                        nc.scalar.activation(gel[0:R, half, :], dots[0:R, half, :], ACT.Gelu
                                             ).then_inc(gel_ready, 1)
                act.wait_ge(sum_ready, i + 1)
                nc.scalar.activation(xt[0:R, :] if False else qn[0:R, :], hs[0:R, :], ACT.Square,
                                     accum_out=sm[0:R, 2:3]).then_inc(sq_done, 1)
                act.wait_ge(ms_ready, 2 * i + 2)
                nc.scalar.activation(sm[0:R, 3:4], sm[0:R, 3:4], ACT.Sqrt).then_inc(rms_ready, 1)

            tile(0, P, True)
            with act.Fori(1, NP) as i:
                tile(i, P, False)
            tile(NP, NS, False)

        @block.vector
        def _(dve):
            v = nc.vector
            LISTS = 2 * HP
            STEPS = [None]

            def top16(link, R, lists, values, spare, best, where):
                for stage in range(5):
                    for n in range(lists):
                        lo, hi = slice(0, 8), slice(8, 16)
                        if stage == 0:
                            ins = v.max(best(n)[0:R, lo], values(n)[0:R])
                        elif stage == 1:
                            ins = v.max_index(where(n)[0:R, lo], best(n)[0:R, lo], values(n)[0:R])
                        elif stage == 2:
                            ins = v.match_replace(spare(n)[0:R], best(n)[0:R, lo], values(n)[0:R], LOWEST)
                        elif stage == 3:
                            ins = v.max(best(n)[0:R, hi], spare(n)[0:R])
                        else:
                            ins = v.max_index(where(n)[0:R, hi], best(n)[0:R, hi], spare(n)[0:R])
                        link.mark(ins)
                    hold(dve, link.sem, link.base + link.n, dve_held)

            def tile(i, R, first):
                link = Chain(dve, chain, i * STEPS[0] if not first else 0)
                dve.wait_ge(q_done, 2 * i + 1)
                dve.wait_ge(in_landed, 32 * (i + 1))
                if not first:
                    dve.wait_ge(y_saved, 16 * i)
                v.tensor_tensor(hs[0:R, :], a_ps[0:R, :], xt[0:R, :], ALU.add).then_inc(h_ready, 1)
                dve.wait_ge(sq_done, 2 * i + 1)
                v.tensor_scalar(sm[0:R, 1:2], sm[0:R, 0:1], 1.0 / D, EPS, ALU.mult, ALU.add).then_inc(ms_ready, 1)
                dve.wait_ge(rms_ready, 2 * i + 1)
                link(v.reciprocal(sm[0:R, 1:2], sm[0:R, 1:2]))
                v.scalar_tensor_tensor(out=n2[0:R, :], in0=hs[0:R, :], scalar=sm[0:R, 1:2], in1=norm2[0:R, :],
                                       op0=ALU.mult, op1=ALU.mult).then_inc(n2_ready, 1)
                hold(dve, s_done, i + 1, dve_held)
                top16(link, R, LISTS, lambda n: s_ps[:, n % 2, n // 2, :],
                      lambda n: work[:, n * NK:(n + 1) * NK],
                      lambda n: s16[:, n // 2, n % 2, :], lambda n: i16[:, n // 2, n % 2, :])
                link.mark(v.tensor_copy(i16f[0:R], i16[0:R]))
                shape = [R, HP, TOPK, TOPK]
                c4 = comb[0:R].rearrange("p h (a b) -> p h a b", a=TOPK)
                link(v.tensor_tensor(c4, bcast(s16[0:R, :, 0, :], shape, 3), bcast(s16[0:R, :, 1, :], shape, 2),
                                     ALU.add))
                hold(dve, chain, link.base + link.n, dve_held)
                top16(link, R, HP, lambda n: comb[:, n, :], lambda n: work[:, n * 256:(n + 1) * 256],
                      lambda n: cs[:, n, :], lambda n: ci[:, n, :])
                link(v.tensor_tensor(wgt[0:R], cs[0:R], cs[0:R, :, 0:1].to_broadcast([R, HP, TOPK]), ALU.subtract))
                v.tensor_copy(zz[0:R, :], cs[0:R, :, 0]).then_inc(e_ready, 1)
                onehot = work[0:R, :].rearrange("p (h s k) -> p h s k", h=HP, s=TOPK)
                onehot3 = work[0:R, :].rearrange("p (n k) -> p n k", k=TOPK)
                for x in range(2):
                    if x == 0:
                        link(v.tensor_scalar(cd[0:R], ci[0:R], 4, None, ALU.logical_shift_right))
                    else:
                        link(v.tensor_scalar(cd[0:R], ci[0:R], TOPK - 1, None, ALU.bitwise_and))
                    link(v.tensor_copy(cf[x][0:R], cd[0:R]))
                    link(v.tensor_tensor(onehot3,
                                         bcast(cf[x][0:R].rearrange("p h s -> p (h s)"), [R, SLOTS, TOPK], 2),
                                         bcast(c["iota"][0:R, :], [R, SLOTS, TOPK], 1), ALU.is_equal))
                    link(v.tensor_tensor(onehot, onehot, bcast(i16f[0:R, :, x, :], shape, 2), ALU.mult))
                    link(v.tensor_reduce(ee[x][0:R, :], onehot3, AX_X, ALU.add))
                v.scalar_tensor_tensor(out=idx[0:R, :], in0=ee[0][0:R, :], scalar=float(NK), in1=ee[1][0:R, :],
                                       op0=ALU.mult, op1=ALU.add).then_inc(idx_ready, 1)
                dve.wait_ge(e_done, i + 1)
                link(v.tensor_reduce(zz[0:R, :], wgt[0:R], AX_X, ALU.add))
                link(v.reciprocal(zz[0:R, :], zz[0:R, :]))
                link.mark(v.tensor_tensor(wgt[0:R], wgt[0:R], bcast(zz[0:R, :], [R, HP, TOPK], 2), ALU.mult))
                hold(dve, chain, link.base + link.n, dve_held)
                if first:
                    STEPS[0] = link.n
                assert link.n == STEPS[0]
                w2 = wgt[:].rearrange("p h s -> p (h s)")
                with dve.Fori(0, HP) as h:
                    for half in range(HALVES):
                        batch = i * (SLOTS // RING) + h * HALVES + half
                        for j in range(RING):
                            dve.wait_ge(landed[j], 16 * batch + 16)
                            if j == 0:
                                pass
                            ins = v.tensor_tensor_reduce(out=ring[0:R, j, 0:D], in0=ring[0:R, j, 0:D],
                                                         in1=n2[0:R, :], scale=1.0, scalar=0.0, op0=ALU.mult,
                                                         op1=ALU.add, accum_out=dots[0:R, half, j:j + 1])
                        ins.then_inc(dots_ready, 1)
                        dve.wait_ge(gel_ready, batch + 1)
                        v.tensor_tensor(coef[0:R, half, :], gel[0:R, half, :],
                                        w2[0:R, bass.ds(h * TOPK + half * RING, RING)], ALU.mult
                                        ).then_inc(coef_ready, 1)
                        dve.wait_ge(coef_ready, batch + 1)
                        for j in range(RING):
                            n = i * SLOTS + h * TOPK + half * RING + j
                            if not (first and half == 0 and j == 0):
                                dve.wait_ge(slot_used, n)
                            v.scalar_tensor_tensor(out=hs[0:R, :], in0=ring[0:R, j, D:2 * D],
                                                   scalar=coef[0:R, half, j:j + 1], in1=hs[0:R, :],
                                                   op0=ALU.mult, op1=ALU.add).then_inc(slot_used, 1)
                dve.wait_ge(slot_used, (i + 1) * SLOTS)
                v.memset(c["zero1"][:], 0.0).then_inc(sum_ready, 1)
                dve.wait_ge(sum_ready, i + 1)
                dve.wait_ge(sq_done, 2 * i + 2)
                v.tensor_scalar(sm[0:R, 3:4], sm[0:R, 2:3], 1.0 / D, EPS, ALU.mult, ALU.add).then_inc(ms_ready, 1)
                dve.wait_ge(rms_ready, 2 * i + 2)
                v.reciprocal(sm[0:R, 3:4], sm[0:R, 3:4]).then_inc(coef_final, 1)
                dve.wait_ge(coef_final, i + 1)
                v.scalar_tensor_tensor(out=hs[0:R, :], in0=hs[0:R, :], scalar=sm[0:R, 3:4], in1=norm_f[0:R, :],
                                       op0=ALU.mult, op1=ALU.mult).then_inc(y_ready, 1)

            dve.wait_ge(w_landed, 16 * 5)
            tile(0, P, True)
            with dve.Fori(1, NP) as i:
                tile(i, P, False)
            tile(NP, NS, False)


def program(nc, io):
    with ExitStack() as st:
        top = Memory(nc, st)
        c = {
            "ident": top.sb("ident", [P, P]),
            "cmask": top.sb("cmask", [P, P]),
            "bmask": top.sb("bmask", [P, P]),
            "iota": top.sb("iota", [P, TOPK]),
            "pick": top.sb("pick", [NS, NS, P]),
            "own_token": top.sb("own_token", [64, NS]),
            "own_head": top.sb("own_head", [NS * H, H]),
            "sum_maps": top.sb("sum_maps", [64, NS * H]),
            "map_coef": top.sb("map_coef", [64, 1]),
            "neg_lam": top.sb("neg_lam", [P, 1]),
            "subln": top.sb("subln", [P, 1]),
            "gnorm": top.sb("gnorm", [P, 1]),
            "lb": top.sb("lb", [P, H]),
            "one_lb": top.sb("one_lb", [P, H]),
            "cache_rows": top.sb("cache_rows", [P, NS * PAGES], U32),
            "zero1": top.sb("zero1", [P, 1]),
            "zeros_i": top.sb("zeros_i", [P, 1]),
            "k_new": top.sb("k_new", [NS, 512]),
            "q_new": top.sb("q_new", [NS, 512]),
        }
        io["mt"] = nc.dram_tensor("mt_scratch", [KD, P, T], F32, kind="Internal").ap()
        with ExitStack() as st2:
            mid = Memory(nc, st2)
            c["xnt"] = mid.sb("xnt", [P, KD, T])
            normalise(nc, mid, top, io, c)
            c["oat"] = mid.sb("oat", [P, H, T])
            with ExitStack() as st3:
                inner = Memory(nc, st3)
                c["qkf"] = inner.sb("qkf", [P, N_QKF, T])
                c["obt"] = c["qkf"][:, CHQ:CHQ + H, :]
                with ExitStack() as st4:
                    c["vig"] = Memory(nc, st4).sb("vig", [P, 3, NT, 512])
                    project(nc, inner, top, io, c)
                    attend_prompt(nc, inner, top, io, c)
                    attend_sample(nc, inner, top, io, c)
                    hgrn(nc, inner, top, io, c)
                merge(nc, inner, top, io, c)
        experts(nc, top, top, io, c)


def lay_out(inputs):
    import numpy as np

    a = {k: np.asarray(v) for k, v in inputs.items()}
    w_in = a["w_in"][0]
    cols = lambda lo, n: w_in[:, lo:lo + n]
    turned = np.concatenate([cols(0, 1024), cols(1536, 1024), cols(3584, 2048)], axis=1)
    by_rows = np.concatenate([cols(1024, 512), cols(2560, 1024)], axis=1)

    def chunks(w, n):
        k = w.shape[0] // P
        return w.reshape(k, P, w.shape[1] // n, n).transpose(2, 1, 0, 3)

    out = {
        "x": np.concatenate([a["x_prompt"].reshape(SEQ, D), a["x_sample"].reshape(NS, D)]),
        "norm1": a["norm1_w"].reshape(KD, P).T,
        "lam_w": np.concatenate([a["lambda_q1"], a["lambda_q2"], a["lambda_k1"], a["lambda_k2"]]).reshape(1, 4 * DH),
        "lb_w": a["lb_param"].reshape(2, H, P).transpose(2, 0, 1),
        "subln": a["subln_w"].reshape(P, 1),
        "gnorm": a["gnorm_w"].reshape(P, 1),
        "pages": a["page_table"].reshape(1, NS * PAGES),
        "w_t": chunks(turned, P),
        "w_n": chunks(by_rows, 512),
        "cache_k": a["cache_k"].reshape(-1, 512),
        "cache_v": a["cache_v"].reshape(-1, 512),
        "state": a["state_hgrn"][0].transpose(2, 0, 1, 3),
        "wa": chunks(a["w_branch_a"][0], P),
        "wb": chunks(a["w_branch_b"][0], P),
        "w_out": chunks(a["w_out"][0], D)[0],
        "w_query": chunks(a["w_query"][0], D)[0],
        "keys": a["sub_keys"][0].transpose(1, 3, 0, 2).reshape(P, HP, NK),
        "norm2": a["norm2_w"].reshape(1, D),
        "norm_f": a["norm_f_w"].reshape(1, D),
        "experts": np.concatenate([a["expert_u"][0], a["expert_v"][0]], axis=1),
    }
    return {k: np.ascontiguousarray(v) for k, v in out.items()}


OUTS = {
    "y": [T, D], "k_out": [T, 512], "v_out": [T, 512],
    "state_prompt": [H, P, DV], "state_sample": [P, NS, H, DV],
}


def kernel(**inputs):
    import numpy as np
    import concourse.bacc as bacc
    from concourse.bass_utils import run_bass_kernel_spmd

    nc = bacc.Bacc("TRN2", target_bir_lowering=False, num_devices=1)
    laid = lay_out(inputs)
    arrays = {f"in_{n}": a for n, a in laid.items()}
    io = {n: nc.dram_tensor(f"in_{n}", a.shape, mybir.dt.from_np(a.dtype), kind="ExternalInput").ap()
          for n, a in laid.items()}
    for n, shape in OUTS.items():
        io[n] = nc.dram_tensor(n, shape, F32, kind="ExternalOutput").ap()
    program(nc, io)
    r = run_bass_kernel_spmd(nc, [arrays], core_ids=[0]).results[0]
    y, k, v = (np.asarray(r[n]) for n in ("y", "k_out", "v_out"))
    return (y[:SEQ].reshape(1, SEQ, D), y[SEQ:].reshape(NS, 1, D),
            k[:SEQ].reshape(1, 1, SEQ, H, 2, DH), v[:SEQ].reshape(1, 1, SEQ, H, DV),
            np.asarray(r["state_prompt"]).reshape(1, 1, H, P, DV),
            k[SEQ:].reshape(1, NS, 1, H, 2, DH), v[SEQ:].reshape(1, NS, 1, H, DV),
            np.asarray(r["state_sample"]).transpose(1, 2, 0, 3).reshape(1, NS, H, P, DV))
```

```python
import math
from contextlib import ExitStack

import concourse.bass as bass
from concourse import mybir

ALU = mybir.AluOpType
ACT = mybir.ActivationFunctionType
AX_X = mybir.AxisListType.X
F32 = mybir.dt.float32
I32 = mybir.dt.int32
U32 = mybir.dt.uint32

P = 128
D = 1024
SEQ = 1024
NS = 8
T = SEQ + NS
NP = SEQ // P
NT = NP + 1
KD = D // P
H = 4
DH = 64
DV = 128
PAGE = 128
PAGES = 4
EPS = 1e-6
LAM_INIT = 0.8 - 0.6 * math.exp(-0.3 * 0)
QK_SCALE = DH ** -0.5
HG_SCALE = 128 ** -0.5
CH = 32
NCH = SEQ // CH
HP = 8
NK = 128
TOPK = 16
SLOTS = HP * TOPK
RING = 8
NEG = -1e30
LOWEST = -3.0e38
CQ, CK, CHQ, CHF, CGA, CGB = 0, 4, 8, 12, 16, 24
N_QKF = 16
SLICES = ((0, 512), (512, 512), (SEQ, NS))


def rows(i):
    return P if i < NP else NS


class Chain:

    def __init__(self, eng, sem, base=0):
        self.eng, self.sem, self.base, self.n = eng, sem, base, 0

    def mark(self, ins):
        self.n += 1
        ins.then_inc(self.sem, 1)

    def wait(self):
        self.eng.wait_ge(self.sem, self.base + self.n)

    def __call__(self, ins):
        self.mark(ins)
        self.wait()


def hold(eng, sem, value, carrier):
    eng.wait_ge(sem, value)
    eng.sem_inc(carrier, 1)


class Memory:

    def __init__(self, nc, stack):
        self.nc, self.stack = nc, stack

    def sb(self, name, shape, dt=F32):
        return self.stack.enter_context(self.nc.sbuf_tensor(name, shape, dt))

    def ps(self, name, shape):
        return self.stack.enter_context(self.nc.psum_tensor(name, shape, F32))



class Stage:

    def __init__(self, nc):
        self.nc, self.sems = nc, []

    def sem(self, name):
        self.sems.append(self.nc.alloc_semaphore(name=name))
        return self.sems[-1]

    def end(self):
        self.nc.clear_and_free_semaphores(self.sems)
        self.nc.all_engine_barrier()


def bcast(ap, shape, axis):
    return ap.unsqueeze(axis).to_broadcast(shape)


def normalise(nc, top, io, c):
    with ExitStack() as st:
        m = Memory(nc, st)
        xs = m.sb("xs", [P, NT, D])
        xn = m.sb("xn", [P, NT, D])
        ss = m.sb("ss", [P, NT])
        rstd = m.sb("rstd", [P, NT])
        norm1 = m.sb("norm1", [P, KD])
        lam_w = m.sb("lam_w", [P, 2, 2, DH])
        lam_p = m.sb("lam_p", [P, 2, DH])
        lam_s = m.sb("lam_s", [P, 2])
        lb_w = m.sb("lb_w", [P, 2, H])
        lb_m = m.sb("lb_m", [P, H])
        pages = m.sb("pages", [P, NS * PAGES], I32)
        pidx_i = m.sb("pidx_i", [P, 1], I32)
        pidx = m.sb("pidx", [P, 1])
        iota_i = m.sb("iota_i", [P, TOPK], I32)
        halves = m.sb("halves", [64, 2, NS])
        heads = m.sb("heads", [32, H, NS])
        tp = [m.ps(f"n_tp{b}", [P, KD, P]) for b in range(2)]

        tail_zeroed = top.sem("tail_zeroed")
        x_landed = top.sem("x_landed")
        small_landed = top.sem("small_landed")
        squares = top.sem("squares")
        mean_ready = top.sem("mean_ready")
        root_ready = top.sem("root_ready")
        xn_ready = top.sem("xn_ready")
        xn_turned = top.sem("xn_turned")
        xnt_stored = top.sem("xnt_stored")
        lam_sum = top.sem("lam_sum")
        lam_exp = top.sem("lam_exp")
        pool_chain = top.sem("norm_pool_chain")
        dve_chain = top.sem("norm_dve_chain")
        ident_ready = top.sem("ident_ready")
        masks_ready = top.sem("masks_ready")
        block = st.enter_context(nc.Block())

        @block.sync
        def _(sp):
            sp.dma_start(norm1[:], io["norm1"]).then_inc(small_landed, 16)
            sp.dma_start(lam_w[:].rearrange("p a b d -> p (a b d)"),
                         io["lam_w"].to_broadcast([P, 4 * DH])).then_inc(small_landed, 16)
            sp.dma_start(lb_w[:], io["lb_w"]).then_inc(small_landed, 16)
            sp.dma_start(c["subln"][:], io["subln"]).then_inc(small_landed, 16)
            sp.dma_start(c["gnorm"][:], io["gnorm"]).then_inc(small_landed, 16)
            sp.dma_start(pages[:], io["pages"].to_broadcast([P, NS * PAGES])).then_inc(small_landed, 16)
            sp.wait_ge(tail_zeroed, 1)
            sp.dma_start(xs[0:NS, NP, :], io["x"][SEQ:T, :]).then_inc(x_landed, 16)
            sp.dma_start(xs[:, 0:NP, :], io["x"][0:SEQ, :].rearrange("(t p) d -> p t d", p=P)
                         ).then_inc(x_landed, 16)

        @block.gpsimd
        def _(pool):
            link = Chain(pool, pool_chain)
            g = nc.gpsimd
            ident, cmask, bmask = c["ident"], c["cmask"], c["bmask"]
            link(g.memset(ident[:], 0.0))
            g.affine_select(out=ident[:], in_=ident[:], compare_op=ALU.not_equal, fill=1.0, base=0,
                            pattern=[[-1, P]], channel_multiplier=1).then_inc(ident_ready, 1)
            link(g.memset(cmask[:], 0.0))
            link(g.affine_select(out=cmask[:], in_=cmask[:], compare_op=ALU.is_ge, fill=NEG, base=0,
                                 pattern=[[-1, P]], channel_multiplier=1))
            link(g.memset(bmask[:], 1.0))
            link(g.affine_select(out=bmask[:], in_=bmask[:], compare_op=ALU.is_ge, fill=0.0, base=0,
                                 pattern=[[1, P]], channel_multiplier=-1))
            b3 = bmask[:].rearrange("p (a b) -> p a b", b=CH)
            link(g.affine_select(out=b3, in_=b3, compare_op=ALU.is_ge, fill=0.0, base=0,
                                 pattern=[[-CH, P // CH], [0, CH]], channel_multiplier=1))
            link(g.iota(iota_i[:], pattern=[[1, TOPK]], base=0, channel_multiplier=0))
            link(g.tensor_copy(c["iota"][:], iota_i[:]))
            link(g.iota(pidx_i[:], pattern=[[0, 1]], base=0, channel_multiplier=1))
            link(g.tensor_copy(pidx[:], pidx_i[:]))
            link(g.memset(c["pick"][:], 0.0))
            link(g.affine_select(out=c["pick"][:], in_=c["pick"][:], compare_op=ALU.not_equal, fill=1.0,
                                 base=0, pattern=[[-1, NS], [0, P]], channel_multiplier=1))
            link(g.memset(halves[:], 1.0))
            link(g.affine_select(out=halves[:], in_=halves[:], compare_op=ALU.is_ge, fill=0.0, base=0,
                                 pattern=[[-32, 2], [-H, NS]], channel_multiplier=1))
            link(g.affine_select(out=halves[:], in_=halves[:], compare_op=ALU.is_ge, fill=0.0, base=H - 1,
                                 pattern=[[32, 2], [H, NS]], channel_multiplier=-1))
            link(g.tensor_tensor(c["own_token"][:], halves[:, 0, :], halves[:, 1, :], ALU.add))
            link(g.memset(heads[:], 0.0))
            link(g.affine_select(out=heads[:], in_=heads[:], compare_op=ALU.not_equal, fill=1.0, base=0,
                                 pattern=[[-1, H], [-H, NS]], channel_multiplier=1))
            g.memset(c["zeros_i"][:], 0.0).then_inc(masks_ready, 1)

        @block.scalar
        def _(act):
            act.wait_ge(x_landed, 32)
            for i in range(NT):
                nc.scalar.activation(xn[:, i, :], xs[:, i, :], ACT.Square,
                                     accum_out=ss[:, i:i + 1]).then_inc(squares, 1)
            act.wait_ge(mean_ready, 1)
            nc.scalar.activation(rstd[:], ss[:], ACT.Sqrt).then_inc(root_ready, 1)
            act.wait_ge(lam_sum, 1)
            nc.scalar.activation(lam_s[:], lam_s[:], ACT.Exp).then_inc(lam_exp, 1)
            act.wait_ge(lam_sum, 2)
            nc.scalar.activation(lb_w[:], lb_w[:], ACT.Exp).then_inc(lam_exp, 1)

        @block.vector
        def _(dve):
            link = Chain(dve, dve_chain)
            v = nc.vector
            v.memset(xs[:, NP, :], 0.0).then_inc(tail_zeroed, 1)
            dve.wait_ge(small_landed, 6 * 16)
            link(v.tensor_tensor(lam_p[:], lam_w[:, 0], lam_w[:, 1], ALU.mult))
            v.tensor_reduce(lam_s[:], lam_p[:], AX_X, ALU.add).then_inc(lam_sum, 1)
            link(v.tensor_tensor(lb_m[:], lb_w[:, 0, :], lb_w[:, 1, :], ALU.max))
            v.tensor_tensor(lb_w[:], lb_w[:], bcast(lb_m[:], [P, 2, H], 1), ALU.subtract).then_inc(lam_sum, 1)
            link(v.tensor_scalar(c["subln"][:], c["subln"][:], 1.0 - LAM_INIT, None, ALU.mult))
            dve.wait_ge(squares, NT)
            link(v.tensor_scalar(ss[:], ss[:], 1.0 / D, EPS, ALU.mult, ALU.add))
            v.memset(c["zero1"][:], 0.0).then_inc(mean_ready, 1)
            dve.wait_ge(root_ready, 1)
            link(v.reciprocal(rstd[:], rstd[:]))
            v.tensor_tensor(xn[:], xs[:], bcast(rstd[:], [P, NT, D], 2), ALU.mult).then_inc(xn_ready, 1)
            for i in range(NT):
                dve.wait_ge(xn_turned, i + 1)
                v.tensor_tensor(c["xnt"][:, :, i * P:i * P + rows(i)], tp[i % 2][:, :, 0:rows(i)],
                                bcast(norm1[:], [P, KD, rows(i)], 2), ALU.mult).then_inc(xnt_stored, 1)
            dve.wait_ge(lam_exp, 1)
            link(v.tensor_tensor(c["neg_lam"][:], lam_s[:, 1:2], lam_s[:, 0:1], ALU.subtract))
            link(v.tensor_scalar(c["neg_lam"][:], c["neg_lam"][:], -LAM_INIT, None, ALU.add))
            link(v.memset(c["map_coef"][:], 1.0))
            link(v.tensor_copy(c["map_coef"][32:64, :], c["neg_lam"][32:64, :]))
            dve.wait_ge(lam_exp, 2)
            link(v.tensor_tensor(lb_m[:], lb_w[:, 0, :], lb_w[:, 1, :], ALU.add))
            link(v.reciprocal(lb_m[:], lb_m[:]))
            link(v.tensor_tensor(c["lb"][:], lb_w[:, 0, :], lb_m[:], ALU.mult))
            link(v.tensor_scalar(c["one_lb"][:], c["lb"][:], -1.0, 1.0, ALU.mult, ALU.add))
            dve.wait_ge(masks_ready, 1)
            link(v.tensor_scalar(c["cache_rows"][:], pages[:], float(PAGE), pidx[:, 0:1], ALU.mult, ALU.add))
            link(v.tensor_reduce(c["own_head"][:], heads[:], AX_X, ALU.add))
            link(v.tensor_tensor(c["sum_maps"][:], c["ident"][0:64, 0:32], c["ident"][0:64, 32:64], ALU.add))

        @block.tensor
        def _(pe):
            pe.wait_ge(ident_ready, 1)
            pe.wait_ge(xn_ready, 1)
            for i in range(NT):
                if i >= 2:
                    pe.wait_ge(xnt_stored, i - 1)
                for k in range(KD):
                    last = nc.tensor.transpose(tp[i % 2][:, k, :], xn[:, i, k * P:(k + 1) * P], c["ident"][:])
                last.then_inc(xn_turned, 1)


def project(nc, top, io, c):
    qkf, vig, xnt, ident = c["qkf"], c["vig"], c["xnt"], c["ident"]
    with ExitStack() as st:
        m = Memory(nc, st)
        wt = [m.sb(f"wt{u}", [P, KD, P]) for u in range(2)]
        wn = m.sb("wn", [P, KD, 512])
        kst = [m.sb(f"kst{u}", [P, 512]) for u in range(2)]
        pt = [[m.ps(f"pt{u}_{s}", [P, 512]) for s in range(3)] for u in range(2)]
        pn = [m.ps(f"pn{u}", [P, 512]) for u in range(2)]

        wt_landed = [top.sem(f"wt_landed{u}") for u in range(2)]
        wt_used = [top.sem(f"wt_used{u}") for u in range(2)]
        cols_stored = [top.sem(f"cols_stored{u}") for u in range(2)]
        wn_landed = top.sem("wn_landed")
        rows_done = [top.sem(f"rows_done{u}") for u in range(2)]
        rows_stored = [top.sem(f"rows_stored{u}") for u in range(2)]
        tail_clear = top.sem("vig_tail_clear")
        k_saved = [top.sem(f"k_saved{u}") for u in range(2)]
        v_saved = top.sem("v_saved")
        sp_held = top.sem("p_sp_held")
        block = st.enter_context(nc.Block())
        n_rows = 3 * NT

        @block.sync
        def _(sp):
            for u in range(2):
                sp.dma_start(wt[u][:], io["w_t"][u]).then_inc(wt_landed[u], 16)
            sp.dma_start(wn[:], io["w_n"][0]).then_inc(wn_landed, 16)
            with sp.Fori(1, N_QKF // 2) as j:
                for u in range(2):
                    hold(sp, wt_used[u], j, sp_held)
                    sp.dma_start(wt[u][:], io["w_t"][bass.ds(2 * j + u, 1)].rearrange(
                        "a p k n -> (a p) k n")).then_inc(wt_landed[u], 16)
            for b in range(1, 3):
                for u in range(2):
                    sp.wait_ge(rows_done[u], (NT * b + 1 - u) // 2)
                sp.dma_start(wn[:], io["w_n"][b]).then_inc(wn_landed, 16)
            for u in range(2):
                sp.wait_ge(rows_stored[u], (NT + 1 - u) // 2)
            sp.dma_start(io["v_out"][0:SEQ, :].rearrange("(t p) n -> p t n", p=P), vig[:, 0, 0:NP, :]
                         ).then_inc(v_saved, 16)
            sp.dma_start(io["v_out"][SEQ:T, :], vig[0:NS, 0, NP, :]).then_inc(v_saved, 16)
            for i in range(NT):
                n = n_rows + i
                sp.wait_ge(rows_stored[n % 2], n // 2 + 1)
                src = kst[n % 2][:] if i < NP else c["k_new"][:]
                sp.dma_start(io["k_out"][i * P:i * P + rows(i), :], src).then_inc(k_saved[n % 2], 16)
            sp.wait_ge(v_saved, 32)
            for u in range(2):
                sp.wait_ge(k_saved[u], 16 * len([i for i in range(NT) if (n_rows + i) % 2 == u]))

        def store_cols(eng, copy, u):
            def one(j, first):
                eng.wait_ge(wt_used[u], j + 1)
                for s, (t0, n) in enumerate(SLICES):
                    last = copy(qkf[:, 0 + u, t0:t0 + n] if first else
                                qkf[:, bass.ds(2 * j + u, 1), t0:t0 + n].rearrange("p a t -> p (a t)"),
                                pt[u][s][:, 0:n])
                    last.then_inc(cols_stored[u], 1)
            one(0, True)
            with eng.Fori(1, N_QKF // 2) as j:
                one(j, False)

        def store_rows(eng, copy, u):
            if u == 0:
                eng.wait_ge(tail_clear, 1)
            else:
                eng.wait_ge(tail_clear, 1)
            for n in range(n_rows + NT + 1):
                if n % 2 != u:
                    continue
                i = n - n_rows
                eng.wait_ge(rows_done[u], n // 2 + 1)
                if i < 0:
                    dst = vig[0:rows(n % NT), n // NT, n % NT, :]
                elif i < NP:
                    dst = kst[u][:]
                    if i >= 2:
                        eng.wait_ge(k_saved[u], 16 * (i // 2))
                elif i == NP:
                    dst = c["k_new"][:]
                else:
                    dst = c["q_new"][:]
                copy(dst, pn[u][0:dst.shape[0], :]).then_inc(rows_stored[u], 1)

        @block.scalar
        def _(act):
            store_cols(act, nc.scalar.copy, 1)
            store_rows(act, nc.scalar.copy, 1)

        @block.vector
        def _(dve):
            nc.vector.memset(vig[:, :, NP, :], 0.0).then_inc(tail_clear, 1)
            store_cols(dve, nc.vector.tensor_copy, 0)
            store_rows(dve, nc.vector.tensor_copy, 0)

        @block.tensor
        def _(pe):
            def chunk(u, j, first):
                if not first:
                    pe.wait_ge(cols_stored[u], 3 * j)
                pe.wait_ge(wt_landed[u], 16 * (j + 1))
                for k in range(KD):
                    for s, (t0, n) in enumerate(SLICES):
                        last = nc.tensor.matmul(pt[u][s][:, 0:n], wt[u][:, k, :], xnt[:, k, t0:t0 + n],
                                                start=(k == 0), stop=(k == KD - 1))
                last.then_inc(wt_used[u], 1)
            for u in range(2):
                chunk(u, 0, True)
            with pe.Fori(1, N_QKF // 2) as j:
                for u in range(2):
                    chunk(u, j, False)
            for n in range(n_rows + NT + 1):
                u, i = n % 2, n - n_rows
                if n >= 2:
                    pe.wait_ge(rows_stored[u], n // 2)
                if i < 0:
                    pe.wait_ge(wn_landed, 16 * (n // NT + 1))
                    t = n % NT
                    for k in range(KD):
                        last = nc.tensor.matmul(pn[u][0:rows(t), :], xnt[:, k, t * P:t * P + rows(t)],
                                                wn[:, k, :], start=(k == 0), stop=(k == KD - 1))
                else:
                    if n == n_rows:
                        for w in range(2):
                            pe.wait_ge(cols_stored[w], 3 * N_QKF // 2)
                    t, c0 = (i, CK) if i < NT else (NP, CQ)
                    for h in range(H):
                        last = nc.tensor.transpose(pn[u][0:rows(t), h * P:(h + 1) * P],
                                                   qkf[:, c0 + h, t * P:t * P + rows(t)], ident[:])
                last.then_inc(rows_done[u], 1)


def attend_prompt(nc, top, io, c):
    qkf, vig, ident, oat = c["qkf"], c["vig"], c["ident"], c["oat"]
    units = [(i, h) for i in range(NP) for h in range(H)]
    with ExitStack() as st:
        m = Memory(nc, st)
        prob = [[m.sb(f"prob{b}{k}", [P, SEQ]) for k in range(2)] for b in range(2)]
        probt = m.sb("probt", [P, SEQ])
        stat = {n: m.sb(f"at_{n}", [P, 2 * len(units)]) for n in ("top", "neg", "sum", "inv")}
        o_sb = m.sb("o_sb", [P, H, DV])
        o_sq = m.sb("o_sq", [P, H, DV])
        o_ss = m.sb("o_ss", [P, NP, H])
        sc = [m.ps(f"sc{k}", [P, SEQ]) for k in range(2)]
        pt = m.ps("at_pt", [P, SEQ])
        o_ps = m.ps("o_ps", [P, H, DV])
        ot_ps = m.ps("ot_ps", [P, H, P])

        scores_done = top.sem("at_scores_done")
        neg_ready = top.sem("at_neg_ready")
        exp_done = top.sem("at_exp_done")
        diff_ready = top.sem("at_diff_ready")
        turned = top.sem("at_turned")
        probt_ready = top.sem("at_probt_ready")
        pv_done = top.sem("at_pv_done")
        o_taken = top.sem("at_o_taken")
        ms_ready = top.sem("at_ms_ready")
        rms_ready = top.sem("at_rms_ready")
        on_ready = top.sem("at_on_ready")
        on_turned = top.sem("at_on_turned")
        oat_stored = top.sem("at_oat_stored")
        chain = top.sem("at_chain")
        block = st.enter_context(nc.Block())

        @block.tensor
        def _(pe):
            def scores(u):
                i, h = units[u]
                w = (i + 1) * P
                for k in range(2):
                    if u >= 1:
                        pe.wait_ge(exp_done, 2 * (u - 1) + k + 1)
                    for k0 in range(0, w, 512):
                        n = min(512, w - k0)
                        last = nc.tensor.matmul(sc[k][:, k0:k0 + n],
                                                qkf[k * DH:(k + 1) * DH, CQ + h, i * P:(i + 1) * P],
                                                qkf[k * DH:(k + 1) * DH, CK + h, k0:k0 + n],
                                                start=True, stop=True)
                    last.then_inc(scores_done, 1)

            def turn(u):
                i, h = units[u]
                pe.wait_ge(diff_ready, u + 1)
                if u >= 1:
                    pe.wait_ge(probt_ready, u)
                for b in range(i + 1):
                    last = nc.tensor.transpose(pt[:, b * P:(b + 1) * P], prob[u % 2][0][:, b * P:(b + 1) * P],
                                               ident[:])
                last.then_inc(turned, 1)

            def pv(u):
                i, h = units[u]
                pe.wait_ge(probt_ready, u + 1)
                if h == 0 and i >= 1:
                    pe.wait_ge(o_taken, i)
                for b in range(i + 1):
                    last = nc.tensor.matmul(o_ps[:, h, :], probt[:, b * P:(b + 1) * P],
                                            vig[:, 0, b, h * DV:(h + 1) * DV], start=(b == 0), stop=(b == i))
                last.then_inc(pv_done, 1)

            def turn_out(i):
                pe.wait_ge(on_ready, i + 1)
                if i >= 1:
                    pe.wait_ge(oat_stored, i)
                for h in range(H):
                    last = nc.tensor.transpose(ot_ps[:, h, :], o_sb[:, h, :], ident[:])
                last.then_inc(on_turned, 1)

            scores(0)
            for u in range(len(units)):
                if u + 1 < len(units):
                    scores(u + 1)
                turn(u)
                pv(u)
                if u % H == 0 and u:
                    turn_out(u // H - 1)
            turn_out(NP - 1)

        @block.scalar
        def _(act):
            def exps(u):
                w = (units[u][0] + 1) * P
                for k in range(2):
                    q = 2 * u + k
                    act.wait_ge(neg_ready, q + 1)
                    if u >= 2:
                        act.wait_ge(turned, u - 1)
                    nc.scalar.activation(prob[u % 2][k][:, 0:w], sc[k][:, 0:w], ACT.Exp, scale=QK_SCALE,
                                         bias=stat["neg"][:, q:q + 1],
                                         accum_out=stat["sum"][:, q:q + 1]).then_inc(exp_done, 1)

            def store(u):
                w = (units[u][0] + 1) * P
                act.wait_ge(turned, u + 1)
                if u >= 1:
                    act.wait_ge(pv_done, u)
                nc.scalar.copy(probt[:, 0:w], pt[:, 0:w]).then_inc(probt_ready, 1)

            def post(i):
                act.wait_ge(ms_ready, i + 1)
                nc.scalar.activation(o_ss[:, i, :], o_ss[:, i, :], ACT.Sqrt).then_inc(rms_ready, 1)
                act.wait_ge(on_turned, i + 1)
                nc.scalar.activation(oat[:, :, i * P:(i + 1) * P], ot_ps[:], ACT.Copy,
                                     scale=c["subln"][:, 0:1]).then_inc(oat_stored, 1)

            exps(0)
            for u in range(len(units)):
                if u + 1 < len(units):
                    exps(u + 1)
                store(u)
                if u % H == 0 and u:
                    post(u // H - 1)
            post(NP - 1)

        @block.vector
        def _(dve):
            link = Chain(dve, chain)
            v = nc.vector

            def tops(u):
                i, h = units[u]
                w = (i + 1) * P
                for k in range(2):
                    q = 2 * u + k
                    dve.wait_ge(scores_done, q + 1)
                    link(v.tensor_tensor(sc[k][:, i * P:w], sc[k][:, i * P:w], c["cmask"][:], ALU.add))
                    link(v.reduce_max(stat["top"][:, q:q + 1], sc[k][:, 0:w], AX_X))
                    v.tensor_scalar(stat["neg"][:, q:q + 1], stat["top"][:, q:q + 1], -QK_SCALE, None,
                                    ALU.mult).then_inc(neg_ready, 1)

            def differ(u):
                w = (units[u][0] + 1) * P
                a, b = prob[u % 2][0][:, 0:w], prob[u % 2][1][:, 0:w]
                q = 2 * u
                dve.wait_ge(exp_done, q + 2)
                link(v.reciprocal(stat["inv"][:, q:q + 2], stat["sum"][:, q:q + 2]))
                link(v.tensor_scalar(stat["inv"][:, q + 1:q + 2], stat["inv"][:, q + 1:q + 2],
                                     c["neg_lam"][:, 0:1], None, ALU.mult))
                link(v.tensor_scalar(a, a, stat["inv"][:, q:q + 1], None, ALU.mult))
                v.scalar_tensor_tensor(out=a, in0=b, scalar=stat["inv"][:, q + 1:q + 2], in1=a,
                                       op0=ALU.mult, op1=ALU.add).then_inc(diff_ready, 1)

            def post(i):
                dve.wait_ge(pv_done, H * (i + 1))
                if i >= 1:
                    dve.wait_ge(on_turned, i)
                v.tensor_copy(o_sb[:], o_ps[:]).then_inc(o_taken, 1)
                dve.wait_ge(o_taken, i + 1)
                link(v.tensor_tensor(o_sq[:], o_sb[:], o_sb[:], ALU.mult))
                link(v.tensor_reduce(o_ss[:, i, :], o_sq[:], AX_X, ALU.add))
                v.tensor_scalar(o_ss[:, i, :], o_ss[:, i, :], 1.0 / DV, EPS, ALU.mult, ALU.add
                                ).then_inc(ms_ready, 1)
                dve.wait_ge(rms_ready, i + 1)
                link(v.reciprocal(o_ss[:, i, :], o_ss[:, i, :]))
                v.tensor_tensor(o_sb[:], o_sb[:], bcast(o_ss[:, i, :], [P, H, DV], 2), ALU.mult
                                ).then_inc(on_ready, 1)

            tops(0)
            for u in range(len(units)):
                if u + 1 < len(units):
                    tops(u + 1)
                differ(u)
                if u % H == 0 and u:
                    post(u // H - 1)
            post(NP - 1)


def attend_sample(nc, top, io, c):
    qkf, vig, ident = c["qkf"], c["vig"], c["ident"]
    G = PAGES + 1
    NR = 2 * NS * H
    with ExitStack() as st:
        m = Memory(nc, st)
        ring = qkf[:, 0:8, :].rearrange("p a t -> p (a t)")[:, 0:4 * PAGES * 512].rearrange(
            "p (r g n) -> p r g n", r=4, g=PAGES)
        q_b = m.sb("q_b", [P, 512])
        own = m.sb("own", [P, 512])
        sco = m.sb("sco", [P, G, 2, NS, H])
        pr = m.sb("pr", [NR, G * PAGE])
        mx = m.sb("as_mx", [NR, 4])
        pown = m.sb("pown", [NR, NS])
        own_w = m.sb("own_w", [NS, NS * H])
        wz = m.sb("wz", [P, NS, PAGES, NS * H])
        osel = m.sb("osel", [NS * H, H, DV])
        o_sb = m.sb("as_o", [NS, H, DV])
        o_sq = m.sb("as_sq", [NS, H, DV])
        o_ss = m.sb("as_ss", [NS, H])
        qb_ps = m.ps("qb_ps", [P, 512])
        kb_ps = m.ps("kb_ps", [P, 512])
        s_ps = m.ps("s_ps", [NR, 2, 512])
        w_ps = m.ps("w_ps", [P, PAGES, NS * H])
        ow_ps = m.ps("ow_ps", [NS, NS * H])
        o_ps = m.ps("as_o_ps", [NS * H, H, DV])
        f_ps = m.ps("as_f_ps", [P, 512])

        row_landed = [top.sem(f"as_landed{r}") for r in range(4)]
        ring_free = top.sem("as_ring_free")
        q_spread = top.sem("as_q_spread")
        q_copied = top.sem("as_q_copied")
        q_used = top.sem("as_q_used")
        s_ready = top.sem("as_s_ready")
        s_turned = top.sem("as_s_turned")
        neg_ready = top.sem("as_neg_ready")
        exp_done = top.sem("as_exp_done")
        pr_ready = top.sem("as_pr_ready")
        w_done = top.sem("as_w_done")
        wz_ready = top.sem("as_wz_ready")
        v_used = top.sem("as_v_used")
        osel_ready = top.sem("as_osel_ready")
        o_done = top.sem("as_o_done")
        ms_ready = top.sem("as_ms_ready")
        rms_ready = top.sem("as_rms_ready")
        on_ready = top.sem("as_on_ready")
        on_turned = top.sem("as_on_turned")
        chain = top.sem("as_chain")
        pr_scores = s_ps[:].rearrange("p a b -> p (a b)")
        block = st.enter_context(nc.Block())

        @block.gpsimd
        def _(pool):
            for n in range(2 * NS):
                cache, b, r = io["cache_k"] if n < NS else io["cache_v"], n % NS, n % 4
                if 4 <= n:
                    if n - 4 < NS:
                        pool.wait_ge(ring_free, n - 3)
                    else:
                        pool.wait_ge(v_used, n - 3 - NS)
                for g in range(PAGES):
                    nc.gpsimd.indirect_dma_start(
                        out=ring[:, r, g, :], out_offset=None, in_=cache,
                        in_offset=bass.IndirectOffsetOnAxis(
                            ap=c["cache_rows"][:, b * PAGES + g:b * PAGES + g + 1], axis=0),
                    ).then_inc(row_landed[r], 16)

        @block.tensor
        def _(pe):
            for b in range(NS):
                if b >= 1:
                    pe.wait_ge(q_used, b)
                nc.tensor.matmul(qb_ps[:], c["pick"][:, b, :], c["q_new"][:], start=True, stop=True)
                nc.tensor.matmul(kb_ps[:], c["pick"][:, b, :], c["k_new"][:], start=True, stop=True
                                 ).then_inc(q_spread, 1)
            pe.wait_ge(s_ready, 1)
            for g in range(G):
                last = nc.tensor.transpose(pr_scores[:, g * P:(g + 1) * P],
                                           sco[:, g].rearrange("p c b h -> p (c b h)"), ident[:])
            last.then_inc(s_turned, 1)
            pe.wait_ge(pr_ready, 1)
            for g in range(PAGES):
                nc.tensor.matmul(w_ps[:, g, :], pr[:, g * P:(g + 1) * P], c["sum_maps"][:],
                                 start=True, stop=True)
            nc.tensor.matmul(ow_ps[:], pown[:], c["sum_maps"][:], start=True, stop=True).then_inc(w_done, 1)
            pe.wait_ge(wz_ready, 1)
            nc.tensor.matmul(o_ps[:].rearrange("p h d -> p (h d)"), own_w[:], vig[0:NS, 0, NP, :],
                             start=True, stop=False)
            for b in range(NS):
                pe.wait_ge(row_landed[b % 4], 16 * PAGES * ((NS + b) // 4 + 1))
                for g in range(PAGES):
                    last = nc.tensor.matmul(o_ps[:].rearrange("p h d -> p (h d)"), wz[:, b, g, :],
                                            ring[:, b % 4, g, :], start=False,
                                            stop=(b == NS - 1 and g == PAGES - 1))
                last.then_inc(v_used, 1)
            pe.wait_ge(osel_ready, 1)
            nc.tensor.matmul(f_ps[0:NS, :], c["own_token"][0:NS * H, :],
                             osel[:].rearrange("p h d -> p (h d)"), start=True, stop=True).then_inc(o_done, 1)
            pe.wait_ge(on_ready, 1)
            for h in range(H):
                last = nc.tensor.transpose(qb_ps[:, h * NS:(h + 1) * NS], o_sb[:, h, :], ident[0:NS, 0:NS])
            last.then_inc(on_turned, 1)

        @block.scalar
        def _(act):
            for b in range(NS):
                act.wait_ge(q_spread, b + 1)
                if b >= 1:
                    act.wait_ge(q_used, b)
                nc.scalar.copy(q_b[:], qb_ps[:]).then_inc(q_copied, 1)
            act.wait_ge(neg_ready, 1)
            nc.scalar.activation(pr[:, 0:PAGES * PAGE + 1], pr_scores[:, 0:PAGES * PAGE + 1], ACT.Exp,
                                 scale=QK_SCALE, bias=mx[:, 1:2], accum_out=mx[:, 2:3]).then_inc(exp_done, 1)
            act.wait_ge(ms_ready, 1)
            nc.scalar.activation(o_ss[:], o_ss[:], ACT.Sqrt).then_inc(rms_ready, 1)
            act.wait_ge(on_turned, 1)
            nc.scalar.activation(c["oat"][:, :, SEQ:T], qb_ps[:, 0:H * NS].rearrange("p (h b) -> p h b", h=H),
                                 ACT.Copy, scale=c["subln"][:, 0:1])

        @block.vector
        def _(dve):
            link = Chain(dve, chain)
            v = nc.vector
            link(v.memset(wz[:], 0.0))
            for b in range(NS):
                r = b % 4
                k_rows = ring[:, r]
                dve.wait_ge(q_copied, b + 1)
                dve.wait_ge(row_landed[r], 16 * PAGES * (b // 4 + 1))
                link(v.tensor_tensor(k_rows, k_rows, bcast(q_b[:], [P, PAGES, 512], 1), ALU.mult))
                for k in range(2):
                    last = v.tensor_reduce(
                        sco[:, 0:PAGES, k, b, :],
                        k_rows.rearrange("p g (h c d) -> p g h c d", h=H, c=2)[:, :, :, k, :], AX_X, ALU.add)
                    last.then_inc(ring_free, 1) if k else link(last)
                link(v.tensor_tensor(own[:], kb_ps[:], q_b[:], ALU.mult))
                last = v.tensor_reduce(sco[:, PAGES, :, b, :].rearrange("p c h -> p h c"),
                                       own[:].rearrange("p (h c d) -> p h c d", h=H, c=2), AX_X, ALU.add)
                last.then_inc(q_used, 1)
                dve.wait_ge(q_used, b + 1)
            dve.wait_ge(ring_free, NS)
            v.memset(mx[:], 0.0).then_inc(s_ready, 1)
            dve.wait_ge(s_ready, 1)
            dve.wait_ge(s_turned, 1)
            link(v.reduce_max(mx[:, 0:1], pr_scores[:, 0:PAGES * PAGE + 1], AX_X))
            v.tensor_scalar(mx[:, 1:2], mx[:, 0:1], -QK_SCALE, None, ALU.mult).then_inc(neg_ready, 1)
            dve.wait_ge(exp_done, 1)
            link(v.reciprocal(mx[:, 3:4], mx[:, 2:3]))
            link(v.tensor_tensor(mx[:, 3:4], mx[:, 3:4], c["map_coef"][:], ALU.mult))
            link(v.tensor_scalar(pr[:, 0:PAGES * PAGE + 1], pr[:, 0:PAGES * PAGE + 1], mx[:, 3:4], None, ALU.mult))
            v.tensor_scalar(pown[:], c["own_token"][:], pr[:, PAGES * PAGE:PAGES * PAGE + 1], None,
                            ALU.mult).then_inc(pr_ready, 1)
            dve.wait_ge(w_done, 1)
            link(v.tensor_copy(own_w[:], ow_ps[:]))
            for b in range(NS):
                last = v.tensor_copy(wz[:, b, :, b * H:(b + 1) * H], w_ps[:, :, b * H:(b + 1) * H])
                last.then_inc(wz_ready, 1) if b == NS - 1 else link(last)
            dve.wait_ge(v_used, NS)
            v.tensor_tensor(osel[:], o_ps[:], bcast(c["own_head"][:], [NS * H, H, DV], 2), ALU.mult
                            ).then_inc(osel_ready, 1)
            dve.wait_ge(o_done, 1)
            link(v.tensor_copy(o_sb[:], f_ps[0:NS, :].rearrange("p (h d) -> p h d", h=H)))
            link(v.tensor_tensor(o_sq[:], o_sb[:], o_sb[:], ALU.mult))
            link(v.tensor_reduce(o_ss[:], o_sq[:], AX_X, ALU.add))
            v.tensor_scalar(o_ss[:], o_ss[:], 1.0 / DV, EPS, ALU.mult, ALU.add).then_inc(ms_ready, 1)
            dve.wait_ge(rms_ready, 1)
            link(v.reciprocal(o_ss[:], o_ss[:]))
            v.tensor_tensor(o_sb[:], o_sb[:], bcast(o_ss[:], [NS, H, DV], 2), ALU.mult).then_inc(on_ready, 1)


def hgrn(nc, top, io, c):
    qkf, vig, ident, obt = c["qkf"], c["vig"], c["ident"], c["obt"]
    MID = CH // 2 - 1
    NB = P // CH
    with ExitStack() as st:
        m = Memory(nc, st)
        r = lambda n: qkf[:, n, 0:SEQ]
        KM, KK, GG, QM, G2, QE, KDN = range(7)
        kdn = qkf[:, KDN, 0:SEQ].rearrange("p (t n) -> p t n", t=NP)
        restart = m.sb("restart", [P, SEQ])
        apart = [m.sb(f"apart{b}", [P, NB, DV]) for b in range(2)]
        atm = [m.sb(f"atm{b}", [P, P]) for b in range(2)]
        state = [m.sb(f"state{b}", [P, DV]) for b in range(4)]
        tp = [m.ps(f"hg_tp{b}", [P, 4, P]) for b in range(2)]
        a_ps = [m.ps(f"hg_a{b}", [P, P]) for b in range(2)]
        o_ps = [m.ps(f"hg_o{b}", [P, DV]) for b in range(2)]
        u_ps = [m.ps(f"hg_u{b}", [P, NB, DV]) for b in range(2)]

        gates = top.sem("hg_gates")
        f_ready = top.sem("hg_f_ready")
        log_ready = top.sem("hg_log_ready")
        rel_ready = top.sem("hg_rel_ready")
        exps_done = top.sem("hg_exps_done")
        ops_ready = top.sem("hg_ops_ready")
        kd_turned = top.sem("hg_kd_turned")
        kd_stored = top.sem("hg_kd_stored")
        a_done = top.sem("hg_a_done")
        a_masked = top.sem("hg_a_masked")
        u_done = top.sem("hg_u_done")
        inter_done = top.sem("hg_inter_done")
        state_ready = top.sem("hg_state_ready")
        o_stored = top.sem("hg_o_stored")
        state_saved = top.sem("hg_state_saved")
        chain = top.sem("hg_chain")
        apart_zeroed = top.sem("hg_apart_zeroed")
        apart_ready = top.sem("hg_apart_ready")
        block = st.enter_context(nc.Block())

        @block.gpsimd
        def _(pool):
            for b in range(2):
                nc.gpsimd.memset(apart[b][:], 0.0).then_inc(apart_zeroed, 1)
            pool.wait_ge(apart_zeroed, 2)
            for n_tile in range(H * NP):
                h, i = divmod(n_tile, NP)
                if n_tile >= 2:
                    pool.wait_ge(u_done, n_tile - 1)
                for j in range(NB):
                    s = slice(j * CH, (j + 1) * CH)
                    nc.gpsimd.tensor_copy(apart[i % 2][s, j, :], vig[s, 1, i, h * DV:(h + 1) * DV]
                                          ).then_inc(apart_ready, 1)

        def state_count(h, n):
            return h * (NCH + 1) + n + 1

        @block.scalar
        def _(act):
            for h in range(H):
                q, f = qkf[:, CHQ + h, :], qkf[:, CHF + h, :]
                nc.scalar.activation(q, q, ACT.Silu).then_inc(gates, 1)
                nc.scalar.activation(f, f, ACT.Sigmoid).then_inc(gates, 1)
                act.wait_ge(f_ready, h + 1)
                nc.scalar.activation(r(KM), f[:, 0:SEQ], ACT.Ln).then_inc(log_ready, 1)
                act.wait_ge(rel_ready, h + 1)
                nc.scalar.activation(r(QM), r(KM), ACT.Exp).then_inc(exps_done, 1)
                act.wait_ge(exps_done, 4 * h + 1)
                nc.scalar.activation(r(KM), r(KM), ACT.Exp, scale=-1.0).then_inc(exps_done, 1)
                nc.scalar.activation(r(GG), r(GG), ACT.Exp).then_inc(exps_done, 1)
                nc.scalar.activation(r(G2), r(G2), ACT.Exp).then_inc(exps_done, 1)
                for half in range(2):
                    act.wait_ge(kd_turned, 2 * h + half + 1)
                    nc.scalar.copy(kdn[:, 4 * half:4 * half + 4, :], tp[half][:]).then_inc(kd_stored, 1)
                for i in range(NP):
                    act.wait_ge(inter_done, NB * (h * NP + i + 1))
                    nc.scalar.copy(vig[:, 0, i, h * DV:(h + 1) * DV], o_ps[i % 2][:]).then_inc(o_stored, 1)

        @block.vector
        def _(dve):
            link = Chain(dve, chain)
            v = nc.vector
            link(v.memset(restart[:], 1.0))
            link(v.memset(restart[:].rearrange("p (a b) -> p a b", b=CH)[:, :, 0:1], 0.0))
            for b in range(2):
                link(v.memset(atm[b][:], 0.0))
            for h in range(H):
                q, f = qkf[:, CHQ + h, :], qkf[:, CHF + h, :]
                lb, one_lb = c["lb"][:, h:h + 1], c["one_lb"][:, h:h + 1]
                dve.wait_ge(gates, 2 * h + 2)
                v.tensor_scalar(f, f, one_lb, lb, ALU.mult, ALU.add).then_inc(f_ready, 1)
                dve.wait_ge(f_ready, h + 1)
                link(v.tensor_scalar(r(KK), f[:, 0:SEQ], -1.0, 1.0, ALU.mult, ALU.add))
                dve.wait_ge(log_ready, h + 1)
                link(v.tensor_tensor_scan(r(GG), restart[:], r(KM), 0.0, ALU.mult, ALU.add))
                g3 = r(GG).rearrange("p (a b) -> p a b", b=CH)
                shape = [P, NCH, CH]
                link(v.tensor_tensor(r(KM).rearrange("p (a b) -> p a b", b=CH), g3,
                                     g3[:, :, MID:MID + 1].to_broadcast(shape), ALU.subtract))
                v.tensor_tensor(r(G2).rearrange("p (a b) -> p a b", b=CH),
                                g3[:, :, CH - 1:CH].to_broadcast(shape), g3, ALU.subtract).then_inc(rel_ready, 1)
                dve.wait_ge(exps_done, 4 * h + 4)
                sc = q[:, 0:SEQ]
                v.scalar_tensor_tensor(out=r(QM), in0=sc, scalar=HG_SCALE, in1=r(QM), op0=ALU.mult,
                                       op1=ALU.mult).then_inc(ops_ready, 1)
                v.tensor_tensor(r(KM), r(KK), r(KM), ALU.mult).then_inc(ops_ready, 1)
                v.scalar_tensor_tensor(out=r(QE), in0=sc, scalar=HG_SCALE, in1=r(GG), op0=ALU.mult,
                                       op1=ALU.mult).then_inc(ops_ready, 1)
                v.tensor_tensor(r(G2), r(KK), r(G2), ALU.mult).then_inc(ops_ready, 1)
                if h >= 1:
                    dve.wait_ge(state_saved, 16 * h)
                v.memset(state[0][:], 0.0).then_inc(state_ready, 1)
                for i in range(NP):
                    n_tile = h * NP + i
                    dve.wait_ge(a_done, n_tile + 1)
                    if n_tile >= 2:
                        dve.wait_ge(inter_done, NB * (n_tile - 1))
                    v.copy_predicated(atm[i % 2][:], c["bmask"][:].bitcast(U32), a_ps[i % 2][:]
                                      ).then_inc(a_masked, 1)
                    dve.wait_ge(u_done, n_tile + 1)
                    for j in range(NB):
                        n = i * NB + j
                        dve.wait_ge(state_ready, state_count(h, n))
                        if h * NCH + n >= 3:
                            dve.wait_ge(inter_done, h * NCH + n - 2)
                        v.scalar_tensor_tensor(out=state[(n + 1) % 4][:], in0=state[n % 4][:],
                                               scalar=r(GG)[:, n * CH + CH - 1:n * CH + CH],
                                               in1=u_ps[i % 2][:, j, :], op0=ALU.mult, op1=ALU.add
                                               ).then_inc(state_ready, 1)
                dve.wait_ge(state_ready, state_count(h, NCH))

        @block.tensor
        def _(pe):
            for h in range(H):
                pe.wait_ge(ops_ready, 4 * h + 4)
                for half in range(2):
                    if h >= 1:
                        pe.wait_ge(kd_stored, 2 * h)
                    for t in range(4):
                        i = 4 * half + t
                        last = nc.tensor.transpose(tp[half][:, t, :], r(G2)[:, i * P:(i + 1) * P], ident[:])
                    last.then_inc(kd_turned, 1)
                for i in range(NP):
                    n_tile = h * NP + i
                    tok = slice(i * P, (i + 1) * P)
                    if n_tile >= 2:
                        pe.wait_ge(a_masked, n_tile - 1)
                    nc.tensor.matmul(a_ps[i % 2][:], r(KM)[:, tok], r(QM)[:, tok], start=True, stop=True
                                     ).then_inc(a_done, 1)
                    pe.wait_ge(kd_stored, 2 * h + 1 + (i >= 4))
                    if n_tile >= 2:
                        pe.wait_ge(state_ready, state_count((n_tile - 2) // NP, ((n_tile - 2) % NP + 1) * NB))
                    pe.wait_ge(apart_ready, NB * (n_tile + 1))
                    last = nc.tensor.matmul(u_ps[i % 2][:].rearrange("p j d -> p (j d)"), kdn[:, i, :],
                                            apart[i % 2][:].rearrange("p j d -> p (j d)"),
                                            start=True, stop=True)
                    last.then_inc(u_done, 1)
                    pe.wait_ge(a_masked, n_tile + 1)
                    if n_tile >= 2:
                        pe.wait_ge(o_stored, n_tile - 1)
                    nc.tensor.matmul(o_ps[i % 2][:], atm[i % 2][:], vig[:, 1, i, h * DV:(h + 1) * DV],
                                     start=True, stop=False, skip_group_check=True)
                    for j in range(NB):
                        n = i * NB + j
                        pe.wait_ge(state_ready, state_count(h, n))
                        nc.tensor.matmul(o_ps[i % 2][j * CH:(j + 1) * CH, :],
                                         r(QE)[:, n * CH:(n + 1) * CH], state[n % 4][:], start=False,
                                         stop=True, skip_group_check=True, tile_position=(0, j * CH)
                                         ).then_inc(inter_done, 1)

        @block.sync
        def _(sp):
            for h in range(H):
                sp.wait_ge(state_ready, state_count(h, NCH))
                sp.dma_start(io["state_prompt"][h], state[NCH % 4][:]).then_inc(state_saved, 16)
            sp.wait_ge(state_saved, 16 * H)

    with ExitStack() as st:
        m = Memory(nc, st)
        s0 = qkf[:, 0:4, :].rearrange("p a t -> p (a t)")[:, 0:NS * H * DV].rearrange(
            "p (b h d) -> p b h d", b=NS, h=H)
        kv = m.sb("kv", [P, H, DV])
        v_sb = m.sb("v_sb", [P, H, DV])
        k_s = m.sb("k_s2", [P, H, NS])
        q_z = m.sb("q_z2", [P, H, NS, NS])
        ss = m.sb("hp_ss", [P, NT, H])
        v_ps = m.ps("v_ps", [P, H, DV])
        o_ps = m.ps("hs_o_ps", [NS, H, DV])
        t_ps = [m.ps(f"hp_t{b}", [P, H, P]) for b in range(2)]
        s_landed = top.sem("hs_landed")
        v_spread = top.sem("hs_v_spread")
        v_copied = top.sem("hs_v_copied")
        kv_ready = top.sem("hs_kv_ready")
        new_ready = top.sem("hs_new_ready")
        qz_ready = top.sem("hs_qz_ready")
        o_done = top.sem("hs_o_done")
        s_saved = top.sem("hs_saved")
        silu_done = top.sem("hp_silu_done")
        ms_ready = top.sem("hp_ms_ready")
        rms_ready = top.sem("hp_rms_ready")
        y_ready = top.sem("hp_y_ready")
        turned = top.sem("hp_turned")
        stored = top.sem("hp_stored")
        chain = top.sem("hs_chain")
        squares = vig[:, 1].rearrange("p t (h d) -> p t h d", h=H)
        o_all = vig[:, 0].rearrange("p t (h d) -> p t h d", h=H)
        gate = vig[:, 2].rearrange("p t (h d) -> p t h d", h=H)
        block = st.enter_context(nc.Block())

        @block.sync
        def _(sp):
            sp.dma_start(s0.rearrange("p b h d -> p (b h d)"), io["state"].rearrange("p b h d -> p (b h d)")
                         ).then_inc(s_landed, 16)
            for b in range(NS):
                sp.wait_ge(new_ready, b + 1)
                sp.dma_start(io["state_sample"][:, b], s0[:, b]).then_inc(s_saved, 16)
            sp.wait_ge(s_saved, 16 * NS)

        @block.scalar
        def _(act):
            for b in range(NS):
                act.wait_ge(v_spread, b + 1)
                if b >= 1:
                    act.wait_ge(kv_ready, b)
                nc.scalar.copy(v_sb[:], v_ps[:]).then_inc(v_copied, 1)
            nc.scalar.activation(vig[:, 2], vig[:, 2], ACT.Silu).then_inc(silu_done, 1)
            act.wait_ge(ms_ready, 1)
            nc.scalar.activation(ss[:], ss[:], ACT.Sqrt).then_inc(rms_ready, 1)
            for i in range(NT):
                act.wait_ge(turned, i + 1)
                nc.scalar.activation(obt[:, :, i * P:i * P + rows(i)], t_ps[i % 2][:, :, 0:rows(i)], ACT.Copy,
                                     scale=c["gnorm"][:, 0:1]).then_inc(stored, 1)

        @block.vector
        def _(dve):
            link = Chain(dve, chain)
            v = nc.vector
            q_s, f_s = qkf[:, CHQ:CHQ + H, SEQ:T], qkf[:, CHF:CHF + H, SEQ:T]
            link(v.tensor_scalar(k_s[:], f_s, -1.0, 1.0, ALU.mult, ALU.add))
            link(v.memset(q_z[:], 0.0))
            for b in range(NS):
                last = v.tensor_scalar(q_z[:, :, b, b], q_s[:, :, b], HG_SCALE, None, ALU.mult)
                last.then_inc(qz_ready, 1)
            dve.wait_ge(s_landed, 16)
            for b in range(NS):
                dve.wait_ge(v_copied, b + 1)
                v.tensor_tensor(kv[:], v_sb[:], bcast(k_s[:, :, b], [P, H, DV], 2), ALU.mult).then_inc(kv_ready, 1)
                link(v.tensor_tensor(s0[:, b], s0[:, b], bcast(f_s[:, :, b], [P, H, DV], 2), ALU.mult))
                dve.wait_ge(kv_ready, b + 1)
                v.tensor_tensor(s0[:, b], s0[:, b], kv[:], ALU.add).then_inc(new_ready, 1)
                dve.wait_ge(new_ready, b + 1)
            dve.wait_ge(o_done, 1)
            link(v.memset(vig[:, 0, NP, :], 0.0))
            link(v.tensor_copy(o_all[0:NS, NP], o_ps[:]))
            link(v.tensor_tensor(squares, o_all, o_all, ALU.mult))
            link(v.tensor_reduce(ss[:], squares, AX_X, ALU.add))
            v.tensor_scalar(ss[:], ss[:], 1.0 / DV, EPS, ALU.mult, ALU.add).then_inc(ms_ready, 1)
            dve.wait_ge(rms_ready, 1)
            link(v.reciprocal(ss[:], ss[:]))
            link(v.tensor_tensor(o_all.rearrange("p t h d -> p (t h) d"), o_all.rearrange("p t h d -> p (t h) d"),
                                 bcast(ss[:].rearrange("p t h -> p (t h)"), [P, NT * H, DV], 2), ALU.mult))
            dve.wait_ge(silu_done, 1)
            v.tensor_tensor(vig[:, 0], vig[:, 0], vig[:, 2], ALU.mult).then_inc(y_ready, 1)

        @block.tensor
        def _(pe):
            for b in range(NS):
                if b >= 1:
                    pe.wait_ge(v_copied, b)
                nc.tensor.matmul(v_ps[:].rearrange("p h d -> p (h d)"), c["pick"][:, b, :], vig[0:NS, 1, NP, :],
                                 start=True, stop=True).then_inc(v_spread, 1)
            pe.wait_ge(qz_ready, NS)
            pe.wait_ge(new_ready, NS)
            for h in range(H):
                for b in range(NS):
                    last = nc.tensor.matmul(o_ps[:, h, :], q_z[:, h, b, :], s0[:, b, h, :],
                                            start=(b == 0), stop=(b == NS - 1))
            last.then_inc(o_done, 1)
            pe.wait_ge(y_ready, 1)
            for i in range(NT):
                if i >= 2:
                    pe.wait_ge(stored, i - 1)
                for h in range(H):
                    last = nc.tensor.transpose(t_ps[i % 2][:, h, :], vig[:, 0, i, h * DV:(h + 1) * DV], ident[:])
                last.then_inc(turned, 1)


def merge(nc, top, io, c):
    xnt, branch = c["xnt"], (c["oat"], c["obt"])
    NSL = len(SLICES)
    with ExitStack() as st:
        m = Memory(nc, st)
        wg = [[m.sb(f"wg{u}{x}", [P, KD, P]) for x in range(2)] for u in range(2)]
        wb = [[m.sb(f"wb{u}{x}", [P, H, P]) for x in range(2)] for u in range(2)]
        gate = [[m.sb(f"mg{z}{x}", [P, 512]) for x in range(2)] for z in range(2)]
        mt = [m.sb(f"mt{u}", [P, T]) for u in range(2)]
        g_ps = [[m.ps(f"mg_ps{z}{x}", [P, 512]) for x in range(2)] for z in range(2)]
        b_ps = [[m.ps(f"mb_ps{z}{x}", [P, 512]) for x in range(2)] for z in range(2)]
        w_landed = [top.sem(f"mw_landed{u}") for u in range(2)]
        chunk_done = top.sem("m_chunk_done")
        slice_done = top.sem("m_slice_done")
        gates_done = top.sem("m_gates_done")
        sums_done = top.sem("m_sums_done")
        m_saved = [top.sem(f"m_saved{u}") for u in range(2)]
        chain = top.sem("m_chain")
        block = st.enter_context(nc.Block())

        @block.sync
        def _(sp):
            for k in range(KD):
                u = k % 2
                if k >= 2:
                    sp.wait_ge(slice_done, NSL * (k - 1))
                sp.dma_start(wg[u][0][:], io["w_t"][CGA + k]).then_inc(w_landed[u], 16)
                sp.dma_start(wg[u][1][:], io["w_t"][CGB + k]).then_inc(w_landed[u], 16)
                sp.dma_start(wb[u][0][:], io["wa"][k]).then_inc(w_landed[u], 16)
                sp.dma_start(wb[u][1][:], io["wb"][k]).then_inc(w_landed[u], 16)
                if k >= 1:
                    sp.wait_ge(sums_done, NSL * k)
                    sp.dma_start(io["mt"][k - 1], mt[(k - 1) % 2][:]).then_inc(m_saved[(k - 1) % 2], 16)
            sp.wait_ge(sums_done, NSL * KD)
            sp.dma_start(io["mt"][KD - 1], mt[(KD - 1) % 2][:]).then_inc(m_saved[(KD - 1) % 2], 16)
            for u in range(2):
                sp.wait_ge(m_saved[u], 16 * KD // 2)

        @block.tensor
        def _(pe):
            for k in range(KD):
                u = k % 2
                pe.wait_ge(w_landed[u], 64 * (k // 2 + 1))
                for s, (t0, n) in enumerate(SLICES):
                    q = NSL * k + s
                    if q >= 2:
                        pe.wait_ge(sums_done, q - 1)
                    for x in range(2):
                        for d in range(KD):
                            nc.tensor.matmul(g_ps[q % 2][x][:, 0:n], wg[u][x][:, d, :], xnt[:, d, t0:t0 + n],
                                             start=(d == 0), stop=(d == KD - 1))
                        for d in range(H):
                            last = nc.tensor.matmul(b_ps[q % 2][x][:, 0:n], wb[u][x][:, d, :],
                                                    branch[x][:, d, t0:t0 + n], start=(d == 0), stop=(d == H - 1))
                    last.then_inc(slice_done, 1)

        @block.scalar
        def _(act):
            for q in range(NSL * KD):
                n = SLICES[q % NSL][1]
                act.wait_ge(slice_done, q + 1)
                if q >= 2:
                    act.wait_ge(sums_done, q - 1)
                for x in range(2):
                    nc.scalar.activation(gate[q % 2][x][:, 0:n], g_ps[q % 2][x][:, 0:n], ACT.Sigmoid
                                         ).then_inc(gates_done, 1)

        @block.vector
        def _(dve):
            link = Chain(dve, chain)
            v = nc.vector
            for k in range(KD):
                if k >= 2:
                    dve.wait_ge(m_saved[k % 2], 16 * (k // 2))
                for s, (t0, n) in enumerate(SLICES):
                    q = NSL * k + s
                    dve.wait_ge(gates_done, 2 * q + 2)
                    ga, gb = gate[q % 2][0][:, 0:n], gate[q % 2][1][:, 0:n]
                    link.mark(v.tensor_tensor(ga, ga, b_ps[q % 2][0][:, 0:n], ALU.mult))
                    link(v.tensor_tensor(gb, gb, b_ps[q % 2][1][:, 0:n], ALU.mult))
                    v.tensor_tensor(mt[k % 2][:, t0:t0 + n], ga, gb, ALU.add).then_inc(sums_done, 1)


def experts(nc, top, io, c):
    ident = c["ident"]
    BATCH = 2
    NB = SLOTS // BATCH
    with ExitStack() as st:
        m = Memory(nc, st)
        w_out = m.sb("w_out", [P, KD, D])
        w_q = m.sb("w_q", [P, KD, D])
        keys = m.sb("keys", [P, HP, NK])
        norm2 = m.sb("norm2", [P, D])
        norm_f = m.sb("norm_f", [P, D])
        xt = m.sb("xt", [P, D])
        mts = m.sb("mts", [P, KD, P])
        h_next = m.sb("h_next", [P, D])
        h_cur = m.sb("h_cur", [P, D])
        n2_next = m.sb("n2_next", [P, D])
        n2_cur = m.sb("n2_cur", [P, D])
        n2t = m.sb("n2t", [P, KD, P])
        work = m.sb("work", [P, 2 * HP * NK])
        comb = m.sb("comb", [P, HP, TOPK * TOPK])
        flat = comb[:].rearrange("p h n -> p (h n)")
        qn = flat[:, 0:D]
        qt = flat[:, D:2 * D].rearrange("p (h t) -> p h t", h=HP)
        s16 = m.sb("s16", [P, HP, 2, TOPK])
        i16 = m.sb("i16", [P, HP, 2, TOPK], U32)
        i16f = m.sb("i16f", [P, HP, 2, TOPK])
        cs = m.sb("cs", [P, HP, TOPK])
        ci = m.sb("ci", [P, HP, TOPK], U32)
        cd = m.sb("cd", [P, HP, TOPK], U32)
        cf = m.sb("cf", [P, HP, TOPK])
        ee = [m.sb(f"ee{x}", [P, SLOTS]) for x in range(2)]
        idx_next = m.sb("idx_next", [P, SLOTS], U32)
        idx_cur = m.sb("idx_cur", [P, SLOTS], U32)
        w_next = m.sb("w_next", [P, HP, TOPK])
        w_cur = m.sb("w_cur", [P, SLOTS])
        zz = m.sb("zz", [P, HP])
        sm = m.sb("sm", [P, 4])
        dots = m.sb("dots", [P, RING])
        gel = m.sb("gel", [P, RING])
        diag = m.sb("diag", [P, RING, P])
        ring = m.sb("ring", [P, RING, 2 * D])
        idx_s = m.sb("idx_s", [P, NS], U32)
        w_s = m.sb("w_s", [P, NS])
        coef_s = m.sb("coef_s", [P, NS, NS])
        a_ps = m.ps("xa_ps", [P, D])
        s_ps = m.ps("xs_ps", [P, 2, HP, NK])
        acc = m.ps("x_acc", [P, D])
        t_ps = s_ps[:, 0]

        sem = lambda n: top.sem("x_" + n)
        w_landed, in_landed, x_used = sem("w_landed"), sem("in_landed"), sem("x_used")
        h_done, h_ready, sq_done, ms_ready, rms_ready = (
            sem("h_done"), sem("h_ready"), sem("sq_done"), sem("ms_ready"), sem("rms_ready"))
        n2_ready, n2_turned, n2t_ready, q_done, q_ready, q_turned, qt_ready, s_done = (
            sem("n2_ready"), sem("n2_turned"), sem("n2t_ready"), sem("q_done"), sem("q_ready"),
            sem("q_turned"), sem("qt_ready"), sem("s_done"))
        e_ready, e_done, idx_ready, idx_taken, w_ready = (
            sem("e_ready"), sem("e_done"), sem("idx_ready"), sem("idx_taken"), sem("w_ready"))
        landed = [sem(f"landed{j}") for j in range(RING)]
        dots_ready, gel_ready, diag_ready, slot_used = (
            sem("dots_ready"), sem("gel_ready"), sem("diag_ready"), sem("slot_used"))
        cur_taken, h_taken, sum_ready, fsq_done, fms_ready, frms_ready, y_ready, y_saved = (
            sem("cur_taken"), sem("h_taken"), sem("sum_ready"), sem("fsq_done"), sem("fms_ready"),
            sem("frms_ready"), sem("y_ready"), sem("y_saved"))
        s_turned, s_idx_ready, s_spread, s_coef_ready, s_used = (
            sem("s_turned"), sem("s_idx_ready"), sem("s_spread"), sem("s_coef_ready"), sem("s_used"))
        chain, fin_chain, s_chain = sem("chain"), sem("fin_chain"), sem("s_chain")
        sp_held, pool_held, dve_held = sem("sp_held"), sem("pool_held"), sem("dve_held")
        block = st.enter_context(nc.Block())

        def slots_with_front(i, R, batch, front, only=None):
            following = i + 1
            for b in range(NB):
                batch(b)
                for at, step in front:
                    if at == b:
                        step(following, R)

        AT_H, AT_ADD, AT_ROOT, AT_N2, AT_N2T, AT_Q, AT_QN, AT_QT, AT_S = (1, 3), 5, 7, 9, 11, (13, 15), 16, 18, 20
        AT_KEYS, AT_COMB, AT_BEST, AT_EXP, AT_ROWS, AT_IDX, AT_W = 23, 34, 36, 47, 49, 59, 60

        @block.sync
        def _(sp):
            sp.dma_start(w_out[:], io["w_out"]).then_inc(w_landed, 16)
            sp.dma_start(norm2[:], io["norm2"].to_broadcast([P, D])).then_inc(w_landed, 16)
            sp.dma_start(norm_f[:], io["norm_f"].to_broadcast([P, D])).then_inc(w_landed, 16)
            sp.dma_start(keys[:], io["keys"]).then_inc(w_landed, 16)
            sp.dma_start(w_q[:], io["w_query"]).then_inc(w_landed, 16)

            def load(i, R, first=False):
                if not first:
                    hold(sp, h_ready, i, sp_held)
                tok = bass.ds(i * P, R)
                sp.dma_start(xt[0:R, :], io["x"][tok, :]).then_inc(in_landed, 16)
                sp.dma_start(mts[:, :, 0:R], io["mt"][:, :, tok].rearrange("k p t -> p k t")).then_inc(in_landed, 16)

            def store(i, R):
                hold(sp, y_ready, i + 1, sp_held)
                sp.dma_start(io["y"][bass.ds(i * P, R), :], h_cur[0:R, :]).then_inc(y_saved, 16)

            load(0, P, True)
            with sp.Fori(0, NP - 1) as i:
                load(i + 1, P)
                store(i, P)
            load(NP, NS)
            store(NP - 1, P)
            store(NP, NS)
            sp.wait_ge(y_saved, 16 * NT)

        @block.gpsimd
        def _(pool):
            def gather(r, rows_at, n=P):
                nc.gpsimd.indirect_dma_start(
                    out=ring[:, r, :], out_offset=None, in_=io["experts"],
                    in_offset=bass.IndirectOffsetOnAxis(ap=rows_at, axis=0)).then_inc(landed[r], 16)

            def copy_rows(i, lo, hi, n):
                nc.gpsimd.tensor_copy(idx_cur[:, lo:hi], idx_next[:, lo:hi]).then_inc(idx_taken, 1)
                hold(pool, idx_taken, 2 * i + n, pool_held)

            def take(i):
                hold(pool, idx_ready, i + 1, pool_held)
                copy_rows(i, 0, SLOTS - RING, 1)

            def tile(i, first=False):
                for s in range(SLOTS):
                    if s % BATCH == 0 and not (first and s < RING):
                        hold(pool, slot_used, i * NB + (s - RING) // BATCH + 1, pool_held)
                    if s == SLOTS - RING:
                        copy_rows(i, SLOTS - RING, SLOTS, 2)
                    gather(s % RING, idx_cur[:, s:s + 1])

            take(0)
            tile(0, True)
            with pool.Fori(1, NP) as i:
                take(i)
                tile(i)
            pool.wait_ge(s_idx_ready, 1)
            for b in range(NS):
                if b % BATCH == 0:
                    pool.wait_ge(slot_used, NP * NB + (b - RING) // BATCH + 1)
                gather(b % RING, idx_s[:, b:b + 1])

        @block.tensor
        def _(pe):
            pe.wait_ge(w_landed, 16 * 5)

            def product(lhs, rhs, R, ks):
                for k in ks:
                    for n in range(2):
                        last = nc.tensor.matmul(a_ps[0:R, n * 512:(n + 1) * 512], lhs[:, k, 0:R],
                                                rhs[:, k, n * 512:(n + 1) * 512],
                                                start=(k == 0), stop=(k == KD - 1))
                return last

            def h_part(part):
                def step(i, R):
                    if part == 0:
                        pe.wait_ge(in_landed, 32 * (i + 1))
                    last = product(mts, w_out, R, range(4 * part, 4 * part + 4))
                    if part:
                        last.then_inc(h_done, 1)
                return step

            def turn_n2(i, R):
                pe.wait_ge(n2_ready, i + 1)
                for k in range(KD):
                    last = nc.tensor.transpose(t_ps[:, k, 0:R], n2_next[0:R, k * P:(k + 1) * P], ident[0:R, 0:R])
                last.then_inc(n2_turned, 1)

            def q_part(part):
                def step(i, R):
                    if part == 0:
                        pe.wait_ge(n2t_ready, i + 1)
                    last = product(n2t, w_q, R, range(4 * part, 4 * part + 4))
                    if part:
                        last.then_inc(q_done, 1)
                return step

            def turn_q(i, R):
                pe.wait_ge(q_ready, i + 1)
                for k in range(HP):
                    last = nc.tensor.transpose(t_ps[:, k, 0:R], qn[0:R, k * P:(k + 1) * P], ident[0:R, 0:R])
                last.then_inc(q_turned, 1)

            def scores(i, R):
                pe.wait_ge(qt_ready, i + 1)
                for k in range(HP):
                    for x in range(2):
                        s = slice(x * DH, (x + 1) * DH)
                        last = nc.tensor.matmul(s_ps[0:R, x, k, :], qt[s, k, 0:R], keys[s, k, :],
                                                start=True, stop=True)
                last.then_inc(s_done, 1)

            front = [(AT_H[0], h_part(0)), (AT_H[1], h_part(1)), (AT_N2T, turn_n2), (AT_Q[0], q_part(0)),
                     (AT_Q[1], q_part(1)), (AT_QT, turn_q), (AT_S, scores)]

            def peer(i, R, front):
                def sums(b):
                    pe.wait_ge(diag_ready, (i * NB + b + 1) * BATCH)
                    for s in range(b * BATCH, (b + 1) * BATCH):
                        for n in range(2):
                            last = nc.tensor.matmul(acc[:, n * 512:(n + 1) * 512], diag[:, s % RING, :],
                                                    ring[:, s % RING, D + n * 512:D + (n + 1) * 512],
                                                    start=(s == 0), stop=(s == SLOTS - 1))
                    last.then_inc(slot_used, 1)

                slots_with_front(i, R, lambda b: sums(b - 1) if b else None, front)
                sums(NB - 1)

            for at, step in front:
                step(0, P)
            peer(0, P, front)
            with pe.Fori(1, NP - 1) as i:
                pe.wait_ge(sum_ready, i)
                peer(i, P, front)
            pe.wait_ge(sum_ready, NP - 1)
            peer(NP - 1, NS, front)
            pe.wait_ge(idx_ready, NP + 1)
            pe.wait_ge(w_ready, NP + 1)
            nc.tensor.transpose(s_ps[:, 0, 0, 0:NS], ee[0][0:NS, :], ident[0:NS, 0:NS])
            nc.tensor.transpose(s_ps[:, 0, 1, 0:NS], w_next[0:NS].rearrange("p h s -> p (h s)"),
                                ident[0:NS, 0:NS]).then_inc(s_turned, 1)
            spread = [a_ps[:], s_ps[:, 1].rearrange("p h n -> p (h n)")]
            for b in range(NS):
                if b >= 2:
                    pe.wait_ge(dots_ready, NP * NB + b - 1)
                for n in range(2):
                    last = nc.tensor.matmul(spread[b % 2][:, n * 512:(n + 1) * 512], c["pick"][:, b, :],
                                            n2_next[0:NS, n * 512:(n + 1) * 512], start=True, stop=True)
                last.then_inc(s_spread, 1)
            pe.wait_ge(sum_ready, NP)
            for b in range(NS):
                pe.wait_ge(s_coef_ready, b + 1)
                for n in range(2):
                    last = nc.tensor.matmul(acc[0:NS, n * 512:(n + 1) * 512], coef_s[:, b, :],
                                            ring[:, b, D + n * 512:D + (n + 1) * 512],
                                            start=(b == 0), stop=(b == NS - 1))
            last.then_inc(s_used, 1)

        @block.scalar
        def _(act):
            def squares(i, R):
                act.wait_ge(h_ready, i + 1)
                nc.scalar.activation(n2_next[0:R, :], h_next[0:R, :], ACT.Square, accum_out=sm[0:R, 0:1]
                                     ).then_inc(sq_done, 1)

            def root(i, R):
                act.wait_ge(ms_ready, i + 1)
                nc.scalar.activation(sm[0:R, 1:2], sm[0:R, 1:2], ACT.Sqrt).then_inc(rms_ready, 1)

            def take_n2t(i, R):
                act.wait_ge(n2_turned, i + 1)
                nc.scalar.copy(n2t[:, :, 0:R], t_ps[:, :, 0:R]).then_inc(n2t_ready, 1)

            def take_q(i, R):
                act.wait_ge(q_done, i + 1)
                nc.scalar.copy(qn[0:R, :], a_ps[0:R, :]).then_inc(q_ready, 1)

            def take_qt(i, R):
                act.wait_ge(q_turned, i + 1)
                nc.scalar.copy(qt[:, :, 0:R], t_ps[:, :, 0:R]).then_inc(qt_ready, 1)

            def exps(i, R):
                act.wait_ge(e_ready, i + 1)
                nc.scalar.activation(w_next[0:R], w_next[0:R], ACT.Exp).then_inc(e_done, 1)

            front = [(AT_ADD, squares), (AT_ROOT, root), (AT_N2T, take_n2t), (AT_QN, take_q),
                     (AT_QT, take_qt), (AT_EXP, exps)]

            def finish(i, R):
                act.wait_ge(sum_ready, i + 1)
                nc.scalar.activation(ring_junk[0:R, :], h_cur[0:R, :], ACT.Square, accum_out=sm[0:R, 2:3]
                                     ).then_inc(fsq_done, 1)
                act.wait_ge(fms_ready, i + 1)
                nc.scalar.activation(sm[0:R, 3:4], sm[0:R, 3:4], ACT.Sqrt).then_inc(frms_ready, 1)

            ring_junk = n2_cur

            def gelus(i):
                def batch(b):
                    r = slice(b * BATCH % RING, b * BATCH % RING + BATCH)
                    act.wait_ge(dots_ready, i * NB + b + 1)
                    nc.scalar.activation(gel[:, r], dots[:, r], ACT.Gelu).then_inc(gel_ready, 1)
                return batch

            for at, step in front:
                step(0, P)
            with act.Fori(0, NP - 1) as i:
                slots_with_front(i, P, gelus(i), front)
                finish(i, P)
            slots_with_front(NP - 1, NS, gelus(NP - 1), front)
            finish(NP - 1, P)
            for b in range(NS):
                act.wait_ge(dots_ready, NP * NB + b + 1)
                nc.scalar.activation(gel[:, b:b + 1], dots[:, b:b + 1], ACT.Gelu).then_inc(gel_ready, 1)
            finish(NP, NS)

        @block.vector
        def _(dve):
            v = nc.vector
            steps = []
            links = {}

            def link_of(i):
                if id(i) not in links:
                    base = 0 if not steps else i * steps[0]
                    links[id(i)] = (Chain(dve, chain, base), i)
                return links[id(i)][0]

            def add(i, R):
                dve.wait_ge(h_done, i + 1)
                dve.wait_ge(in_landed, 32 * (i + 1))
                if not (isinstance(i, int) and i == 0):
                    dve.wait_ge(h_taken, i)
                v.tensor_tensor(h_next[0:R, :], a_ps[0:R, :], xt[0:R, :], ALU.add).then_inc(h_ready, 1)

            def means(i, R):
                dve.wait_ge(sq_done, i + 1)
                v.tensor_scalar(sm[0:R, 1:2], sm[0:R, 0:1], 1.0 / D, EPS, ALU.mult, ALU.add).then_inc(ms_ready, 1)

            def norm(i, R):
                link = link_of(i)
                dve.wait_ge(rms_ready, i + 1)
                link(v.reciprocal(sm[0:R, 1:2], sm[0:R, 1:2]))
                v.scalar_tensor_tensor(out=n2_next[0:R, :], in0=h_next[0:R, :], scalar=sm[0:R, 1:2],
                                       in1=norm2[0:R, :], op0=ALU.mult, op1=ALU.mult).then_inc(n2_ready, 1)

            def top16(stage, lists, values, spare, best, where, guard):
                def step(i, R):
                    link = link_of(i)
                    guard(i)
                    if link.n:
                        hold(dve, chain, link.base + link.n, dve_held)
                    lo, hi = slice(0, 8), slice(8, 16)
                    for n in range(lists):
                        if stage == 0:
                            ins = v.max(best(n)[0:R, lo], values(n)[0:R])
                        elif stage == 1:
                            ins = v.max_index(where(n)[0:R, lo], best(n)[0:R, lo], values(n)[0:R])
                        elif stage == 2:
                            ins = v.match_replace(spare(n)[0:R], best(n)[0:R, lo], values(n)[0:R], LOWEST)
                        elif stage == 3:
                            ins = v.max(best(n)[0:R, hi], spare(n)[0:R])
                        else:
                            ins = v.max_index(where(n)[0:R, hi], best(n)[0:R, hi], spare(n)[0:R])
                        link.mark(ins)
                return step

            keys_top = [top16(s, 2 * HP, lambda n: s_ps[:, n % 2, n // 2, :], lambda n: work[:, n * NK:(n + 1) * NK],
                              lambda n: s16[:, n // 2, n % 2, :], lambda n: i16[:, n // 2, n % 2, :],
                              (lambda i: hold(dve, s_done, i + 1, dve_held)) if s == 0 else (lambda i: None))
                        for s in range(5)]
            best_top = [top16(s, HP, lambda n: comb[:, n, :], lambda n: work[:, n * 256:(n + 1) * 256],
                              lambda n: cs[:, n, :], lambda n: ci[:, n, :], lambda i: None) for s in range(5)]

            def combine(i, R):
                link = link_of(i)
                link.wait()
                shape = [R, HP, TOPK, TOPK]
                link.mark(v.tensor_copy(i16f[0:R], i16[0:R]))
                c4 = comb[0:R].rearrange("p h (a b) -> p h a b", a=TOPK)
                link.mark(v.tensor_tensor(c4, bcast(s16[0:R, :, 0, :], shape, 3), bcast(s16[0:R, :, 1, :], shape, 2),
                                          ALU.add))

            def less_top(i, R):
                link = link_of(i)
                link.wait()
                v.tensor_tensor(w_next[0:R], cs[0:R], cs[0:R, :, 0:1].to_broadcast([R, HP, TOPK]), ALU.subtract
                                ).then_inc(e_ready, 1)

            def half_rows(x, part):
                def step(i, R):
                    link = link_of(i)
                    link.wait()
                    onehot = work[0:R, :].rearrange("p (h s k) -> p h s k", h=HP, s=TOPK)
                    onehot3 = work[0:R, :].rearrange("p (n k) -> p n k", k=TOPK)
                    if part == 0:
                        if x == 0:
                            link(v.tensor_scalar(cd[0:R], ci[0:R], 4, None, ALU.logical_shift_right))
                        else:
                            link(v.tensor_scalar(cd[0:R], ci[0:R], TOPK - 1, None, ALU.bitwise_and))
                        link(v.tensor_copy(cf[0:R], cd[0:R]))
                        link.mark(v.tensor_tensor(
                            onehot3, bcast(cf[0:R].rearrange("p h s -> p (h s)"), [R, SLOTS, TOPK], 2),
                            bcast(c["iota"][0:R, :], [R, SLOTS, TOPK], 1), ALU.is_equal))
                    elif part == 1:
                        link.mark(v.tensor_tensor(onehot, onehot, bcast(i16f[0:R, :, x, :], [R, HP, TOPK, TOPK], 2),
                                                  ALU.mult))
                    else:
                        link.mark(v.tensor_reduce(ee[x][0:R, :], onehot3, AX_X, ALU.add))
                return step

            def row_numbers(i, R):
                link = link_of(i)
                link.wait()
                link(v.scalar_tensor_tensor(out=ee[0][0:R, :], in0=ee[0][0:R, :], scalar=float(NK),
                                            in1=ee[1][0:R, :], op0=ALU.mult, op1=ALU.add))
                if not (isinstance(i, int) and i == 0):
                    dve.wait_ge(idx_taken, 2 * i)
                v.tensor_copy(idx_next[0:R, :], ee[0][0:R, :]).then_inc(idx_ready, 1)

            def weights(i, R):
                link = link_of(i)
                dve.wait_ge(e_done, i + 1)
                link(v.tensor_reduce(zz[0:R, :], w_next[0:R], AX_X, ALU.add))
                link(v.reciprocal(zz[0:R, :], zz[0:R, :]))
                v.tensor_tensor(w_next[0:R], w_next[0:R], bcast(zz[0:R, :], [R, HP, TOPK], 2), ALU.mult
                                ).then_inc(w_ready, 1)
                if not steps:
                    steps.append(link.n)
                assert link.n == steps[0]

            front = [(AT_ADD, add), (AT_ROOT, means), (AT_N2, norm)]
            front += [(AT_KEYS + 2 * s, keys_top[s]) for s in range(5)] + [(AT_COMB, combine)]
            front += [(AT_BEST + 2 * s, best_top[s]) for s in range(5)] + [(AT_EXP, less_top)]
            front += [(AT_ROWS + 3 * x + p, half_rows(x, p)) for x in range(2) for p in range(3)]
            front += [(AT_IDX, row_numbers), (AT_W, weights)]

            def take(i):
                dve.wait_ge(w_ready, i + 1)
                if not (isinstance(i, int) and i == 0):
                    dve.wait_ge(fsq_done, i)
                    dve.wait_ge(diag_ready, i * SLOTS)
                v.tensor_copy(n2_cur[:], n2_next[:]).then_inc(cur_taken, 1)
                v.tensor_copy(w_cur[:], w_next[:].rearrange("p h s -> p (h s)")).then_inc(cur_taken, 1)
                if not (isinstance(i, int) and i == 0):
                    dve.wait_ge(y_saved, 16 * i)
                v.tensor_copy(h_cur[:], h_next[:]).then_inc(h_taken, 1)
                hold(dve, cur_taken, 2 * i + 2, dve_held)
                hold(dve, h_taken, i + 1, dve_held)

            def peer(i, R, front):
                def diags(b):
                    dve.wait_ge(gel_ready, i * NB + b + 1)
                    for s in range(b * BATCH, (b + 1) * BATCH):
                        v.tensor_scalar(diag[:, s % RING, :], ident[:], gel[:, s % RING:s % RING + 1],
                                        w_cur[:, s:s + 1], ALU.mult, ALU.mult).then_inc(diag_ready, 1)

                def batch(b):
                    for s in range(b * BATCH, (b + 1) * BATCH):
                        r = s % RING
                        dve.wait_ge(landed[r], 16 * (i * (SLOTS // RING) + s // RING + 1))
                        ins = v.tensor_tensor_reduce(out=ring[:, r, 0:D], in0=ring[:, r, 0:D], in1=n2_cur[:],
                                                     scale=1.0, scalar=0.0, op0=ALU.mult, op1=ALU.add,
                                                     accum_out=dots[:, r:r + 1])
                    ins.then_inc(dots_ready, 1)
                    if b:
                        diags(b - 1)

                slots_with_front(i, R, batch, front)
                diags(NB - 1)

            def finish(i, R, used):
                used()
                v.tensor_tensor(h_cur[0:R, :], acc[0:R, :], h_cur[0:R, :], ALU.add).then_inc(sum_ready, 1)
                dve.wait_ge(fsq_done, i + 1)
                v.tensor_scalar(sm[0:R, 3:4], sm[0:R, 2:3], 1.0 / D, EPS, ALU.mult, ALU.add).then_inc(fms_ready, 1)
                dve.wait_ge(frms_ready, i + 1)
                v.reciprocal(sm[0:R, 3:4], sm[0:R, 3:4]).then_inc(fin_chain, 1)
                dve.wait_ge(fin_chain, i + 1)
                v.scalar_tensor_tensor(out=h_cur[0:R, :], in0=h_cur[0:R, :], scalar=sm[0:R, 3:4],
                                       in1=norm_f[0:R, :], op0=ALU.mult, op1=ALU.mult).then_inc(y_ready, 1)

            dve.wait_ge(w_landed, 16 * 5)
            for at, step in front:
                step(0, P)
            take(0)
            with dve.Fori(0, NP - 1) as i:
                peer(i, P, front)
                finish(i, P, lambda: dve.wait_ge(slot_used, (i + 1) * NB))
                take(i + 1)
            links.clear()
            peer(NP - 1, NS, front)
            finish(NP - 1, P, lambda: dve.wait_ge(slot_used, NP * NB))
            link = Chain(dve, s_chain)
            dve.wait_ge(s_turned, 1)
            link.mark(v.tensor_copy(w_s[:], s_ps[:, 0, 1, 0:NS]))
            link.mark(v.memset(coef_s[:], 0.0))
            v.tensor_copy(idx_s[:], s_ps[:, 0, 0, 0:NS]).then_inc(s_idx_ready, 1)
            link.wait()
            spread = [a_ps[:], s_ps[:, 1].rearrange("p h n -> p (h n)")]
            for b in range(NS):
                dve.wait_ge(s_spread, b + 1)
                dve.wait_ge(landed[b], 16 * (NP * SLOTS // RING + 1))
                v.tensor_tensor_reduce(out=ring[:, b, 0:D], in0=ring[:, b, 0:D], in1=spread[b % 2], scale=1.0,
                                       scalar=0.0, op0=ALU.mult, op1=ALU.add, accum_out=dots[:, b:b + 1]
                                       ).then_inc(dots_ready, 1)
            for b in range(NS):
                dve.wait_ge(gel_ready, NP * NB + b + 1)
                v.tensor_tensor(coef_s[:, b, b:b + 1], gel[:, b:b + 1], w_s[:, b:b + 1], ALU.mult
                                ).then_inc(s_coef_ready, 1)
            dve.wait_ge(y_saved, 16 * NP)
            v.tensor_copy(h_cur[0:NS, :], h_next[0:NS, :]).then_inc(h_taken, 1)
            dve.wait_ge(h_taken, NT)
            finish(NP, NS, lambda: dve.wait_ge(s_used, 1))


def stage(nc, build, io, c):
    sems = Stage(nc)
    build(nc, sems, io, c)
    sems.end()


def program(nc, io):
    with ExitStack() as st:
        top = Memory(nc, st)
        c = {
            "ident": top.sb("ident", [P, P]),
            "cmask": top.sb("cmask", [P, P]),
            "bmask": top.sb("bmask", [P, P]),
            "iota": top.sb("iota", [P, TOPK]),
            "pick": top.sb("pick", [NS, NS, P]),
            "own_token": top.sb("own_token", [64, NS]),
            "own_head": top.sb("own_head", [NS * H, H]),
            "sum_maps": top.sb("sum_maps", [64, NS * H]),
            "map_coef": top.sb("map_coef", [64, 1]),
            "neg_lam": top.sb("neg_lam", [P, 1]),
            "subln": top.sb("subln", [P, 1]),
            "gnorm": top.sb("gnorm", [P, 1]),
            "lb": top.sb("lb", [P, H]),
            "one_lb": top.sb("one_lb", [P, H]),
            "cache_rows": top.sb("cache_rows", [P, NS * PAGES], U32),
            "zero1": top.sb("zero1", [P, 1]),
            "zeros_i": top.sb("zeros_i", [P, 1]),
            "k_new": top.sb("k_new", [NS, 512]),
            "q_new": top.sb("q_new", [NS, 512]),
        }
        io["mt"] = nc.dram_tensor("mt_scratch", [KD, P, T], F32, kind="Internal").ap()
        with ExitStack() as st2:
            mid = Memory(nc, st2)
            c["xnt"] = mid.sb("xnt", [P, KD, T])
            stage(nc, normalise, io, c)
            c["oat"] = mid.sb("oat", [P, H, T])
            with ExitStack() as st3:
                inner = Memory(nc, st3)
                c["qkf"] = inner.sb("qkf", [P, N_QKF, T])
                c["obt"] = c["qkf"][:, CHQ:CHQ + H, :]
                with ExitStack() as st4:
                    c["vig"] = Memory(nc, st4).sb("vig", [P, 3, NT, 512])
                    stage(nc, project, io, c)
                    stage(nc, attend_prompt, io, c)
                    stage(nc, attend_sample, io, c)
                    stage(nc, hgrn, io, c)
                stage(nc, merge, io, c)
        stage(nc, experts, io, c)


def lay_out(inputs):
    import numpy as np

    a = {k: np.asarray(v) for k, v in inputs.items()}
    w_in = a["w_in"][0]
    cols = lambda lo, n: w_in[:, lo:lo + n]
    turned = np.concatenate([cols(0, 1024), cols(1536, 1024), cols(3584, 2048)], axis=1)
    by_rows = np.concatenate([cols(1024, 512), cols(2560, 1024)], axis=1)

    def chunks(w, n):
        k = w.shape[0] // P
        return w.reshape(k, P, w.shape[1] // n, n).transpose(2, 1, 0, 3)

    out = {
        "x": np.concatenate([a["x_prompt"].reshape(SEQ, D), a["x_sample"].reshape(NS, D)]),
        "norm1": a["norm1_w"].reshape(KD, P).T,
        "lam_w": np.concatenate([a["lambda_q1"], a["lambda_q2"], a["lambda_k1"], a["lambda_k2"]]).reshape(1, 4 * DH),
        "lb_w": a["lb_param"].reshape(2, H, P).transpose(2, 0, 1),
        "subln": a["subln_w"].reshape(P, 1),
        "gnorm": a["gnorm_w"].reshape(P, 1),
        "pages": a["page_table"].reshape(1, NS * PAGES),
        "w_t": chunks(turned, P),
        "w_n": chunks(by_rows, 512),
        "cache_k": a["cache_k"].reshape(-1, 512),
        "cache_v": a["cache_v"].reshape(-1, 512),
        "state": a["state_hgrn"][0].transpose(2, 0, 1, 3),
        "wa": chunks(a["w_branch_a"][0], P),
        "wb": chunks(a["w_branch_b"][0], P),
        "w_out": chunks(a["w_out"][0], D)[0],
        "w_query": chunks(a["w_query"][0], D)[0],
        "keys": a["sub_keys"][0].transpose(1, 3, 0, 2).reshape(P, HP, NK),
        "norm2": a["norm2_w"].reshape(1, D),
        "norm_f": a["norm_f_w"].reshape(1, D),
        "experts": np.concatenate([a["expert_u"][0], a["expert_v"][0]], axis=1),
    }
    return {k: np.ascontiguousarray(v) for k, v in out.items()}


OUTS = {
    "y": [T, D], "k_out": [T, 512], "v_out": [T, 512],
    "state_prompt": [H, P, DV], "state_sample": [P, NS, H, DV],
}


def kernel(**inputs):
    import numpy as np
    import concourse.bacc as bacc
    from concourse.bass_utils import run_bass_kernel_spmd

    nc = bacc.Bacc("TRN2", target_bir_lowering=False, num_devices=1)
    laid = lay_out(inputs)
    arrays = {f"in_{n}": a for n, a in laid.items()}
    io = {n: nc.dram_tensor(f"in_{n}", a.shape, mybir.dt.from_np(a.dtype), kind="ExternalInput").ap()
          for n, a in laid.items()}
    for n, shape in OUTS.items():
        io[n] = nc.dram_tensor(n, shape, F32, kind="ExternalOutput").ap()
    program(nc, io)
    r = run_bass_kernel_spmd(nc, [arrays], core_ids=[0]).results[0]
    y, k, v = (np.asarray(r[n]) for n in ("y", "k_out", "v_out"))
    return (y[:SEQ].reshape(1, SEQ, D), y[SEQ:].reshape(NS, 1, D),
            k[:SEQ].reshape(1, 1, SEQ, H, 2, DH), v[:SEQ].reshape(1, 1, SEQ, H, DV),
            np.asarray(r["state_prompt"]).reshape(1, 1, H, P, DV),
            k[SEQ:].reshape(1, NS, 1, H, 2, DH), v[SEQ:].reshape(1, NS, 1, H, DV),
            np.asarray(r["state_sample"]).transpose(1, 2, 0, 3).reshape(1, NS, H, P, DV))
```

```python
import math
from contextlib import ExitStack

import concourse.bass as bass
from concourse import mybir

ALU = mybir.AluOpType
ACT = mybir.ActivationFunctionType
AX_X = mybir.AxisListType.X
F32 = mybir.dt.float32
I32 = mybir.dt.int32
U32 = mybir.dt.uint32

P = 128
D = 1024
SEQ = 1024
NS = 8
T = SEQ + NS
NP = SEQ // P
NT = NP + 1
KD = D // P
H = 4
DH = 64
DV = 128
PAGE = 128
PAGES = 4
EPS = 1e-6
LAM_INIT = 0.8 - 0.6 * math.exp(-0.3 * 0)
QK_SCALE = DH ** -0.5
HG_SCALE = 128 ** -0.5
CH = 32
NCH = SEQ // CH
HP = 8
NK = 128
TOPK = 16
SLOTS = HP * TOPK
RING = 8
NEG = -1e30
LOWEST = -3.0e38
CQ, CK, CHQ, CHF, CGA, CGB = 0, 4, 8, 12, 16, 24
N_COLS = 16
GROUPS = ((0, 4), (4, NT))
N_BESIDE = 3
ARENA = 50400


def rows(i):
    return P if i < NP else NS


class Chain:

    def __init__(self, eng, sem, base=0):
        self.eng, self.sem, self.base, self.n = eng, sem, base, 0

    def mark(self, ins):
        self.n += 1
        ins.then_inc(self.sem, 1)

    def wait(self):
        self.eng.wait_ge(self.sem, self.base + self.n)

    def __call__(self, ins):
        self.mark(ins)
        self.wait()


def hold(eng, sem, value, carrier):
    eng.wait_ge(sem, value)
    eng.sem_inc(carrier, 1)


class Region:

    def __init__(self, arena, at=0):
        self.arena, self.at = arena, at

    def sb(self, name, shape, dt=F32):
        n = math.prod(shape[1:])
        assert self.at + n <= self.arena.shape[1], (name, self.at, n)
        ap = self.arena[0:shape[0], self.at:self.at + n]
        self.at += n
        if dt is not F32:
            ap = ap.bitcast(dt)
        if len(shape) > 2:
            names = " ".join(f"d{i}" for i in range(len(shape) - 1))
            ap = ap.rearrange(f"p ({names}) -> p {names}", **{f"d{i}": x for i, x in enumerate(shape[1:])})
        return ap


class Consts:

    def __init__(self, nc, stack):
        self.nc, self.stack = nc, stack

    def sb(self, name, shape, dt=F32):
        return self.stack.enter_context(self.nc.sbuf_tensor(name, shape, dt))


class Banks:

    def __init__(self, nc, stack):
        self.nc, self.stack = nc, stack

    def ps(self, name, shape):
        return self.stack.enter_context(self.nc.psum_tensor(name, shape, F32))


class Group:

    def __init__(self, name, lo, hi):
        self.name, self.lo, self.hi = name, lo, hi
        self.tiles = range(lo, hi)
        self.prompt = range(lo, min(hi, NP))
        self.t0 = lo * P
        self.n = min(hi * P, T) - self.t0
        self.np = len(self.prompt) * P
        width = -(-self.n // -(-self.n // 512))
        self.slices = [(a, min(width, self.n - a)) for a in range(0, self.n, width)]
        self.sampled = hi == NT


HANDED = 2 * D + 2 * SLOTS


def parts_of(handed):
    return {"h": handed[:, 0:D], "n2": handed[:, D:2 * D], "idx": handed[:, 2 * D:2 * D + SLOTS].bitcast(U32),
            "w": handed[:, 2 * D + SLOTS:HANDED]}


class Stage:

    def __init__(self, nc, prefix=""):
        self.nc, self.prefix, self.sems = nc, prefix, []

    def sem(self, name):
        self.sems.append(self.nc.alloc_semaphore(name=self.prefix + name))
        return self.sems[-1]

    def end(self):
        self.nc.clear_and_free_semaphores(self.sems)
        self.nc.all_engine_barrier()


def bcast(ap, shape, axis):
    return ap.unsqueeze(axis).to_broadcast(shape)


def normalise(nc, top, io, c):
    with ExitStack() as st:
        m, banks = Region(c["arena"]), Banks(nc, st)
        xs = m.sb("xs", [P, NT, D])
        xn = m.sb("xn", [P, NT, D])
        ss = m.sb("ss", [P, NT])
        rstd = m.sb("rstd", [P, NT])
        xnt = m.sb("xnt", [P, KD, T])
        norm1 = m.sb("norm1", [P, KD])
        lam_w = m.sb("lam_w", [P, 2, 2, DH])
        lam_p = m.sb("lam_p", [P, 2, DH])
        lam_s = m.sb("lam_s", [P, 2])
        lb_w = m.sb("lb_w", [P, 2, H])
        lb_m = m.sb("lb_m", [P, H])
        pages = m.sb("pages", [P, NS * PAGES], I32)
        pidx_i = m.sb("pidx_i", [P, 1], I32)
        pidx = m.sb("pidx", [P, 1])
        iota_i = m.sb("iota_i", [P, TOPK], I32)
        halves = m.sb("halves", [64, 2, NS])
        heads = m.sb("heads", [32, H, NS])
        tp = [banks.ps(f"n_tp{b}", [P, KD, P]) for b in range(2)]

        tail_zeroed = top.sem("tail_zeroed")
        x_landed = [top.sem(f"xs_landed{j}") for j in range(NP // 2 + 1)]
        small_landed = top.sem("small_landed")
        squares = top.sem("squares")
        mean_ready = top.sem("mean_ready")
        root_ready = top.sem("root_ready")
        xn_ready = top.sem("xn_ready")
        xn_turned = top.sem("xn_turned")
        xnt_stored = top.sem("xnt_stored")
        xnt_saved = top.sem("xnt_saved")
        lam_sum = top.sem("lam_sum")
        lam_exp = top.sem("lam_exp")
        pool_chain = top.sem("norm_pool_chain")
        dve_chain = top.sem("norm_dve_chain")
        ident_ready = top.sem("ident_ready")
        masks_ready = top.sem("masks_ready")
        block = st.enter_context(nc.Block())

        @block.sync
        def _(sp):
            for j in range(NP // 2):
                sp.dma_start(xs[:, 2 * j:2 * j + 2, :], io["x"][2 * j * P:2 * (j + 1) * P, :].rearrange(
                    "(t p) d -> p t d", p=P)).then_inc(x_landed[j], 16)
            sp.wait_ge(tail_zeroed, 1)
            sp.dma_start(xs[0:NS, NP, :], io["x"][SEQ:T, :]).then_inc(x_landed[NP // 2], 16)
            sp.dma_start(norm1[:], io["norm1"]).then_inc(small_landed, 16)
            sp.dma_start(lam_w[:].rearrange("p a b d -> p (a b d)"),
                         io["lam_w"].to_broadcast([P, 4 * DH])).then_inc(small_landed, 16)
            sp.dma_start(lb_w[:], io["lb_w"]).then_inc(small_landed, 16)
            sp.dma_start(c["subln"][:], io["subln"]).then_inc(small_landed, 16)
            sp.dma_start(c["gnorm"][:], io["gnorm"]).then_inc(small_landed, 16)
            sp.dma_start(pages[:], io["pages"].to_broadcast([P, NS * PAGES])).then_inc(small_landed, 16)
            for i in range(NT):
                tok = slice(i * P, i * P + rows(i))
                sp.wait_ge(xnt_stored, i + 1)
                sp.dma_start(io["xnt"][:, :, tok], xnt[:, :, tok]).then_inc(xnt_saved, 16)
            sp.wait_ge(xnt_saved, 16 * NT)

        @block.gpsimd
        def _(pool):
            link = Chain(pool, pool_chain)
            g = nc.gpsimd
            ident, cmask, bmask = c["ident"], c["cmask"], c["bmask"]
            link(g.memset(ident[:], 0.0))
            g.affine_select(out=ident[:], in_=ident[:], compare_op=ALU.not_equal, fill=1.0, base=0,
                            pattern=[[-1, P]], channel_multiplier=1).then_inc(ident_ready, 1)
            link(g.memset(cmask[:], 0.0))
            link(g.affine_select(out=cmask[:], in_=cmask[:], compare_op=ALU.is_ge, fill=NEG, base=0,
                                 pattern=[[-1, P]], channel_multiplier=1))
            link(g.memset(bmask[:], 1.0))
            link(g.affine_select(out=bmask[:], in_=bmask[:], compare_op=ALU.is_ge, fill=0.0, base=0,
                                 pattern=[[1, P]], channel_multiplier=-1))
            b3 = bmask[:].rearrange("p (a b) -> p a b", b=CH)
            link(g.affine_select(out=b3, in_=b3, compare_op=ALU.is_ge, fill=0.0, base=0,
                                 pattern=[[-CH, P // CH], [0, CH]], channel_multiplier=1))
            link(g.iota(iota_i[:], pattern=[[1, TOPK]], base=0, channel_multiplier=0))
            link(g.tensor_copy(c["iota"][:], iota_i[:]))
            link(g.iota(pidx_i[:], pattern=[[0, 1]], base=0, channel_multiplier=1))
            link(g.tensor_copy(pidx[:], pidx_i[:]))
            link(g.memset(c["pick"][:], 0.0))
            link(g.affine_select(out=c["pick"][:], in_=c["pick"][:], compare_op=ALU.not_equal, fill=1.0,
                                 base=0, pattern=[[-1, NS], [0, P]], channel_multiplier=1))
            link(g.memset(halves[:], 1.0))
            link(g.affine_select(out=halves[:], in_=halves[:], compare_op=ALU.is_ge, fill=0.0, base=0,
                                 pattern=[[-32, 2], [-H, NS]], channel_multiplier=1))
            link(g.affine_select(out=halves[:], in_=halves[:], compare_op=ALU.is_ge, fill=0.0, base=H - 1,
                                 pattern=[[32, 2], [H, NS]], channel_multiplier=-1))
            link(g.tensor_tensor(c["own_token"][:], halves[:, 0, :], halves[:, 1, :], ALU.add))
            link(g.memset(heads[:], 0.0))
            link(g.affine_select(out=heads[:], in_=heads[:], compare_op=ALU.not_equal, fill=1.0, base=0,
                                 pattern=[[-1, H], [-H, NS]], channel_multiplier=1))
            g.memset(c["zeros_i"][:], 0.0).then_inc(masks_ready, 1)

        @block.scalar
        def _(act):
            for i in range(NT):
                act.wait_ge(x_landed[i // 2], 16)
                nc.scalar.activation(xn[:, i, :], xs[:, i, :], ACT.Square,
                                     accum_out=ss[:, i:i + 1]).then_inc(squares, 1)
            act.wait_ge(mean_ready, 1)
            nc.scalar.activation(rstd[:], ss[:], ACT.Sqrt).then_inc(root_ready, 1)
            act.wait_ge(lam_sum, 1)
            nc.scalar.activation(lam_s[:], lam_s[:], ACT.Exp).then_inc(lam_exp, 1)
            act.wait_ge(lam_sum, 2)
            nc.scalar.activation(lb_w[:], lb_w[:], ACT.Exp).then_inc(lam_exp, 1)

        @block.vector
        def _(dve):
            link = Chain(dve, dve_chain)
            v = nc.vector
            v.memset(xs[:, NP, :], 0.0).then_inc(tail_zeroed, 1)
            dve.wait_ge(small_landed, 6 * 16)
            link(v.tensor_tensor(lam_p[:], lam_w[:, 0], lam_w[:, 1], ALU.mult))
            v.tensor_reduce(lam_s[:], lam_p[:], AX_X, ALU.add).then_inc(lam_sum, 1)
            link(v.tensor_tensor(lb_m[:], lb_w[:, 0, :], lb_w[:, 1, :], ALU.max))
            v.tensor_tensor(lb_w[:], lb_w[:], bcast(lb_m[:], [P, 2, H], 1), ALU.subtract).then_inc(lam_sum, 1)
            link(v.tensor_scalar(c["subln"][:], c["subln"][:], 1.0 - LAM_INIT, None, ALU.mult))
            dve.wait_ge(squares, NT)
            link(v.tensor_scalar(ss[:], ss[:], 1.0 / D, EPS, ALU.mult, ALU.add))
            v.memset(c["zero1"][:], 0.0).then_inc(mean_ready, 1)
            dve.wait_ge(root_ready, 1)
            link(v.reciprocal(rstd[:], rstd[:]))
            def scale(i):
                v.tensor_scalar(xn[:, i, :], xs[:, i, :], rstd[:, i:i + 1], None, ALU.mult).then_inc(xn_ready, 1)

            scale(0)
            scale(1)
            for i in range(NT):
                if i + 2 < NT:
                    scale(i + 2)
                dve.wait_ge(xn_turned, i + 1)
                v.tensor_tensor(xnt[:, :, i * P:i * P + rows(i)], tp[i % 2][:, :, 0:rows(i)],
                                bcast(norm1[:], [P, KD, rows(i)], 2), ALU.mult).then_inc(xnt_stored, 1)
            dve.wait_ge(lam_exp, 1)
            link(v.tensor_tensor(c["neg_lam"][:], lam_s[:, 1:2], lam_s[:, 0:1], ALU.subtract))
            link(v.tensor_scalar(c["neg_lam"][:], c["neg_lam"][:], -LAM_INIT, None, ALU.add))
            link(v.memset(c["map_coef"][:], 1.0))
            link(v.tensor_copy(c["map_coef"][32:64, :], c["neg_lam"][32:64, :]))
            dve.wait_ge(lam_exp, 2)
            link(v.tensor_tensor(lb_m[:], lb_w[:, 0, :], lb_w[:, 1, :], ALU.add))
            link(v.reciprocal(lb_m[:], lb_m[:]))
            link(v.tensor_tensor(c["lb"][:], lb_w[:, 0, :], lb_m[:], ALU.mult))
            link(v.tensor_scalar(c["one_lb"][:], c["lb"][:], -1.0, 1.0, ALU.mult, ALU.add))
            dve.wait_ge(masks_ready, 1)
            link(v.tensor_scalar(c["cache_rows"][:], pages[:], float(PAGE), pidx[:, 0:1], ALU.mult, ALU.add))
            link(v.tensor_reduce(c["own_head"][:], heads[:], AX_X, ALU.add))
            link(v.tensor_tensor(c["sum_maps"][:], c["ident"][0:64, 0:32], c["ident"][0:64, 32:64], ALU.add))

        @block.tensor
        def _(pe):
            pe.wait_ge(ident_ready, 1)
            for i in range(NT):
                pe.wait_ge(xn_ready, i + 1)
                if i >= 2:
                    pe.wait_ge(xnt_stored, i - 1)
                for k in range(KD):
                    last = nc.tensor.transpose(tp[i % 2][:, k, :], xn[:, i, k * P:(k + 1) * P], c["ident"][:])
                last.then_inc(xn_turned, 1)


def project(nc, top, io, c, g, side):
    qk, v_all, ident = c["qk"], c["v"], c["ident"]
    with ExitStack() as st:
        m, banks = Region(c["arena"], c["free"]), Banks(nc, st)
        xnt = m.sb("xnt_g", [P, KD, g.n])
        wt = [m.sb(f"wt{u}", [P, KD, P]) for u in range(2)]
        wn = [m.sb(f"wn{u}", [P, KD, 512]) for u in range(1 if g.lo else 2)]
        row_st = [m.sb(f"row_st{u}", [P, 512]) for u in range(2)]
        col_st = m.sb("col_st", [P, g.n])
        pt = [[banks.ps(f"pt{g.name}{u}_{s}", [P, 512]) for s in range(len(g.slices))] for u in range(2)]
        pn = [banks.ps(f"pn{g.name}{u}", [P, 512]) for u in range(2)]

        xnt_landed = top.sem("xnt_landed")
        wt_landed = [top.sem(f"wt_landed{u}") for u in range(2)]
        cols_done = top.sem("cols_done")
        cols_stored = top.sem("cols_stored")
        cols_saved = top.sem("cols_saved")
        wn_landed = [top.sem(f"wn_landed{u}") for u in range(len(wn))]
        rows_done = top.sem("rows_done")
        rows_stored = top.sem("rows_stored")
        rows_saved = [top.sem(f"rows_saved{u}") for u in range(2)]
        v_saved = top.sem("v_saved")
        block = st.enter_context(nc.Block())
        NG = len(g.tiles)
        items = [(b, t) for b in ("v", "i", "g") for t in g.tiles] + [("k", t) for t in g.tiles]
        if g.sampled:
            items.append(("q", NP))
        staged = [n for n, (b, t) in enumerate(items) if b in "ig" or (b == "k" and t < NP)]
        n_direct = N_COLS // 2
        NSL = len(g.slices)

        def staging(n):
            q = staged.index(n)
            return q % 2, q // 2

        def load_w(sp, k):
            if k >= 2:
                sp.wait_ge(cols_done, k - 1)
            sp.dma_start(wt[k % 2], io["w_t"][k]).then_inc(wt_landed[k % 2], 16)

        @block.sync
        def _(sp):
            sp.dma_start(xnt, io["xnt"][:, :, g.t0:g.t0 + g.n]).then_inc(xnt_landed, 16)
            load_w(sp, 0)
            load_w(sp, 1)
            for u in range(len(wn)):
                sp.dma_start(wn[u], io["w_n"][u]).then_inc(wn_landed[u], 16)
            for k in range(2, N_COLS):
                load_w(sp, k)
                if k > n_direct + 1:
                    sp.wait_ge(cols_stored, NSL * (k - 1))
                    sp.dma_start(io["hqf"][k - 2 - n_direct][:, g.t0:g.t0 + g.n], col_st).then_inc(cols_saved, 16)
            for k in range(N_COLS - 2, N_COLS):
                sp.wait_ge(cols_stored, NSL * (k + 1))
                sp.dma_start(io["hqf"][k - n_direct][:, g.t0:g.t0 + g.n], col_st).then_inc(cols_saved, 16)
            for n, (b, t) in enumerate(items):
                block_w = n // NG + len(wn) - 1
                if n % NG == 0 and n and block_w < 3:
                    sp.wait_ge(rows_done, n)
                    sp.dma_start(wn[block_w % len(wn)], io["w_n"][block_w]).then_inc(wn_landed[block_w % len(wn)], 16)
                if b == "q":
                    continue
                sp.wait_ge(rows_stored, n + 1)
                tok = slice(t * P, t * P + rows(t))
                if b == "v":
                    sp.dma_start(io["v_out"][tok, :], v_all[0:rows(t), t, :]).then_inc(v_saved, 16)
                elif b == "k" and t == NP:
                    sp.dma_start(io["k_out"][tok, :], c["k_new"][:]).then_inc(v_saved, 16)
                else:
                    u, _ = staging(n)
                    dst = io["k_out"][tok, :] if b == "k" else io["ig"][tok, :] if b == "i" else io["gg"][tok, :]
                    sp.dma_start(dst, row_st[u][0:rows(t), :]).then_inc(rows_saved[u], 16)
            sp.wait_ge(cols_saved, 16 * n_direct)
            sp.wait_ge(v_saved, 16 * (NG + g.sampled))
            for u in range(2):
                sp.wait_ge(rows_saved[u], 16 * len(staged[u::2]))

        total = N_COLS + len(items)

        @block.scalar
        def _(act):
            for k in range(N_COLS):
                act.wait_ge(cols_done, k + 1)
                if k > n_direct:
                    act.wait_ge(cols_saved, 16 * (k - n_direct))
                for s, (a, n) in enumerate(g.slices):
                    dst = qk[:, k, g.t0 + a:g.t0 + a + n] if k < n_direct else col_st[:, a:a + n]
                    last = nc.scalar.copy(dst, pt[k % 2][s][:, 0:n])
                    last.then_inc(cols_stored, 1)
                side.act(k + 1, total)
            for n, (b, t) in enumerate(items):
                act.wait_ge(rows_done, n + 1)
                if b == "v":
                    dst = v_all[0:rows(t), t, :]
                elif b == "k" and t == NP:
                    dst = c["k_new"][:]
                elif b == "q":
                    dst = c["q_new"][:]
                else:
                    u, before = staging(n)
                    dst = row_st[u][0:rows(t), :]
                    if before:
                        act.wait_ge(rows_saved[u], 16 * before)
                nc.scalar.copy(dst, pn[n % 2][0:rows(t), :]).then_inc(rows_stored, 1)
                side.act(N_COLS + n + 1, total)

        @block.vector
        def _(dve):
            side.dve(1, 1)

        @block.gpsimd
        def _(pool):
            side.pool(1, 1)

        @block.tensor
        def _(pe):
            pe.wait_ge(xnt_landed, 16)
            for k in range(N_COLS):
                u = k % 2
                if k >= 2:
                    pe.wait_ge(cols_stored, NSL * (k - 1))
                pe.wait_ge(wt_landed[u], 16 * (k // 2 + 1))
                for d in range(KD):
                    for s, (a, n) in enumerate(g.slices):
                        last = nc.tensor.matmul(pt[u][s][:, 0:n], wt[u][:, d, :], xnt[:, d, a:a + n],
                                                start=(d == 0), stop=(d == KD - 1))
                last.then_inc(cols_done, 1)
            for n, (b, t) in enumerate(items):
                if n >= 2:
                    pe.wait_ge(rows_stored, n - 1)
                out = pn[n % 2]
                if b in "vig":
                    u = n // NG % len(wn)
                    pe.wait_ge(wn_landed[u], 16 * (n // NG // len(wn) + 1))
                    a = t * P - g.t0
                    for d in range(KD):
                        last = nc.tensor.matmul(out[0:rows(t), :], xnt[:, d, a:a + rows(t)], wn[u][:, d, :],
                                                start=(d == 0), stop=(d == KD - 1))
                else:
                    pe.wait_ge(cols_stored, NSL * N_COLS)
                    c0 = CK if b == "k" else CQ
                    for h in range(H):
                        last = nc.tensor.transpose(out[0:rows(t), h * P:(h + 1) * P],
                                                   qk[:, c0 + h, t * P:t * P + rows(t)], ident[:])
                last.then_inc(rows_done, 1)


def attend_prompt(nc, top, io, c, g, side):
    qk, v_all, ident = c["qk"], c["v"], c["ident"]
    units = [(i, h) for i in g.prompt for h in range(H)]
    NG = len(g.prompt)
    with ExitStack() as st:
        m, banks = Region(c["arena"], c["free"]), Banks(nc, st)
        prob = [[m.sb(f"prob{b}{k}", [P, SEQ]) for k in range(2)] for b in range(2)]
        probt = m.sb("probt", [P, SEQ])
        stat = {n: m.sb(f"at_{n}", [P, 2 * len(units)]) for n in ("top", "neg", "sum", "inv")}
        o_sb = m.sb("o_sb", [P, H, DV])
        o_sq = m.sb("o_sq", [P, H, DV])
        o_ss = m.sb("o_ss", [P, NG, H])
        oat = [m.sb(f"oat{b}", [P, H, P]) for b in range(2)]
        NSC = 2 if len(g.prompt) + g.lo <= NP // 2 else 1
        sc = [[banks.ps(g.name + f"sc{b}{k}", [P, SEQ // NSC]) for k in range(2)] for b in range(NSC)]
        pt = banks.ps(g.name + "at_pt", [P, SEQ])
        o_ps = banks.ps(g.name + "o_ps", [P, H, DV])
        ot_ps = banks.ps(g.name + "ot_ps", [P, H, P])

        scores_done = top.sem("at_scores_done")
        neg_ready = top.sem("at_neg_ready")
        exp_done = top.sem("at_exp_done")
        diff_ready = top.sem("at_diff_ready")
        turned = top.sem("at_turned")
        probt_ready = top.sem("at_probt_ready")
        pv_done = top.sem("at_pv_done")
        o_taken = top.sem("at_o_taken")
        ms_ready = top.sem("at_ms_ready")
        rms_ready = top.sem("at_rms_ready")
        on_ready = top.sem("at_on_ready")
        on_turned = top.sem("at_on_turned")
        oat_stored = top.sem("at_oat_stored")
        oat_saved = [top.sem(f"at_oat_saved{b}") for b in range(2)]
        chain = top.sem("at_chain")
        block = st.enter_context(nc.Block())

        @block.tensor
        def _(pe):
            def scores(u):
                i, h = units[u]
                w = (i + 1) * P
                for k in range(2):
                    if u >= NSC:
                        pe.wait_ge(exp_done, 2 * (u - NSC) + k + 1)
                    for k0 in range(0, w, 512):
                        n = min(512, w - k0)
                        last = nc.tensor.matmul(sc[u % NSC][k][:, k0:k0 + n],
                                                qk[k * DH:(k + 1) * DH, CQ + h, i * P:(i + 1) * P],
                                                qk[k * DH:(k + 1) * DH, CK + h, k0:k0 + n],
                                                start=True, stop=True)
                    last.then_inc(scores_done, 1)

            def turn(u):
                i, h = units[u]
                pe.wait_ge(diff_ready, u + 1)
                if u >= 1:
                    pe.wait_ge(probt_ready, u)
                for b in range(i + 1):
                    last = nc.tensor.transpose(pt[:, b * P:(b + 1) * P], prob[u % 2][0][:, b * P:(b + 1) * P],
                                               ident[:])
                last.then_inc(turned, 1)

            def pv(u):
                i, h = units[u]
                pe.wait_ge(probt_ready, u + 1)
                if u % H == 0 and u:
                    pe.wait_ge(o_taken, u // H)
                for b in range(i + 1):
                    last = nc.tensor.matmul(o_ps[:, h, :], probt[:, b * P:(b + 1) * P],
                                            v_all[:, b, h * DV:(h + 1) * DV], start=(b == 0), stop=(b == i))
                last.then_inc(pv_done, 1)

            def turn_out(i):
                pe.wait_ge(on_ready, i + 1)
                if i >= 1:
                    pe.wait_ge(oat_stored, i)
                for h in range(H):
                    last = nc.tensor.transpose(ot_ps[:, h, :], o_sb[:, h, :], ident[:])
                last.then_inc(on_turned, 1)

            scores(0)
            scores(1)
            for u in range(len(units)):
                turn(u)
                if u + 2 < len(units):
                    scores(u + 2)
                pv(u)
                if u % H == 0 and u:
                    turn_out(u // H - 1)
            turn_out(NG - 1)

        @block.scalar
        def _(act):
            def exps(u):
                w = (units[u][0] + 1) * P
                for k in range(2):
                    q = 2 * u + k
                    act.wait_ge(neg_ready, u + 1)
                    if u >= 2:
                        act.wait_ge(turned, u - 1)
                    nc.scalar.activation(prob[u % 2][k][:, 0:w], sc[u % NSC][k][:, 0:w], ACT.Exp, scale=QK_SCALE,
                                         bias=stat["neg"][:, q:q + 1],
                                         accum_out=stat["sum"][:, q:q + 1]).then_inc(exp_done, 1)

            def store(u):
                w = (units[u][0] + 1) * P
                act.wait_ge(turned, u + 1)
                if u >= 1:
                    act.wait_ge(pv_done, u)
                nc.scalar.copy(probt[:, 0:w], pt[:, 0:w]).then_inc(probt_ready, 1)

            def post(i):
                act.wait_ge(ms_ready, i + 1)
                nc.scalar.activation(o_ss[:, i, :], o_ss[:, i, :], ACT.Sqrt).then_inc(rms_ready, 1)
                act.wait_ge(on_turned, i + 1)
                if i >= 2:
                    act.wait_ge(oat_saved[i % 2], 16 * (i // 2))
                nc.scalar.activation(oat[i % 2], ot_ps[:], ACT.Copy,
                                     scale=c["subln"][:, 0:1]).then_inc(oat_stored, 1)

            exps(0)
            for u in range(len(units)):
                if u + 1 < len(units):
                    exps(u + 1)
                store(u)
                side.act(u + 1, len(units))
                if u % H == 0 and u:
                    post(u // H - 1)
            post(NG - 1)

        @block.vector
        def _(dve):
            link = Chain(dve, chain)
            v = nc.vector

            def tops(u):
                i, h = units[u]
                w = (i + 1) * P
                for k in range(2):
                    dve.wait_ge(scores_done, 2 * u + k + 1)
                    own = sc[u % NSC][k][:, i * P:w]
                    link.mark(v.tensor_tensor(own, own, c["cmask"][:], ALU.add))
                link.wait()
                for k in range(2):
                    link.mark(v.reduce_max(stat["top"][:, 2 * u + k:2 * u + k + 1], sc[u % NSC][k][:, 0:w], AX_X))
                link.wait()
                q = slice(2 * u, 2 * u + 2)
                v.tensor_scalar(stat["neg"][:, q], stat["top"][:, q], -QK_SCALE, None, ALU.mult).then_inc(neg_ready, 1)

            def differ(u):
                w = (units[u][0] + 1) * P
                a, b = prob[u % 2][0][:, 0:w], prob[u % 2][1][:, 0:w]
                q = 2 * u
                dve.wait_ge(exp_done, q + 2)
                link(v.reciprocal(stat["inv"][:, q:q + 2], stat["sum"][:, q:q + 2]))
                link(v.scalar_tensor_tensor(out=stat["inv"][:, q + 1:q + 2], in0=stat["inv"][:, q + 1:q + 2],
                                            scalar=c["neg_lam"][:, 0:1], in1=stat["sum"][:, q:q + 1],
                                            op0=ALU.mult, op1=ALU.mult))
                v.scalar_tensor_tensor(out=a, in0=b, scalar=stat["inv"][:, q + 1:q + 2], in1=a,
                                       op0=ALU.mult, op1=ALU.add).then_inc(diff_ready, 1)

            def post(i):
                dve.wait_ge(pv_done, H * (i + 1))
                if i >= 1:
                    dve.wait_ge(on_turned, i)
                inv0 = stat["inv"][:, 2 * H * i:2 * H * (i + 1)].rearrange("p (h k) -> p h k", k=2)[:, :, 0]
                v.tensor_tensor(o_sb[:], o_ps[:], bcast(inv0, [P, H, DV], 2), ALU.mult).then_inc(o_taken, 1)
                dve.wait_ge(o_taken, i + 1)
                link(v.tensor_tensor(o_sq[:], o_sb[:], o_sb[:], ALU.mult))
                link(v.tensor_reduce(o_ss[:, i, :], o_sq[:], AX_X, ALU.add))
                v.tensor_scalar(o_ss[:, i, :], o_ss[:, i, :], 1.0 / DV, EPS, ALU.mult, ALU.add
                                ).then_inc(ms_ready, 1)
                dve.wait_ge(rms_ready, i + 1)
                link(v.reciprocal(o_ss[:, i, :], o_ss[:, i, :]))
                v.tensor_tensor(o_sb[:], o_sb[:], bcast(o_ss[:, i, :], [P, H, DV], 2), ALU.mult
                                ).then_inc(on_ready, 1)

            tops(0)
            for u in range(len(units)):
                if u + 1 < len(units):
                    tops(u + 1)
                differ(u)
                side.dve(u + 1, len(units))
                if u % H == 0 and u:
                    post(u // H - 1)
            post(NG - 1)

        @block.gpsimd
        def _(pool):
            side.pool(1, 1)

        @block.sync
        def _(sp):
            for i, t in enumerate(g.prompt):
                sp.wait_ge(oat_stored, i + 1)
                sp.dma_start(io["oat"][:, :, t * P:(t + 1) * P], oat[i % 2]).then_inc(oat_saved[i % 2], 16)
            for b in range(2):
                sp.wait_ge(oat_saved[b], 16 * len(range(b, NG, 2)))


def attend_sample(nc, top, io, c, g, side):
    v_all, ident = c["v"], c["ident"]
    G = PAGES + 1
    NR = 2 * NS * H
    with ExitStack() as st:
        m, banks = Region(c["arena"], c["free"]), Banks(nc, st)
        NRING = 2
        ring = m.sb("cached", [P, NRING, PAGES, 512])
        oat = m.sb("oat_s", [P, H, NS])
        q_b = m.sb("q_b", [P, 512])
        own = m.sb("own", [P, 512])
        sco = m.sb("sco", [P, G, 2, NS, H])
        pr = m.sb("pr", [NR, G * PAGE])
        mx = m.sb("as_mx", [NR, 4])
        pown = m.sb("pown", [NR, NS])
        own_w = m.sb("own_w", [NS, NS * H])
        wz = m.sb("wz", [P, NS, PAGES, NS * H])
        osel = m.sb("osel", [NS * H, H, DV])
        o_sb = m.sb("as_o", [NS, H, DV])
        o_sq = m.sb("as_sq", [NS, H, DV])
        o_ss = m.sb("as_ss", [NS, H])
        qb_ps = banks.ps("qb_ps", [P, 512])
        kb_ps = banks.ps("kb_ps", [P, 512])
        s_ps = banks.ps("s_ps", [NR, 2, 512])
        w_ps = banks.ps("w_ps", [P, PAGES, NS * H])
        ow_ps = banks.ps("ow_ps", [NS, NS * H])
        o_ps = banks.ps("as_o_ps", [NS * H, H, DV])
        f_ps = banks.ps("as_f_ps", [P, 512])

        row_landed = [top.sem(f"as_landed{r}") for r in range(NRING)]
        ring_free = top.sem("as_ring_free")
        q_spread = top.sem("as_q_spread")
        q_copied = top.sem("as_q_copied")
        q_used = top.sem("as_q_used")
        s_ready = top.sem("as_s_ready")
        s_turned = top.sem("as_s_turned")
        neg_ready = top.sem("as_neg_ready")
        exp_done = top.sem("as_exp_done")
        pr_ready = top.sem("as_pr_ready")
        w_done = top.sem("as_w_done")
        wz_ready = top.sem("as_wz_ready")
        v_used = top.sem("as_v_used")
        osel_ready = top.sem("as_osel_ready")
        o_done = top.sem("as_o_done")
        ms_ready = top.sem("as_ms_ready")
        rms_ready = top.sem("as_rms_ready")
        on_ready = top.sem("as_on_ready")
        on_turned = top.sem("as_on_turned")
        oat_stored = top.sem("as_oat_stored")
        oat_saved = top.sem("as_oat_saved")
        chain = top.sem("as_chain")
        pr_scores = s_ps[:].rearrange("p a b -> p (a b)")
        block = st.enter_context(nc.Block())

        @block.sync
        def _(sp):
            sp.wait_ge(oat_stored, 1)
            sp.dma_start(io["oat"][:, :, SEQ:T], oat).then_inc(oat_saved, 16)
            sp.wait_ge(oat_saved, 16)

        @block.gpsimd
        def _(pool):
            for n in range(2 * NS):
                cache, b, r = io["cache_k"] if n < NS else io["cache_v"], n % NS, n % NRING
                if NRING <= n:
                    if n - NRING < NS:
                        pool.wait_ge(ring_free, n - NRING + 1)
                    else:
                        pool.wait_ge(v_used, n - NRING + 1 - NS)
                for g in range(PAGES):
                    nc.gpsimd.indirect_dma_start(
                        out=ring[:, r, g, :], out_offset=None, in_=cache,
                        in_offset=bass.IndirectOffsetOnAxis(
                            ap=c["cache_rows"][:, b * PAGES + g:b * PAGES + g + 1], axis=0),
                    ).then_inc(row_landed[r], 16)
                side.pool(n, 2 * NS)
            side.pool(1, 1)

        @block.tensor
        def _(pe):
            for b in range(NS):
                if b >= 1:
                    pe.wait_ge(q_used, b)
                nc.tensor.matmul(qb_ps[:], c["pick"][:, b, :], c["q_new"][:], start=True, stop=True)
                nc.tensor.matmul(kb_ps[:], c["pick"][:, b, :], c["k_new"][:], start=True, stop=True
                                 ).then_inc(q_spread, 1)
            pe.wait_ge(s_ready, 1)
            for g in range(G):
                last = nc.tensor.transpose(pr_scores[:, g * P:(g + 1) * P],
                                           sco[:, g].rearrange("p c b h -> p (c b h)"), ident[:])
            last.then_inc(s_turned, 1)
            pe.wait_ge(pr_ready, 1)
            for g in range(PAGES):
                nc.tensor.matmul(w_ps[:, g, :], pr[:, g * P:(g + 1) * P], c["sum_maps"][:],
                                 start=True, stop=True)
            nc.tensor.matmul(ow_ps[:], pown[:], c["sum_maps"][:], start=True, stop=True).then_inc(w_done, 1)
            pe.wait_ge(wz_ready, 1)
            nc.tensor.matmul(o_ps[:].rearrange("p h d -> p (h d)"), own_w[:], v_all[0:NS, NP, :],
                             start=True, stop=False)
            for b in range(NS):
                pe.wait_ge(row_landed[b % NRING], 16 * PAGES * ((NS + b) // NRING + 1))
                for g in range(PAGES):
                    last = nc.tensor.matmul(o_ps[:].rearrange("p h d -> p (h d)"), wz[:, b, g, :],
                                            ring[:, b % NRING, g, :], start=False,
                                            stop=(b == NS - 1 and g == PAGES - 1))
                last.then_inc(v_used, 1)
            pe.wait_ge(osel_ready, 1)
            nc.tensor.matmul(f_ps[0:NS, :], c["own_token"][0:NS * H, :],
                             osel[:].rearrange("p h d -> p (h d)"), start=True, stop=True).then_inc(o_done, 1)
            pe.wait_ge(on_ready, 1)
            for h in range(H):
                last = nc.tensor.transpose(qb_ps[:, h * NS:(h + 1) * NS], o_sb[:, h, :], ident[0:NS, 0:NS])
            last.then_inc(on_turned, 1)

        @block.scalar
        def _(act):
            for b in range(NS):
                act.wait_ge(q_spread, b + 1)
                if b >= 1:
                    act.wait_ge(q_used, b)
                nc.scalar.copy(q_b[:], qb_ps[:]).then_inc(q_copied, 1)
                side.act(b + 1, 2 * NS)
            act.wait_ge(neg_ready, 1)
            nc.scalar.activation(pr[:, 0:PAGES * PAGE + 1], pr_scores[:, 0:PAGES * PAGE + 1], ACT.Exp,
                                 scale=QK_SCALE, bias=mx[:, 1:2], accum_out=mx[:, 2:3]).then_inc(exp_done, 1)
            side.act(1, 1)
            act.wait_ge(ms_ready, 1)
            nc.scalar.activation(o_ss[:], o_ss[:], ACT.Sqrt).then_inc(rms_ready, 1)
            act.wait_ge(on_turned, 1)
            nc.scalar.activation(oat, qb_ps[:, 0:H * NS].rearrange("p (h b) -> p h b", h=H),
                                 ACT.Copy, scale=c["subln"][:, 0:1]).then_inc(oat_stored, 1)

        @block.vector
        def _(dve):
            link = Chain(dve, chain)
            v = nc.vector
            link(v.memset(wz[:], 0.0))
            for b in range(NS):
                r = b % NRING
                k_rows = ring[:, r]
                dve.wait_ge(q_copied, b + 1)
                dve.wait_ge(row_landed[r], 16 * PAGES * (b // NRING + 1))
                link(v.tensor_tensor(k_rows, k_rows, bcast(q_b[:], [P, PAGES, 512], 1), ALU.mult))
                for k in range(2):
                    last = v.tensor_reduce(
                        sco[:, 0:PAGES, k, b, :],
                        k_rows.rearrange("p g (h c d) -> p g h c d", h=H, c=2)[:, :, :, k, :], AX_X, ALU.add)
                    last.then_inc(ring_free, 1) if k else link(last)
                link(v.tensor_tensor(own[:], kb_ps[:], q_b[:], ALU.mult))
                last = v.tensor_reduce(sco[:, PAGES, :, b, :].rearrange("p c h -> p h c"),
                                       own[:].rearrange("p (h c d) -> p h c d", h=H, c=2), AX_X, ALU.add)
                last.then_inc(q_used, 1)
                dve.wait_ge(q_used, b + 1)
                side.dve(b + 1, 2 * NS)
            dve.wait_ge(ring_free, NS)
            v.memset(mx[:], 0.0).then_inc(s_ready, 1)
            dve.wait_ge(s_ready, 1)
            dve.wait_ge(s_turned, 1)
            link(v.reduce_max(mx[:, 0:1], pr_scores[:, 0:PAGES * PAGE + 1], AX_X))
            v.tensor_scalar(mx[:, 1:2], mx[:, 0:1], -QK_SCALE, None, ALU.mult).then_inc(neg_ready, 1)
            dve.wait_ge(exp_done, 1)
            link(v.reciprocal(mx[:, 3:4], mx[:, 2:3]))
            link(v.tensor_tensor(mx[:, 3:4], mx[:, 3:4], c["map_coef"][:], ALU.mult))
            link(v.tensor_scalar(pr[:, 0:PAGES * PAGE + 1], pr[:, 0:PAGES * PAGE + 1], mx[:, 3:4], None, ALU.mult))
            v.tensor_scalar(pown[:], c["own_token"][:], pr[:, PAGES * PAGE:PAGES * PAGE + 1], None,
                            ALU.mult).then_inc(pr_ready, 1)
            dve.wait_ge(w_done, 1)
            link(v.tensor_copy(own_w[:], ow_ps[:]))
            for b in range(NS):
                last = v.tensor_copy(wz[:, b, :, b * H:(b + 1) * H], w_ps[:, :, b * H:(b + 1) * H])
                last.then_inc(wz_ready, 1) if b == NS - 1 else link(last)
            side.dve(1, 1)
            dve.wait_ge(v_used, NS)
            v.tensor_tensor(osel[:], o_ps[:], bcast(c["own_head"][:], [NS * H, H, DV], 2), ALU.mult
                            ).then_inc(osel_ready, 1)
            dve.wait_ge(o_done, 1)
            link(v.tensor_copy(o_sb[:], f_ps[0:NS, :].rearrange("p (h d) -> p h d", h=H)))
            link(v.tensor_tensor(o_sq[:], o_sb[:], o_sb[:], ALU.mult))
            link(v.tensor_reduce(o_ss[:], o_sq[:], AX_X, ALU.add))
            v.tensor_scalar(o_ss[:], o_ss[:], 1.0 / DV, EPS, ALU.mult, ALU.add).then_inc(ms_ready, 1)
            dve.wait_ge(rms_ready, 1)
            link(v.reciprocal(o_ss[:], o_ss[:]))
            v.tensor_tensor(o_sb[:], o_sb[:], bcast(o_ss[:], [NS, H, DV], 2), ALU.mult).then_inc(on_ready, 1)


def hgrn(nc, top, io, c, g, side):
    ident = c["ident"]
    MID = CH // 2 - 1
    NB = P // CH
    N = g.np
    NG = len(g.prompt)
    NC = N // CH
    with ExitStack() as st:
        m, banks = Region(c["arena"], c["free"]), Banks(nc, st)
        o_all = m.sb("o_all", [P, len(g.tiles), H, DV])
        q_h = m.sb("q_h", [P, g.n])
        f_h = m.sb("f_h", [P, g.n])
        i_h = [m.sb(f"i_h{b}", [P, NG, DV]) for b in range(2)]
        km, kk, gc, qm, ge, qe = (m.sb("hg_" + n, [P, N]) for n in ("km", "kk", "gc", "qm", "ge", "qe"))
        kdn = m.sb("kdn", [P, NG, P])
        restart = m.sb("restart", [P, N])
        apart = [m.sb(f"apart{b}", [P, NB, DV]) for b in range(2)]
        atm = [m.sb(f"atm{b}", [P, P]) for b in range(2)]
        state = [m.sb(f"state{b}", [P, DV]) for b in range(4)]
        tp = [banks.ps(g.name + f"hg_tp{b}", [P, 4, P]) for b in range(2)]
        a_ps = [banks.ps(g.name + f"hg_a{b}", [P, P]) for b in range(2)]
        o_ps = [banks.ps(g.name + f"hg_o{b}", [P, DV]) for b in range(2)]
        u_ps = [banks.ps(g.name + f"hg_u{b}", [P, NB, DV]) for b in range(2)]

        in_landed = top.sem("hg_in_landed")
        i_landed = [top.sem(f"hg_i_landed{b}") for b in range(2)]
        gates = top.sem("hg_gates")
        f_ready = top.sem("hg_f_ready")
        f_used = top.sem("hg_f_used")
        log_ready = top.sem("hg_log_ready")
        rel_ready = top.sem("hg_rel_ready")
        exps_done = top.sem("hg_exps_done")
        ops_ready = top.sem("hg_ops_ready")
        kd_turned = top.sem("hg_kd_turned")
        kd_stored = top.sem("hg_kd_stored")
        a_done = top.sem("hg_a_done")
        a_masked = top.sem("hg_a_masked")
        apart_zeroed = top.sem("hg_apart_zeroed")
        apart_ready = top.sem("hg_apart_ready")
        u_done = top.sem("hg_u_done")
        inter_done = top.sem("hg_inter_done")
        state_landed = top.sem("hg_state_landed")
        state_ready = top.sem("hg_state_ready")
        o_stored = top.sem("hg_o_stored")
        state_saved = top.sem("hg_state_saved")
        chain = top.sem("hg_chain")
        block = st.enter_context(nc.Block())
        parts = [(a, min(4, NG - a)) for a in range(0, NG, 4)]
        steps = H * (NG + 3)

        def step(h, n):
            return h * (NG + 3) + n + 1


        def state_count(h, n):
            return h * (NC + 1) + n + 1

        @block.sync
        def _(sp):
            for h in range(H):
                if h:
                    sp.wait_ge(ops_ready, 4 * h)
                    sp.wait_ge(f_used, h)
                sp.dma_start(q_h, io["hqf"][h][:, g.t0:g.t0 + g.n]).then_inc(in_landed, 16)
                sp.dma_start(f_h, io["hqf"][H + h][:, g.t0:g.t0 + g.n]).then_inc(in_landed, 16)
                if h >= 2:
                    sp.wait_ge(o_stored, NG * (h - 1))
                sp.dma_start(i_h[h % 2], io["ig"][g.t0:g.t0 + N, h * DV:(h + 1) * DV].rearrange(
                    "(t p) d -> p t d", p=P)).then_inc(i_landed[h % 2], 16)
                if h:
                    sp.wait_ge(state_ready, state_count(h - 1, NC))
                    sp.dma_start(io["state_prompt"][h - 1] if g.sampled else io["state_mid"][h - 1],
                                 state[NC % 4]).then_inc(state_saved, 16)
                    sp.wait_ge(state_saved, 16 * h)
                if g.lo:
                    if h:
                        sp.wait_ge(inter_done, NB * NG * h)
                    sp.dma_start(state[0], io["state_mid"][h]).then_inc(state_landed, 16)
            sp.wait_ge(state_ready, state_count(H - 1, NC))
            sp.dma_start(io["state_prompt"][H - 1] if g.sampled else io["state_mid"][H - 1],
                         state[NC % 4]).then_inc(state_saved, 16)
            sp.wait_ge(state_saved, 16 * H)

        @block.gpsimd
        def _(pool):
            side.pool(1, 1)

        @block.scalar
        def _(act):
            def spread_rows(n_tile):
                h, i = divmod(n_tile, NG)
                act.wait_ge(i_landed[h % 2], 16 * (h // 2 + 1))
                if n_tile >= 2:
                    act.wait_ge(u_done, n_tile - 1)
                for j in range(NB):
                    s = slice(j * CH, (j + 1) * CH)
                    nc.scalar.copy(apart[n_tile % 2][s, j, :], i_h[h % 2][s, i, :]).then_inc(apart_ready, 1)

            act.wait_ge(apart_zeroed, 2)
            for h in range(H):
                act.wait_ge(in_landed, 32 * (h + 1))
                nc.scalar.activation(q_h, q_h, ACT.Silu).then_inc(gates, 1)
                nc.scalar.activation(f_h, f_h, ACT.Sigmoid).then_inc(gates, 1)
                side.act(step(h, 0), steps)
                act.wait_ge(f_ready, h + 1)
                if h:
                    act.wait_ge(inter_done, NB * NG * h)
                nc.scalar.activation(km, f_h[:, 0:N], ACT.Ln).then_inc(log_ready, 1)
                side.act(step(h, 1), steps)
                act.wait_ge(rel_ready, h + 1)
                nc.scalar.activation(qm, km, ACT.Exp).then_inc(exps_done, 1)
                act.wait_ge(exps_done, 4 * h + 1)
                nc.scalar.activation(km, km, ACT.Exp, scale=-1.0).then_inc(exps_done, 1)
                nc.scalar.activation(gc, gc, ACT.Exp).then_inc(exps_done, 1)
                nc.scalar.activation(ge, ge, ACT.Exp).then_inc(exps_done, 1)
                side.act(step(h, 2), steps)
                spread_rows(h * NG)
                for b, (a, n) in enumerate(parts):
                    act.wait_ge(kd_turned, len(parts) * h + b + 1)
                    nc.scalar.copy(kdn[:, a:a + n, :], tp[b][:, 0:n, :]).then_inc(kd_stored, 1)
                for i in range(NG):
                    n_tile = h * NG + i
                    if i + 1 < NG:
                        spread_rows(n_tile + 1)
                    side.act(step(h, 3 + i), steps)
                    act.wait_ge(inter_done, NB * (n_tile + 1))
                    nc.scalar.copy(o_all[:, i, h, :], o_ps[n_tile % 2][:]).then_inc(o_stored, 1)

        @block.vector
        def _(dve):
            link = Chain(dve, chain)
            v = nc.vector
            link(v.memset(restart, 1.0))
            link(v.memset(restart.rearrange("p (a b) -> p a b", b=CH)[:, :, 0:1], 0.0))
            for b in range(2):
                v.memset(apart[b], 0.0).then_inc(apart_zeroed, 1)
                link(v.memset(atm[b], 0.0))
            for h in range(H):
                lb, one_lb = c["lb"][:, h:h + 1], c["one_lb"][:, h:h + 1]
                side.dve(step(h, 0), steps)
                dve.wait_ge(gates, 2 * h + 2)
                v.tensor_scalar(f_h, f_h, one_lb, lb, ALU.mult, ALU.add).then_inc(f_ready, 1)
                dve.wait_ge(f_ready, h + 1)
                if g.sampled:
                    link(v.tensor_copy(c["f_new"][:, h, :], f_h[:, N:g.n]))
                    link(v.tensor_copy(c["qh_new"][:, h, :], q_h[:, N:g.n]))
                link(v.tensor_scalar(kk, f_h[:, 0:N], -1.0, 1.0, ALU.mult, ALU.add))
                side.dve(step(h, 1), steps)
                dve.wait_ge(log_ready, h + 1)
                link(v.tensor_tensor_scan(gc, restart, km, 0.0, ALU.mult, ALU.add))
                g3 = gc.rearrange("p (a b) -> p a b", b=CH)
                shape = [P, NC, CH]
                link(v.tensor_tensor(km.rearrange("p (a b) -> p a b", b=CH), g3,
                                     g3[:, :, MID:MID + 1].to_broadcast(shape), ALU.subtract))
                v.tensor_tensor(ge.rearrange("p (a b) -> p a b", b=CH),
                                g3[:, :, CH - 1:CH].to_broadcast(shape), g3, ALU.subtract).then_inc(rel_ready, 1)
                v.memset(c["zero1"][:], 0.0).then_inc(f_used, 1)
                dve.wait_ge(f_used, h + 1)
                side.dve(step(h, 2), steps)
                dve.wait_ge(exps_done, 4 * h + 4)
                sc = q_h[:, 0:N]
                v.scalar_tensor_tensor(out=qm, in0=sc, scalar=HG_SCALE, in1=qm, op0=ALU.mult,
                                       op1=ALU.mult).then_inc(ops_ready, 1)
                v.tensor_tensor(km, kk, km, ALU.mult).then_inc(ops_ready, 1)
                v.scalar_tensor_tensor(out=qe, in0=sc, scalar=HG_SCALE, in1=gc, op0=ALU.mult,
                                       op1=ALU.mult).then_inc(ops_ready, 1)
                v.tensor_tensor(ge, kk, ge, ALU.mult).then_inc(ops_ready, 1)
                if g.lo:
                    dve.wait_ge(state_landed, 16 * (h + 1))
                    v.memset(c["zero1"][:], 0.0).then_inc(state_ready, 1)
                else:
                    if h >= 1:
                        dve.wait_ge(state_saved, 16 * h)
                    v.memset(state[0], 0.0).then_inc(state_ready, 1)
                for i in range(NG):
                    n_tile = h * NG + i
                    dve.wait_ge(a_done, n_tile + 1)
                    if n_tile >= 2:
                        dve.wait_ge(inter_done, NB * (n_tile - 1))
                    v.copy_predicated(atm[n_tile % 2], c["bmask"][:].bitcast(U32), a_ps[n_tile % 2][:]
                                      ).then_inc(a_masked, 1)
                    dve.wait_ge(u_done, n_tile + 1)
                    for j in range(NB):
                        n = i * NB + j
                        dve.wait_ge(state_ready, state_count(h, n))
                        if h * NC + n >= 3:
                            dve.wait_ge(inter_done, h * NC + n - 2)
                        v.scalar_tensor_tensor(out=state[(n + 1) % 4], in0=state[n % 4],
                                               scalar=gc[:, n * CH + CH - 1:n * CH + CH],
                                               in1=u_ps[n_tile % 2][:, j, :], op0=ALU.mult, op1=ALU.add
                                               ).then_inc(state_ready, 1)
                    side.dve(step(h, 3 + i), steps)
                dve.wait_ge(state_ready, state_count(h, NC))

        @block.tensor
        def _(pe):
            for h in range(H):
                pe.wait_ge(ops_ready, 4 * h + 4)
                for b, (a, n) in enumerate(parts):
                    if h >= 1:
                        pe.wait_ge(kd_stored, len(parts) * h)
                    for t in range(n):
                        last = nc.tensor.transpose(tp[b][:, t, :], ge[:, (a + t) * P:(a + t + 1) * P], ident[:])
                    last.then_inc(kd_turned, 1)
                pe.wait_ge(i_landed[h % 2], 16 * (h // 2 + 1))
                for i in range(NG):
                    n_tile = h * NG + i
                    u = n_tile % 2
                    tok = slice(i * P, (i + 1) * P)
                    if n_tile >= 2:
                        pe.wait_ge(a_masked, n_tile - 1)
                    nc.tensor.matmul(a_ps[u][:], km[:, tok], qm[:, tok], start=True, stop=True
                                     ).then_inc(a_done, 1)
                    pe.wait_ge(kd_stored, len(parts) * h + i // 4 + 1)
                    if n_tile >= 2:
                        pe.wait_ge(state_ready, state_count((n_tile - 2) // NG, ((n_tile - 2) % NG + 1) * NB))
                    pe.wait_ge(apart_ready, NB * (n_tile + 1))
                    nc.tensor.matmul(u_ps[u][:].rearrange("p j d -> p (j d)"), kdn[:, i, :],
                                     apart[u].rearrange("p j d -> p (j d)"), start=True, stop=True
                                     ).then_inc(u_done, 1)
                    pe.wait_ge(a_masked, n_tile + 1)
                    if n_tile >= 2:
                        pe.wait_ge(o_stored, n_tile - 1)
                    nc.tensor.matmul(o_ps[u][:], atm[u], i_h[h % 2][:, i, :], start=True, stop=False,
                                     skip_group_check=True)
                    for j in range(NB):
                        n = i * NB + j
                        pe.wait_ge(state_ready, state_count(h, n))
                        nc.tensor.matmul(o_ps[u][j * CH:(j + 1) * CH, :], qe[:, n * CH:(n + 1) * CH], state[n % 4],
                                         start=False, stop=True, skip_group_check=True,
                                         tile_position=(0, j * CH)).then_inc(inter_done, 1)


def hgrn_out(nc, top, io, c, g, side):
    ident = c["ident"]
    NG = len(g.tiles)
    with ExitStack() as st:
        m, banks = Region(c["arena"], c["free"]), Banks(nc, st)
        o_all = m.sb("o_all", [P, NG, H, DV])
        gate = m.sb("gate", [P, NG, H, DV])
        ob = [m.sb(f"ob{b}", [P, H, P]) for b in range(2)]
        ss = m.sb("hp_ss", [P, NG, H])
        space = max(NG, 8 * g.sampled)
        squares = Region(c["arena"], m.at).sb("hp_squares", [P, NG, H, DV])
        s0 = m.sb("s0", [P, space, H, DV])
        if g.sampled:
            kv = m.sb("kv", [P, H, DV])
            v_sb = m.sb("v_sb", [P, H, DV])
            i_s = m.sb("i_s", [NS, H * DV])
            k_s = m.sb("k_s", [P, H, NS])
            q_z = m.sb("q_z", [P, H, NS, NS])
        v_ps = banks.ps(g.name + "v_ps", [P, H, DV])
        o_ps = banks.ps(g.name + "hs_o_ps", [NS, H, DV])
        t_ps = [banks.ps(g.name + f"hp_t{b}", [P, H, P]) for b in range(2)]
        tail_clear = top.sem("hs_tail_clear")
        gate_landed = top.sem("hs_gate_landed")
        s_landed = top.sem("hs_landed")
        v_spread = top.sem("hs_v_spread")
        v_copied = top.sem("hs_v_copied")
        kv_ready = top.sem("hs_kv_ready")
        new_ready = top.sem("hs_new_ready")
        qz_ready = top.sem("hs_qz_ready")
        o_done = top.sem("hs_o_done")
        s_saved = top.sem("hs_saved")
        silu_done = top.sem("hp_silu_done")
        ms_ready = top.sem("hp_ms_ready")
        rms_ready = top.sem("hp_rms_ready")
        y_ready = top.sem("hp_y_ready")
        turned = top.sem("hp_turned")
        stored = top.sem("hp_stored")
        ob_saved = [top.sem(f"hp_ob_saved{b}") for b in range(2)]
        chain = top.sem("hs_chain")
        flat = lambda ap: ap.rearrange("p t h d -> p (t h d)")
        block = st.enter_context(nc.Block())

        @block.sync
        def _(sp):
            if g.sampled:
                sp.dma_start(s0.rearrange("p b h d -> p (b h d)"), io["state"].rearrange("p b h d -> p (b h d)")
                             ).then_inc(s_landed, 16)
                sp.dma_start(i_s, io["ig"][SEQ:T, :]).then_inc(s_landed, 16)
                sp.wait_ge(tail_clear, 1)
                sp.dma_start(gate[0:NS, NG - 1].rearrange("p h d -> p (h d)"), io["gg"][SEQ:T, :]
                             ).then_inc(gate_landed, 16)
            sp.dma_start(gate[:, 0:len(g.prompt)].rearrange("p t h d -> p t (h d)"),
                         io["gg"][g.t0:g.t0 + g.np, :].rearrange("(t p) n -> p t n", p=P)).then_inc(gate_landed, 16)
            if g.sampled:
                for b in range(NS):
                    sp.wait_ge(new_ready, b + 1)
                    sp.dma_start(io["state_sample"][:, b], s0[:, b]).then_inc(s_saved, 16)
            for i, t in enumerate(g.tiles):
                sp.wait_ge(stored, i + 1)
                sp.dma_start(io["obt"][:, :, t * P:t * P + rows(t)], ob[i % 2][:, :, 0:rows(t)]
                             ).then_inc(ob_saved[i % 2], 16)
            if g.sampled:
                sp.wait_ge(s_saved, 16 * NS)
            for b in range(2):
                sp.wait_ge(ob_saved[b], 16 * len(range(b, NG, 2)))

        @block.gpsimd
        def _(pool):
            side.pool(1, 1)

        @block.scalar
        def _(act):
            if g.sampled:
                for b in range(NS):
                    act.wait_ge(v_spread, b + 1)
                    if b >= 1:
                        act.wait_ge(kv_ready, b)
                    nc.scalar.copy(v_sb[:], v_ps[:]).then_inc(v_copied, 1)
            act.wait_ge(gate_landed, 16 * (1 + g.sampled))
            nc.scalar.activation(flat(gate), flat(gate), ACT.Silu).then_inc(silu_done, 1)
            side.act(1, 2)
            act.wait_ge(ms_ready, 1)
            nc.scalar.activation(ss[:], ss[:], ACT.Sqrt).then_inc(rms_ready, 1)
            side.act(1, 1)
            for i, t in enumerate(g.tiles):
                act.wait_ge(turned, i + 1)
                if i >= 2:
                    act.wait_ge(ob_saved[i % 2], 16 * (i // 2))
                nc.scalar.activation(ob[i % 2][:, :, 0:rows(t)], t_ps[i % 2][:, :, 0:rows(t)], ACT.Copy,
                                     scale=c["gnorm"][:, 0:1]).then_inc(stored, 1)

        @block.vector
        def _(dve):
            link = Chain(dve, chain)
            v = nc.vector
            if g.sampled:
                q_s, f_s = c["qh_new"], c["f_new"]
                v.memset(gate[:, NG - 1], 0.0).then_inc(tail_clear, 1)
                link(v.tensor_scalar(k_s[:], f_s[:], -1.0, 1.0, ALU.mult, ALU.add))
                link(v.memset(q_z[:], 0.0))
                for b in range(NS):
                    v.tensor_scalar(q_z[:, :, b, b], q_s[:, :, b], HG_SCALE, None, ALU.mult).then_inc(qz_ready, 1)
                dve.wait_ge(s_landed, 32)
                for b in range(NS):
                    dve.wait_ge(v_copied, b + 1)
                    v.tensor_tensor(kv[:], v_sb[:], bcast(k_s[:, :, b], [P, H, DV], 2), ALU.mult).then_inc(kv_ready, 1)
                    link(v.tensor_tensor(s0[:, b], s0[:, b], bcast(f_s[:, :, b], [P, H, DV], 2), ALU.mult))
                    dve.wait_ge(kv_ready, b + 1)
                    v.tensor_tensor(s0[:, b], s0[:, b], kv[:], ALU.add).then_inc(new_ready, 1)
                    dve.wait_ge(new_ready, b + 1)
                link(v.memset(o_all[:, NG - 1], 0.0))
            side.dve(1, 2)
            if g.sampled:
                dve.wait_ge(o_done, 1)
                link(v.tensor_copy(o_all[0:NS, NG - 1], o_ps[:]))
                dve.wait_ge(s_saved, 16 * NS)
            link(v.tensor_tensor(flat(squares), flat(o_all), flat(o_all), ALU.mult))
            link(v.tensor_reduce(ss[:], squares, AX_X, ALU.add))
            v.tensor_scalar(ss[:], ss[:], 1.0 / DV, EPS, ALU.mult, ALU.add).then_inc(ms_ready, 1)
            dve.wait_ge(rms_ready, 1)
            link(v.reciprocal(ss[:], ss[:]))
            merged = o_all.rearrange("p t h d -> p (t h) d")
            link(v.tensor_tensor(merged, merged, bcast(ss[:].rearrange("p t h -> p (t h)"), [P, NG * H, DV], 2),
                                 ALU.mult))
            dve.wait_ge(silu_done, 1)
            v.tensor_tensor(flat(o_all), flat(o_all), flat(gate), ALU.mult).then_inc(y_ready, 1)
            side.dve(1, 1)

        @block.tensor
        def _(pe):
            if g.sampled:
                pe.wait_ge(s_landed, 32)
                for b in range(NS):
                    if b >= 1:
                        pe.wait_ge(v_copied, b)
                    nc.tensor.matmul(v_ps[:].rearrange("p h d -> p (h d)"), c["pick"][:, b, :], i_s,
                                     start=True, stop=True).then_inc(v_spread, 1)
                pe.wait_ge(qz_ready, NS)
                pe.wait_ge(new_ready, NS)
                for h in range(H):
                    for b in range(NS):
                        last = nc.tensor.matmul(o_ps[:, h, :], q_z[:, h, b, :], s0[:, b, h, :],
                                                start=(b == 0), stop=(b == NS - 1))
                last.then_inc(o_done, 1)
            pe.wait_ge(y_ready, 1)
            for i in range(NG):
                if i >= 2:
                    pe.wait_ge(stored, i - 1)
                for h in range(H):
                    last = nc.tensor.transpose(t_ps[i % 2][:, h, :], o_all[:, i, h, :], ident[:])
                last.then_inc(turned, 1)


def merge(nc, top, io, c, g, side):
    NSL = len(g.slices)
    with ExitStack() as st:
        m, banks = Region(c["arena"], c["free"]), Banks(nc, st)
        w_out = None if g.lo else m.sb("w_out", [P, KD, D])
        low = Region(c["arena"]) if g.lo else m
        empty = Region(c["arena"], 2 * H * T + g.hi * H * DV) if g.lo and not g.sampled else m
        xnt = low.sb("m_xnt", [P, KD, g.n])
        assert g.sampled or not g.lo or low.at <= H * T and 2 * g.n <= (NT - g.hi) * H * DV
        branch = [(low if g.sampled else m).sb(f"m_branch{x}", [P, H, g.n]) for x in range(2)]
        wg = [[m.sb(f"wg{u}{x}", [P, KD, P]) for x in range(2)] for u in range(2)]
        wb = [[m.sb(f"wb{u}{x}", [P, H, P]) for x in range(2)] for u in range(2)]
        gate = [[m.sb(f"mg{z}{x}", [P, 512]) for x in range(2)] for z in range(2)]
        mt = [empty.sb(f"mt{u}", [P, g.n]) for u in range(2)]
        g_ps = [[banks.ps(g.name + f"mg_ps{z}{x}", [P, 512]) for x in range(2)] for z in range(2)]
        b_ps = [[banks.ps(g.name + f"mb_ps{z}{x}", [P, 512]) for x in range(2)] for z in range(2)]
        in_landed = top.sem("m_in_landed")
        w_landed = [top.sem(f"mw_landed{u}") for u in range(2)]
        chunk_done = top.sem("m_chunk_done")
        slice_done = top.sem("m_slice_done")
        gates_done = top.sem("m_gates_done")
        sums_done = top.sem("m_sums_done")
        m_saved = [top.sem(f"m_saved{u}") for u in range(2)]
        w_out_landed = top.sem("m_w_out_landed")
        chain = top.sem("m_chain")
        block = st.enter_context(nc.Block())

        @block.sync
        def _(sp):
            tok = slice(g.t0, g.t0 + g.n)
            sp.dma_start(xnt, io["xnt"][:, :, tok]).then_inc(in_landed, 16)
            sp.dma_start(branch[0], io["oat"][:, :, tok]).then_inc(in_landed, 16)
            sp.dma_start(branch[1], io["obt"][:, :, tok]).then_inc(in_landed, 16)
            for k in range(KD):
                u = k % 2
                if k >= 2:
                    sp.wait_ge(slice_done, NSL * (k - 1))
                sp.dma_start(wg[u][0][:], io["w_t"][CGA + k]).then_inc(w_landed[u], 16)
                sp.dma_start(wg[u][1][:], io["w_t"][CGB + k]).then_inc(w_landed[u], 16)
                sp.dma_start(wb[u][0][:], io["wa"][k]).then_inc(w_landed[u], 16)
                sp.dma_start(wb[u][1][:], io["wb"][k]).then_inc(w_landed[u], 16)
                if k >= 1:
                    sp.wait_ge(sums_done, NSL * k)
                    sp.dma_start(io["mt"][k - 1][:, tok], mt[(k - 1) % 2][:]).then_inc(m_saved[(k - 1) % 2], 16)
                if k == 1 and not g.lo:
                    sp.dma_start(w_out, io["w_out"]).then_inc(w_out_landed, 16)
            sp.wait_ge(sums_done, NSL * KD)
            sp.dma_start(io["mt"][KD - 1][:, tok], mt[(KD - 1) % 2][:]).then_inc(m_saved[(KD - 1) % 2], 16)
            if not g.lo:
                sp.wait_ge(w_out_landed, 16)
            side.store(sp)
            for u in range(2):
                sp.wait_ge(m_saved[u], 16 * KD // 2)

        @block.tensor
        def _(pe):
            pe.wait_ge(in_landed, 48)
            for k in range(KD):
                u = k % 2
                pe.wait_ge(w_landed[u], 64 * (k // 2 + 1))
                for s, (t0, n) in enumerate(g.slices):
                    q = NSL * k + s
                    if q >= 2:
                        pe.wait_ge(sums_done, q - 1)
                    for x in range(2):
                        for d in range(KD):
                            nc.tensor.matmul(g_ps[q % 2][x][:, 0:n], wg[u][x][:, d, :], xnt[:, d, t0:t0 + n],
                                             start=(d == 0), stop=(d == KD - 1))
                        for d in range(H):
                            last = nc.tensor.matmul(b_ps[q % 2][x][:, 0:n], wb[u][x][:, d, :],
                                                    branch[x][:, d, t0:t0 + n], start=(d == 0), stop=(d == H - 1))
                    last.then_inc(slice_done, 1)

        @block.scalar
        def _(act):
            for q in range(NSL * KD):
                n = g.slices[q % NSL][1]
                act.wait_ge(slice_done, q + 1)
                if q >= 2:
                    act.wait_ge(sums_done, q - 1)
                for x in range(2):
                    nc.scalar.activation(gate[q % 2][x][:, 0:n], g_ps[q % 2][x][:, 0:n], ACT.Sigmoid
                                         ).then_inc(gates_done, 1)
                side.act(q + 1, NSL * KD)

        @block.vector
        def _(dve):
            link = Chain(dve, chain)
            v = nc.vector
            for k in range(KD):
                if k >= 2:
                    dve.wait_ge(m_saved[k % 2], 16 * (k // 2))
                for s, (t0, n) in enumerate(g.slices):
                    q = NSL * k + s
                    dve.wait_ge(gates_done, 2 * q + 2)
                    ga, gb = gate[q % 2][0][:, 0:n], gate[q % 2][1][:, 0:n]
                    link.mark(v.tensor_tensor(ga, ga, b_ps[q % 2][0][:, 0:n], ALU.mult))
                    link(v.tensor_tensor(gb, gb, b_ps[q % 2][1][:, 0:n], ALU.mult))
                    v.tensor_tensor(mt[k % 2][:, t0:t0 + n], ga, gb, ALU.add).then_inc(sums_done, 1)
                    side.dve(q + 1, NSL * KD)

        @block.gpsimd
        def _(pool):
            side.pool(1, 1)


class Nothing:

    def dve(self, done, total):
        pass

    act = pool = dve

    def stage(self, build):
        pass

    def store(self, sp):
        pass


class Side:

    LAG = 2

    def __init__(self, nc, c, io, tiles, beside_last):
        self.nc, self.c, self.io, self.tiles, self.shares = nc, c, io, tiles, SHARES[beside_last]
        self.n = len(tiles)
        self.per_tile = SLOTS
        self.end = self.n * self.per_tile
        self.sems = Stage(nc, f"t{tiles[0]}_")
        sem = lambda n: self.sems.sem("side_" + n)
        self.landed = [sem(f"landed{r}") for r in range(RING)]
        self.dots_ready, self.gel_ready, self.coef_ready = sem("dots_ready"), sem("gel_ready"), sem("coef_ready")
        self.slot_used, self.chain = sem("slot_used"), sem("chain")
        self.root_asked, self.root_ready, self.y_ready, self.y_saved = (
            sem("root_asked"), sem("root_ready"), sem("y_ready"), sem("y_saved"))
        self.links = 0
        self.start = {"dve": 0, "act": 0, "pool": 0}
        self.at = dict(self.start)
        self.given = 0
        self.share = 0
        self.last = False
        self.closed = {"act": False, "dve": False}

    def stage(self, build):
        share, last = -(-self.end * self.shares[build] // 100), build is merge
        for e in self.at:
            self.start[e] = self.given
        self.start["ref"] = self.given
        self.given = min(self.end, self.given + share)
        self.share, self.last = share, last

    def due(self, e, done, total):
        if self.last and done == total:
            return self.end
        return min(self.end, self.start[e] + self.share * done // total)

    def where(self, b):
        i, k = divmod(b, self.per_tile)
        return i, k

    def pool(self, done, total):
        pool, c = self.nc.gpsimd, self.c
        ahead = RING - self.LAG
        to = min(self.end, self.due("ref", done, total) + ahead) if not self.last or done < total else self.end
        for b in range(self.at["pool"], to):
            i, s0 = self.where(b)
            if b >= RING:
                pool.wait_ge(self.slot_used, b - RING + 1)
            pool.indirect_dma_start(
                out=c["ring"][:, s0 % RING, :], out_offset=None, in_=self.io["experts"],
                in_offset=bass.IndirectOffsetOnAxis(ap=c["first_idx"][:, i, s0:s0 + 1], axis=0),
            ).then_inc(self.landed[s0 % RING], 16)
        self.at["pool"] = max(self.at["pool"], to)

    def act(self, done, total):
        act, c = self.nc.scalar, self.c
        to = self.due("act", done, total)
        for b in range(self.at["act"], to):
            i, s0 = self.where(b)
            r = slice(s0 % RING, s0 % RING + 1)
            act.wait_ge(self.dots_ready, b + 1)
            act.activation(c["dots"][:, r], c["dots"][:, r], ACT.Gelu).then_inc(self.gel_ready, 1)
            act.wait_ge(self.gel_ready, b + 1)
            act.activation(c["coef"][:, r], c["dots"][:, r], ACT.Copy,
                           scale=c["first_w"][:, i, s0:s0 + 1]).then_inc(self.coef_ready, 1)
            if s0 == 12 and i:
                self.root(i - 1)
        self.at["act"] = max(self.at["act"], to)
        if to == self.end and not self.closed["act"]:
            self.closed["act"] = True
            self.root(self.n - 1)

    def root(self, i):
        self.nc.scalar.wait_ge(self.root_asked, i + 1)
        sm = self.c["side_sm"][:, i:i + 1]
        self.nc.scalar.activation(sm, sm, ACT.Sqrt).then_inc(self.root_ready, 1)

    def sums(self, b):
        dve, c = self.nc.vector, self.c
        i, s0 = self.where(b)
        r = s0 % RING
        h = c["first_h"][:, i, :]
        dve.wait_ge(self.coef_ready, b + 1)
        if b:
            dve.wait_ge(self.slot_used, b)
        dve.scalar_tensor_tensor(out=h, in0=c["ring"][:, r, D:2 * D], scalar=c["coef"][:, r:r + 1], in1=h,
                                 op0=ALU.mult, op1=ALU.add).then_inc(self.slot_used, 1)

    def squares(self, i):
        dve, c = self.nc.vector, self.c
        h, sm = c["first_h"][:, i, :], c["side_sm"][:, i:i + 1]
        dve.wait_ge(self.slot_used, (i + 1) * SLOTS)
        dve.tensor_tensor_reduce(out=c["first_n2"][:, i, :], in0=h, in1=h, scale=1.0, scalar=0.0, op0=ALU.mult,
                                 op1=ALU.add, accum_out=sm).then_inc(self.chain, 1)
        self.links += 1
        dve.wait_ge(self.chain, self.links)
        dve.tensor_scalar(sm, sm, 1.0 / D, EPS, ALU.mult, ALU.add).then_inc(self.root_asked, 1)

    def scale(self, i):
        dve, c = self.nc.vector, self.c
        h, sm = c["first_h"][:, i, :], c["side_sm"][:, i:i + 1]
        dve.wait_ge(self.root_ready, i + 1)
        dve.reciprocal(sm, sm).then_inc(self.chain, 1)
        self.links += 1
        dve.wait_ge(self.chain, self.links)
        dve.scalar_tensor_tensor(out=h, in0=h, scalar=sm, in1=c["norm_f"][:], op0=ALU.mult, op1=ALU.mult
                                 ).then_inc(self.y_ready, 1)

    def dve(self, done, total):
        dve, c = self.nc.vector, self.c
        to = self.due("dve", done, total)
        for b in range(self.at["dve"], to):
            i, s0 = self.where(b)
            r = s0 % RING
            u = c["ring"][:, r, 0:D]
            dve.wait_ge(self.landed[r], 16 * (b // RING + 1))
            dve.tensor_tensor_reduce(out=u, in0=u, in1=c["first_n2"][:, i, :], scale=1.0, scalar=0.0, op0=ALU.mult,
                                     op1=ALU.add, accum_out=c["dots"][:, r:r + 1]).then_inc(self.dots_ready, 1)
            if b >= self.LAG:
                self.sums(b - self.LAG)
            if i and s0 == 8:
                self.squares(i - 1)
            if i and s0 == 16:
                self.scale(i - 1)
        self.at["dve"] = max(self.at["dve"], to)
        if to == self.end and not self.closed["dve"]:
            self.closed["dve"] = True
            for b in range(self.end - self.LAG, self.end):
                self.sums(b)
            self.squares(self.n - 1)
            self.scale(self.n - 1)

    def store(self, sp):
        for i, t in enumerate(self.tiles):
            sp.wait_ge(self.y_ready, i + 1)
            sp.dma_start(self.io["y"][t * P:(t + 1) * P, :], self.c["first_h"][:, i, :]).then_inc(self.y_saved, 16)
        sp.wait_ge(self.y_saved, 16 * self.n)


class Front:

    AT_H, AT_ADD, AT_ROOT, AT_N2, AT_N2T, AT_Q, AT_QN, AT_QT, AT_S = (1, 3), 5, 7, 9, 11, (13, 15), 16, 18, 20
    AT_KEYS, AT_COMB, AT_BEST, AT_EXP, AT_ROWS, AT_IDX, AT_W = 23, 34, 36, 47, 49, 59, 60

    LINKS = 1 + 5 * 2 * HP + 2 + 5 * HP + 2 * (3 + 1 + 1) + 1 + 2

    def __init__(self, nc, m, banks, top, io, c, name, lo, to, begun):
        self.nc, self.io, self.c, self.lo, self.to, self.begun = nc, io, c, lo, to, begun
        self.w_out_count = 16 if lo == 0 else 32
        self.own = lambda i: i if begun else i + 1
        self.w_out = m.sb("w_out", [P, KD, D])
        self.w_q = m.sb("w_q", [P, KD, D])
        self.keys = m.sb("keys", [P, HP, NK])
        self.norm2 = m.sb("norm2", [P, D])
        self.xt = m.sb("xt", [P, D])
        self.mts = m.sb("mts", [P, KD, P])
        self.n2t = m.sb("n2t", [P, KD, P])
        self.work = m.sb("work", [P, 2 * HP * NK])
        self.comb = m.sb("comb", [P, HP, TOPK * TOPK])
        flat = (self.comb if begun else m.sb("queries", [P, HP, TOPK * TOPK])).rearrange("p h n -> p (h n)")
        self.qn = flat[:, 0:D]
        self.qt = flat[:, D:2 * D].rearrange("p (h t) -> p h t", h=HP)
        self.s16 = m.sb("s16", [P, HP, 2, TOPK])
        self.i16 = m.sb("i16", [P, HP, 2, TOPK], U32)
        self.i16f = m.sb("i16f", [P, HP, 2, TOPK])
        self.cs = m.sb("cs", [P, HP, TOPK])
        self.ci = m.sb("ci", [P, HP, TOPK], U32)
        self.cd = m.sb("cd", [P, HP, TOPK], U32)
        self.cf = m.sb("cf", [P, HP, TOPK])
        self.ee = [m.sb(f"ee{x}", [P, SLOTS]) for x in range(2)]
        self.zz = m.sb("zz", [P, HP])
        self.sm = m.sb("f_sm", [P, 2])
        self.a_ps = banks.ps(name + "a_ps", [P, D])
        self.s_ps = banks.ps(name + "s_ps", [P, 2, HP, NK])
        self.t_ps = self.s_ps[:, 0] if begun else banks.ps(name + "t_ps", [P, HP, P])

        sem = lambda n: top.sem(name + n)
        self.w_out_landed, self.w_q_landed, self.in_landed = sem("w_out_landed"), sem("w_q_landed"), sem("in_landed")
        self.h_done, self.h_ready, self.sq_done, self.ms_ready, self.rms_ready = (
            sem("h_done"), sem("h_ready"), sem("sq_done"), sem("ms_ready"), sem("rms_ready"))
        self.n2_ready, self.n2_turned, self.n2t_ready, self.q_done, self.q_ready, self.q_turned = (
            sem("n2_ready"), sem("n2_turned"), sem("n2t_ready"), sem("q_done"), sem("q_ready"), sem("q_turned"))
        self.qt_ready, self.s_done, self.e_ready, self.e_done, self.idx_ready, self.w_ready = (
            sem("qt_ready"), sem("s_done"), sem("e_ready"), sem("e_done"), sem("idx_ready"), sem("w_ready"))
        self.h_taken, self.idx_taken = sem("h_taken"), sem("idx_taken")
        self.chain, self.sp_held, self.dve_held = sem("chain"), sem("sp_held"), sem("dve_held")

    def load_weights(self, sp, w_out=True):
        io = self.io
        if w_out:
            sp.dma_start(self.w_out, io["w_out"]).then_inc(self.w_out_landed, 16)
        sp.dma_start(self.norm2, io["norm2"].to_broadcast([P, D])).then_inc(self.w_out_landed, 16)
        sp.dma_start(self.keys, io["keys"]).then_inc(self.w_q_landed, 16)
        sp.dma_start(self.w_q, io["w_query"]).then_inc(self.w_q_landed, 16)

    def load(self, sp, i, R, first=False):
        if not first:
            hold(sp, self.h_ready, self.own(i - 1), self.sp_held)
        tok = bass.ds(i * P + self.lo * P, R)
        sp.dma_start(self.xt[0:R, :], self.io["x"][tok, :]).then_inc(self.in_landed, 16)
        sp.dma_start(self.mts[:, :, 0:R], self.io["mt"][:, :, tok].rearrange("k p t -> p k t")
                     ).then_inc(self.in_landed, 16)

    def weights(self, i, R):
        return self.to(i, "w")[0:R].rearrange("p (h s) -> p h s", h=HP)

    def pe_steps(self, pe):
        def product(lhs, rhs, R, ks):
            for k in ks:
                for n in range(2):
                    last = self.nc.tensor.matmul(self.a_ps[0:R, n * 512:(n + 1) * 512], lhs[:, k, 0:R],
                                            rhs[:, k, n * 512:(n + 1) * 512],
                                            start=(k == 0), stop=(k == KD - 1))
            return last

        def h_part(part):
            def step(i, R):
                if part == 0:
                    pe.wait_ge(self.w_out_landed, self.w_out_count)
                    pe.wait_ge(self.in_landed, 32 * self.own(i))
                last = product(self.mts, self.w_out, R, range(4 * part, 4 * part + 4))
                if part:
                    last.then_inc(self.h_done, 1)
            return step

        def turn_n2(i, R):
            pe.wait_ge(self.n2_ready, self.own(i))
            for k in range(KD):
                last = self.nc.tensor.transpose(self.t_ps[:, k, 0:R], self.to(i, "n2")[0:R, k * P:(k + 1) * P],
                                                self.c["ident"][0:R, 0:R])
            last.then_inc(self.n2_turned, 1)

        def q_part(part):
            def step(i, R):
                if part == 0:
                    pe.wait_ge(self.w_q_landed, 16 * 2)
                    pe.wait_ge(self.n2t_ready, self.own(i))
                last = product(self.n2t, self.w_q, R, range(4 * part, 4 * part + 4))
                if part:
                    last.then_inc(self.q_done, 1)
            return step

        def turn_q(i, R):
            pe.wait_ge(self.q_ready, self.own(i))
            for k in range(HP):
                last = self.nc.tensor.transpose(self.t_ps[:, k, 0:R], self.qn[0:R, k * P:(k + 1) * P],
                                                self.c["ident"][0:R, 0:R])
            last.then_inc(self.q_turned, 1)

        def scores(i, R):
            pe.wait_ge(self.qt_ready, self.own(i))
            if not self.begun and i:
                pe.wait_ge(self.e_ready, i)
            for k in range(HP):
                for x in range(2):
                    s = slice(x * DH, (x + 1) * DH)
                    last = self.nc.tensor.matmul(self.s_ps[0:R, x, k, :], self.qt[s, k, 0:R], self.keys[s, k, :],
                                            start=True, stop=True)
            last.then_inc(self.s_done, 1)

        return [(self.AT_H[0], h_part(0)), (self.AT_H[1], h_part(1)), (self.AT_N2T, turn_n2), (self.AT_Q[0], q_part(0)),
                 (self.AT_Q[1], q_part(1)), (self.AT_QT, turn_q), (self.AT_S, scores)]

    def act_steps(self, act):
        def squares(i, R):
            act.wait_ge(self.h_ready, self.own(i))
            self.nc.scalar.activation(self.to(i, "n2")[0:R, :], self.to(i, "h")[0:R, :], ACT.Square, accum_out=self.sm[0:R, 0:1]
                                 ).then_inc(self.sq_done, 1)

        def root(i, R):
            act.wait_ge(self.ms_ready, self.own(i))
            self.nc.scalar.activation(self.sm[0:R, 1:2], self.sm[0:R, 1:2], ACT.Sqrt).then_inc(self.rms_ready, 1)

        def take_n2t(i, R):
            act.wait_ge(self.n2_turned, self.own(i))
            self.nc.scalar.copy(self.n2t[:, :, 0:R], self.t_ps[:, :, 0:R]).then_inc(self.n2t_ready, 1)

        def take_q(i, R):
            act.wait_ge(self.q_done, self.own(i))
            self.nc.scalar.copy(self.qn[0:R, :], self.a_ps[0:R, :]).then_inc(self.q_ready, 1)

        def take_qt(i, R):
            act.wait_ge(self.q_turned, self.own(i))
            self.nc.scalar.copy(self.qt[:, :, 0:R], self.t_ps[:, :, 0:R]).then_inc(self.qt_ready, 1)

        def exps(i, R):
            act.wait_ge(self.e_ready, self.own(i))
            self.nc.scalar.activation(self.weights(i, R), self.weights(i, R), ACT.Exp).then_inc(self.e_done, 1)

        return [(self.AT_ADD, squares), (self.AT_ROOT, root), (self.AT_N2T, take_n2t), (self.AT_QN, take_q),
                 (self.AT_QT, take_qt), (self.AT_EXP, exps)]

    def dve_steps(self, dve):
        v = self.nc.vector
        links = {}
        overlapping = Chain(dve, self.chain)

        def link_of(i):
            if not self.begun:
                return overlapping
            if id(i) not in links:
                links[id(i)] = (Chain(dve, self.chain, (i - 1) * self.LINKS if not isinstance(i, int) or i > 1
                                      else 0), i)
            return links[id(i)][0]

        def add(i, R):
            dve.wait_ge(self.w_out_landed, self.w_out_count)
            dve.wait_ge(self.h_done, self.own(i))
            dve.wait_ge(self.in_landed, 32 * self.own(i))
            if self.begun:
                dve.wait_ge(self.h_taken, i)
            v.tensor_tensor(self.to(i, "h")[0:R, :], self.a_ps[0:R, :], self.xt[0:R, :], ALU.add).then_inc(self.h_ready, 1)

        def means(i, R):
            dve.wait_ge(self.sq_done, self.own(i))
            v.tensor_scalar(self.sm[0:R, 1:2], self.sm[0:R, 0:1], 1.0 / D, EPS, ALU.mult, ALU.add).then_inc(self.ms_ready, 1)

        def norm(i, R):
            link = link_of(i)
            dve.wait_ge(self.rms_ready, self.own(i))
            link(v.reciprocal(self.sm[0:R, 1:2], self.sm[0:R, 1:2]))
            v.scalar_tensor_tensor(out=self.to(i, "n2")[0:R, :], in0=self.to(i, "h")[0:R, :], scalar=self.sm[0:R, 1:2],
                                   in1=self.norm2[0:R, :], op0=ALU.mult, op1=ALU.mult).then_inc(self.n2_ready, 1)

        def top16(stage, lists, values, spare, best, where, guard):
            def step(i, R):
                link = link_of(i)
                guard(i)
                if link.n:
                    hold(dve, self.chain, link.base + link.n, self.dve_held)
                lo, hi = slice(0, 8), slice(8, 16)
                for n in range(lists):
                    if stage == 0:
                        ins = v.max(best(n)[0:R, lo], values(n)[0:R])
                    elif stage == 1:
                        ins = v.max_index(where(n)[0:R, lo], best(n)[0:R, lo], values(n)[0:R])
                    elif stage == 2:
                        ins = v.match_replace(spare(n)[0:R], best(n)[0:R, lo], values(n)[0:R], LOWEST)
                    elif stage == 3:
                        ins = v.max(best(n)[0:R, hi], spare(n)[0:R])
                    else:
                        ins = v.max_index(where(n)[0:R, hi], best(n)[0:R, hi], spare(n)[0:R])
                    link.mark(ins)
            return step

        keys_top = [top16(s, 2 * HP, lambda n: self.s_ps[:, n % 2, n // 2, :], lambda n: self.work[:, n * NK:(n + 1) * NK],
                          lambda n: self.s16[:, n // 2, n % 2, :], lambda n: self.i16[:, n // 2, n % 2, :],
                          (lambda i: hold(dve, self.s_done, self.own(i), self.dve_held)) if s == 0 else (lambda i: None))
                    for s in range(5)]
        best_top = [top16(s, HP, lambda n: self.comb[:, n, :], lambda n: self.work[:, n * 256:(n + 1) * 256],
                          lambda n: self.cs[:, n, :], lambda n: self.ci[:, n, :], lambda i: None) for s in range(5)]

        def combine(i, R):
            link = link_of(i)
            link.wait()
            shape = [R, HP, TOPK, TOPK]
            link.mark(v.tensor_copy(self.i16f[0:R], self.i16[0:R]))
            c4 = self.comb[0:R].rearrange("p h (a b) -> p h a b", a=TOPK)
            link.mark(v.tensor_tensor(c4, bcast(self.s16[0:R, :, 0, :], shape, 3), bcast(self.s16[0:R, :, 1, :], shape, 2),
                                      ALU.add))

        def less_top(i, R):
            link = link_of(i)
            link.wait()
            v.tensor_tensor(self.weights(i, R), self.cs[0:R], self.cs[0:R, :, 0:1].to_broadcast([R, HP, TOPK]), ALU.subtract
                            ).then_inc(self.e_ready, 1)

        def half_rows(x, part):
            def step(i, R):
                link = link_of(i)
                link.wait()
                onehot = self.work[0:R, :].rearrange("p (h s k) -> p h s k", h=HP, s=TOPK)
                onehot3 = self.work[0:R, :].rearrange("p (n k) -> p n k", k=TOPK)
                if part == 0:
                    if x == 0:
                        link(v.tensor_scalar(self.cd[0:R], self.ci[0:R], 4, None, ALU.logical_shift_right))
                    else:
                        link(v.tensor_scalar(self.cd[0:R], self.ci[0:R], TOPK - 1, None, ALU.bitwise_and))
                    link(v.tensor_copy(self.cf[0:R], self.cd[0:R]))
                    link.mark(v.tensor_tensor(
                        onehot3, bcast(self.cf[0:R].rearrange("p h s -> p (h s)"), [R, SLOTS, TOPK], 2),
                        bcast(self.c["iota"][0:R, :], [R, SLOTS, TOPK], 1), ALU.is_equal))
                elif part == 1:
                    link.mark(v.tensor_tensor(onehot, onehot, bcast(self.i16f[0:R, :, x, :], [R, HP, TOPK, TOPK], 2),
                                              ALU.mult))
                else:
                    link.mark(v.tensor_reduce(self.ee[x][0:R, :], onehot3, AX_X, ALU.add))
            return step

        def row_numbers(i, R):
            link = link_of(i)
            link.wait()
            link(v.scalar_tensor_tensor(out=self.ee[0][0:R, :], in0=self.ee[0][0:R, :], scalar=float(NK),
                                        in1=self.ee[1][0:R, :], op0=ALU.mult, op1=ALU.add))
            if self.begun:
                dve.wait_ge(self.idx_taken, 2 * i)
            v.tensor_copy(self.to(i, "idx")[0:R, :], self.ee[0][0:R, :]).then_inc(self.idx_ready, 1)

        def weights(i, R):
            link = link_of(i)
            dve.wait_ge(self.e_done, self.own(i))
            link(v.tensor_reduce(self.zz[0:R, :], self.weights(i, R), AX_X, ALU.add))
            link(v.reciprocal(self.zz[0:R, :], self.zz[0:R, :]))
            v.tensor_tensor(self.weights(i, R), self.weights(i, R), bcast(self.zz[0:R, :], [R, HP, TOPK], 2), ALU.mult
                            ).then_inc(self.w_ready, 1)
            assert not self.begun or link.n == self.LINKS

        front = [(self.AT_ADD, add), (self.AT_ROOT, means), (self.AT_N2, norm)]
        front += [(self.AT_KEYS + 2 * s, keys_top[s]) for s in range(5)] + [(self.AT_COMB, combine)]
        front += [(self.AT_BEST + 2 * s, best_top[s]) for s in range(5)] + [(self.AT_EXP, less_top)]
        front += [(self.AT_ROWS + 3 * x + p, half_rows(x, p)) for x in range(2) for p in range(3)]
        front += [(self.AT_IDX, row_numbers), (self.AT_W, weights)]
        self.links = links
        return front


def fronts(nc, top, io, c, g, handed_tile):
    NG = len(g.tiles)
    with ExitStack() as st:
        m, banks = Region(c["arena"], c["free"]), Banks(nc, st)
        w_out_at = Region(c["arena"], c["free"])
        handed = w_out_at.sb("handed", [P, HANDED])
        last_to = parts_of(handed)
        to = lambda i, what: last_to[what] if g.lo + i == handed_tile else c["first_" + what][:, i, :]
        f = Front(nc, m, banks, top, io, c, g.name + "f_", g.lo, to, False)
        norm_f_landed = top.sem("f_norm_f_landed")
        handed_saved = top.sem("f_handed_saved")
        block = st.enter_context(nc.Block())

        @block.sync
        def _(sp):
            for i in range(NG):
                f.load(sp, i, P, i == 0)
                if i == 0:
                    f.load_weights(sp, g.lo > 0)
                    sp.dma_start(c["norm_f"], io["norm_f"].to_broadcast([P, D])).then_inc(norm_f_landed, 16)
            sp.wait_ge(norm_f_landed, 16)
            if handed_tile is not None:
                sp.wait_ge(f.idx_ready, NG)
                sp.wait_ge(f.w_ready, NG)
                sp.dma_start(io["handed"], handed).then_inc(handed_saved, 16)
                sp.wait_ge(handed_saved, 16)

        @block.tensor
        def _(pe):
            steps = f.pe_steps(pe)
            for i in range(NG):
                for _, step in steps:
                    step(i, P)

        @block.scalar
        def _(act):
            *early, (_, exps) = f.act_steps(act)
            for i in range(NG + 1):
                if i < NG:
                    for _, step in early:
                        step(i, P)
                if i:
                    exps(i - 1, P)

        @block.vector
        def _(dve):
            steps = [step for _, step in f.dve_steps(dve)]
            early, late = steps[:3], steps[3:]
            for step in early:
                step(0, P)
            for i in range(NG):
                for n, step in enumerate(late):
                    step(i, P)
                    if n in (0, 2, 4) and i + 1 < NG:
                        early[n // 2](i + 1, P)


def experts(nc, top, io, c, lo):
    ident = c["ident"]
    BATCH = 2
    NB = SLOTS // BATCH
    N = NP - lo
    with ExitStack() as st:
        m, banks = Region(c["arena"]), Banks(nc, st)
        handed = m.sb("handed", [P, HANDED])
        next_of = parts_of(handed)
        h_next, n2_next, idx_next, w_next = (next_of[n] for n in ("h", "n2", "idx", "w"))
        f = Front(nc, m, banks, top, io, c, "x_", lo, lambda i, what: next_of[what], True)
        s_ps, a_ps = f.s_ps, f.a_ps
        in_landed, h_taken, idx_taken, idx_ready, w_ready = f.in_landed, f.h_taken, f.idx_taken, f.idx_ready, f.w_ready
        norm_f = m.sb("norm_f", [P, D])
        h_cur = m.sb("h_cur", [P, D])
        n2_cur = m.sb("n2_cur", [P, D])
        idx_cur = m.sb("idx_cur", [P, SLOTS], U32)
        w_cur = m.sb("w_cur", [P, SLOTS])
        sm = m.sb("sm", [P, 2])
        dots = m.sb("dots", [P, RING])
        gel = m.sb("gel", [P, RING])
        diag = m.sb("diag", [P, RING, P])
        ring = m.sb("ring", [P, RING, 2 * D])
        idx_s = m.sb("idx_s", [P, NS], U32)
        w_s = m.sb("w_s", [P, NS])
        coef_s = m.sb("coef_s", [P, NS, NS])
        acc = banks.ps("x_acc", [P, D])

        sem = lambda n: top.sem("x_" + n)
        landed = [sem(f"landed{j}") for j in range(RING)]
        norm_f_landed, handed_landed = sem("norm_f_landed"), sem("handed_landed")
        dots_ready, gel_ready, diag_ready, slot_used = (
            sem("dots_ready"), sem("gel_ready"), sem("diag_ready"), sem("slot_used"))
        cur_taken, sum_ready, fsq_done, fms_ready, frms_ready, y_ready, y_saved = (
            sem("cur_taken"), sem("sum_ready"), sem("fsq_done"), sem("fms_ready"),
            sem("frms_ready"), sem("y_ready"), sem("y_saved"))
        s_turned, s_idx_ready, s_spread, s_coef_ready, s_used = (
            sem("s_turned"), sem("s_idx_ready"), sem("s_spread"), sem("s_coef_ready"), sem("s_used"))
        fin_chain, s_chain, pool_held, sp_held, dve_held = (
            sem("fin_chain"), sem("s_chain"), sem("pool_held"), f.sp_held, f.dve_held)
        block = st.enter_context(nc.Block())

        def later(front):
            return [(12 + at * 52 // NB, step) for at, step in front]

        def slots_with_front(i, R, batch, front):
            following = i + 1
            for b in range(NB):
                batch(b)
                for at, step in front:
                    if at == b:
                        step(following, R)

        @block.sync
        def _(sp):
            sp.dma_start(handed, io["handed"]).then_inc(handed_landed, 16)
            f.load_weights(sp)
            sp.dma_start(norm_f, io["norm_f"].to_broadcast([P, D])).then_inc(norm_f_landed, 16)

            def store(i, R):
                hold(sp, y_ready, i + 1, sp_held)
                sp.dma_start(io["y"][bass.ds(i * P + lo * P, R), :], h_cur[0:R, :]).then_inc(y_saved, 16)

            f.load(sp, 1, P, True)
            with sp.Fori(1, N - 1) as i:
                f.load(sp, i + 1, P)
                store(i - 1, P)
            f.load(sp, N, NS)
            store(N - 2, P)
            store(N - 1, P)
            store(N, NS)
            sp.wait_ge(norm_f_landed, 16)
            sp.wait_ge(y_saved, 16 * (N + 1))

        @block.gpsimd
        def _(pool):
            def gather(r, rows_at, n=P):
                nc.gpsimd.indirect_dma_start(
                    out=ring[:, r, :], out_offset=None, in_=io["experts"],
                    in_offset=bass.IndirectOffsetOnAxis(ap=rows_at, axis=0)).then_inc(landed[r], 16)

            def copy_rows(i, lo, hi, n):
                nc.gpsimd.tensor_copy(idx_cur[:, lo:hi], idx_next[:, lo:hi]).then_inc(idx_taken, 1)
                hold(pool, idx_taken, 2 * i + n, pool_held)

            def take(i):
                if isinstance(i, int):
                    pool.wait_ge(handed_landed, 16)
                else:
                    hold(pool, idx_ready, i, pool_held)
                copy_rows(i, 0, SLOTS - RING, 1)

            def tile(i, first=False):
                for s in range(SLOTS):
                    if s % BATCH == 0 and not (first and s < RING):
                        hold(pool, slot_used, i * NB + (s - RING) // BATCH + 1, pool_held)
                    if s == SLOTS - RING:
                        copy_rows(i, SLOTS - RING, SLOTS, 2)
                    gather(s % RING, idx_cur[:, s:s + 1])

            take(0)
            tile(0, True)
            with pool.Fori(1, N) as i:
                take(i)
                tile(i)
            pool.wait_ge(s_idx_ready, 1)
            for b in range(NS):
                if b % BATCH == 0:
                    pool.wait_ge(slot_used, N * NB + (b - RING) // BATCH + 1)
                gather(b % RING, idx_s[:, b:b + 1])

        @block.tensor
        def _(pe):

            front = f.pe_steps(pe)

            def peer(i, R, front):
                def sums(b):
                    pe.wait_ge(diag_ready, (i * NB + b + 1) * BATCH)
                    for s in range(b * BATCH, (b + 1) * BATCH):
                        for n in range(2):
                            last = nc.tensor.matmul(acc[:, n * 512:(n + 1) * 512], diag[:, s % RING, :],
                                                    ring[:, s % RING, D + n * 512:D + (n + 1) * 512],
                                                    start=(s == 0), stop=(s == SLOTS - 1))
                    last.then_inc(slot_used, 1)

                slots_with_front(i, R, lambda b: sums(b - 1) if b else None, front)
                sums(NB - 1)

            peer(0, P, later(front))
            with pe.Fori(1, N - 1) as i:
                pe.wait_ge(sum_ready, i)
                peer(i, P, front)
            pe.wait_ge(sum_ready, N - 1)
            peer(N - 1, NS, front)
            pe.wait_ge(idx_ready, N)
            pe.wait_ge(w_ready, N)
            nc.tensor.transpose(s_ps[:, 0, 0, 0:NS], f.ee[0][0:NS, :], ident[0:NS, 0:NS])
            nc.tensor.transpose(s_ps[:, 0, 1, 0:NS], w_next[0:NS, :],
                                ident[0:NS, 0:NS]).then_inc(s_turned, 1)
            spread = [a_ps[:], s_ps[:, 1].rearrange("p h n -> p (h n)")]
            for b in range(NS):
                if b >= 2:
                    pe.wait_ge(dots_ready, N * NB + b - 1)
                for n in range(2):
                    last = nc.tensor.matmul(spread[b % 2][:, n * 512:(n + 1) * 512], c["pick"][:, b, :],
                                            n2_next[0:NS, n * 512:(n + 1) * 512], start=True, stop=True)
                last.then_inc(s_spread, 1)
            pe.wait_ge(sum_ready, N)
            for b in range(NS):
                pe.wait_ge(s_coef_ready, b + 1)
                for n in range(2):
                    last = nc.tensor.matmul(acc[0:NS, n * 512:(n + 1) * 512], coef_s[:, b, :],
                                            ring[:, b, D + n * 512:D + (n + 1) * 512],
                                            start=(b == 0), stop=(b == NS - 1))
            last.then_inc(s_used, 1)

        @block.scalar
        def _(act):
            front = f.act_steps(act)

            spare = f.comb.rearrange("p h n -> p (h n)")[:, 0:D]

            def last_squares(i, R):
                act.wait_ge(sum_ready, i + 1)
                nc.scalar.activation(spare[0:R, :], h_cur[0:R, :], ACT.Square, accum_out=sm[0:R, 0:1]
                                     ).then_inc(fsq_done, 1)

            def last_root(i, R):
                act.wait_ge(fms_ready, i + 1)
                nc.scalar.activation(sm[0:R, 1:2], sm[0:R, 1:2], ACT.Sqrt).then_inc(frms_ready, 1)

            before = [(0, lambda i, R: last_squares(i - 2, P)), (1, lambda i, R: last_root(i - 2, P))]

            def finish(i, R):
                last_squares(i, R)
                last_root(i, R)

            def gelus(i):
                def batch(b):
                    r = slice(b * BATCH % RING, b * BATCH % RING + BATCH)
                    act.wait_ge(dots_ready, i * NB + b + 1)
                    nc.scalar.activation(gel[:, r], dots[:, r], ACT.Gelu).then_inc(gel_ready, 1)
                return batch

            slots_with_front(0, P, gelus(0), later(front))
            with act.Fori(1, N - 1) as i:
                slots_with_front(i, P, gelus(i), before + front)
            slots_with_front(N - 1, NS, gelus(N - 1), before + front)
            finish(N - 1, P)
            for b in range(NS):
                act.wait_ge(dots_ready, N * NB + b + 1)
                nc.scalar.activation(gel[:, b:b + 1], dots[:, b:b + 1], ACT.Gelu).then_inc(gel_ready, 1)
            finish(N, NS)

        @block.vector
        def _(dve):
            v = nc.vector
            front = f.dve_steps(dve)

            def take(i):
                if not (isinstance(i, int) and i == 0):
                    dve.wait_ge(w_ready, i)
                    dve.wait_ge(diag_ready, i * SLOTS)
                v.tensor_copy(n2_cur[:], n2_next[:]).then_inc(cur_taken, 1)
                v.tensor_copy(w_cur[:], w_next).then_inc(cur_taken, 1)
                hold(dve, cur_taken, 2 * i + 2, dve_held)

            def take_h(i):
                if not (isinstance(i, int) and i == 0):
                    dve.wait_ge(y_saved, 16 * i)
                v.tensor_copy(h_cur[:], h_next[:]).then_inc(h_taken, 1)
                hold(dve, h_taken, i + 1, dve_held)

            def peer(i, R, front):
                def diags(b):
                    dve.wait_ge(gel_ready, i * NB + b + 1)
                    for s in range(b * BATCH, (b + 1) * BATCH):
                        v.tensor_scalar(diag[:, s % RING, :], ident[:], gel[:, s % RING:s % RING + 1],
                                        w_cur[:, s:s + 1], ALU.mult, ALU.mult).then_inc(diag_ready, 1)

                def batch(b):
                    for s in range(b * BATCH, (b + 1) * BATCH):
                        r = s % RING
                        dve.wait_ge(landed[r], 16 * (i * (SLOTS // RING) + s // RING + 1))
                        ins = v.tensor_tensor_reduce(out=ring[:, r, 0:D], in0=ring[:, r, 0:D], in1=n2_cur[:],
                                                     scale=1.0, scalar=0.0, op0=ALU.mult, op1=ALU.add,
                                                     accum_out=dots[:, r:r + 1])
                    ins.then_inc(dots_ready, 1)
                    if b:
                        diags(b - 1)

                slots_with_front(i, R, batch, front)
                diags(NB - 1)

            def add_sums(i, R):
                v.tensor_tensor(h_cur[0:R, :], acc[0:R, :], h_cur[0:R, :], ALU.add).then_inc(sum_ready, 1)

            def last_means(i, R):
                dve.wait_ge(fsq_done, i + 1)
                v.tensor_scalar(sm[0:R, 1:2], sm[0:R, 0:1], 1.0 / D, EPS, ALU.mult, ALU.add).then_inc(fms_ready, 1)

            def last_norm(i, R):
                dve.wait_ge(frms_ready, i + 1)
                v.reciprocal(sm[0:R, 1:2], sm[0:R, 1:2]).then_inc(fin_chain, 1)
                dve.wait_ge(fin_chain, i + 1)
                v.scalar_tensor_tensor(out=h_cur[0:R, :], in0=h_cur[0:R, :], scalar=sm[0:R, 1:2],
                                       in1=norm_f[0:R, :], op0=ALU.mult, op1=ALU.mult).then_inc(y_ready, 1)

            before = [(1, lambda i, R: last_means(i - 2, P)), (2, lambda i, R: last_norm(i - 2, P)),
                      (4, lambda i, R: take_h(i - 1))]

            def finish(i, R):
                add_sums(i, R)
                last_means(i, R)
                last_norm(i, R)

            dve.wait_ge(handed_landed, 16)
            take(0)
            take_h(0)
            peer(0, P, later(front))
            f.links.clear()
            dve.wait_ge(norm_f_landed, 16)
            take(1)
            dve.wait_ge(slot_used, NB)
            add_sums(0, P)
            with dve.Fori(1, N - 1) as i:
                peer(i, P, before + front)
                take(i + 1)
                dve.wait_ge(slot_used, (i + 1) * NB)
                add_sums(i, P)
            f.links.clear()
            peer(N - 1, NS, before + front)
            dve.wait_ge(slot_used, N * NB)
            finish(N - 1, P)
            link = Chain(dve, s_chain)
            dve.wait_ge(s_turned, 1)
            link.mark(v.tensor_copy(w_s[:], s_ps[:, 0, 1, 0:NS]))
            link.mark(v.memset(coef_s[:], 0.0))
            v.tensor_copy(idx_s[:], s_ps[:, 0, 0, 0:NS]).then_inc(s_idx_ready, 1)
            link.wait()
            spread = [a_ps[:], s_ps[:, 1].rearrange("p h n -> p (h n)")]
            for b in range(NS):
                dve.wait_ge(s_spread, b + 1)
                dve.wait_ge(landed[b], 16 * (N * SLOTS // RING + 1))
                v.tensor_tensor_reduce(out=ring[:, b, 0:D], in0=ring[:, b, 0:D], in1=spread[b % 2], scale=1.0,
                                       scalar=0.0, op0=ALU.mult, op1=ALU.add, accum_out=dots[:, b:b + 1]
                                       ).then_inc(dots_ready, 1)
            for b in range(NS):
                dve.wait_ge(gel_ready, N * NB + b + 1)
                v.tensor_tensor(coef_s[:, b, b:b + 1], gel[:, b:b + 1], w_s[:, b:b + 1], ALU.mult
                                ).then_inc(s_coef_ready, 1)
            dve.wait_ge(y_saved, 16 * N)
            v.tensor_copy(h_cur[0:NS, :], h_next[0:NS, :]).then_inc(h_taken, 1)
            dve.wait_ge(h_taken, N + 1)
            dve.wait_ge(s_used, 1)
            finish(N, NS)


def stage(nc, build, io, c, *more):
    sems = Stage(nc, more[0].name if more and isinstance(more[0], Group) else "")
    build(nc, sems, io, c, *more)
    sems.end()


def program(nc, io):
    with ExitStack() as st:
        top = Consts(nc, st)
        c = {
            "ident": top.sb("ident", [P, P]),
            "cmask": top.sb("cmask", [P, P]),
            "bmask": top.sb("bmask", [P, P]),
            "iota": top.sb("iota", [P, TOPK]),
            "pick": top.sb("pick", [NS, NS, P]),
            "own_token": top.sb("own_token", [64, NS]),
            "own_head": top.sb("own_head", [NS * H, H]),
            "sum_maps": top.sb("sum_maps", [64, NS * H]),
            "map_coef": top.sb("map_coef", [64, 1]),
            "neg_lam": top.sb("neg_lam", [P, 1]),
            "subln": top.sb("subln", [P, 1]),
            "gnorm": top.sb("gnorm", [P, 1]),
            "lb": top.sb("lb", [P, H]),
            "one_lb": top.sb("one_lb", [P, H]),
            "cache_rows": top.sb("cache_rows", [P, NS * PAGES], U32),
            "zero1": top.sb("zero1", [P, 1]),
            "zeros_i": top.sb("zeros_i", [P, 1]),
            "k_new": top.sb("k_new", [NS, 512]),
            "q_new": top.sb("q_new", [NS, 512]),
            "f_new": top.sb("f_new", [P, H, NS]),
            "qh_new": top.sb("qh_new", [P, H, NS]),
            "arena": top.sb("arena", [P, ARENA]),
        }
        scratch = {"xnt": [P, KD, T], "hqf": [2 * H, P, T], "ig": [T, 512], "gg": [T, 512], "oat": [P, H, T],
                   "obt": [P, H, T], "handed": [P, HANDED], "state_mid": [H, P, DV], "mt": [KD, P, T]}
        for name, shape in scratch.items():
            io[name] = nc.dram_tensor(name + "_scratch", shape, F32, kind="Internal").ap()
        stage(nc, normalise, io, c)

        kept = Region(c["arena"])
        c["qk"] = kept.sb("qk", [P, 2 * H, T])
        c["v"] = kept.sb("v", [P, NT, 512])
        for name, n, dt in (("h", D, F32), ("n2", D, F32), ("idx", SLOTS, U32), ("w", SLOTS, F32)):
            c["first_" + name] = kept.sb("first_" + name, [P, N_BESIDE, n], dt)
        c["norm_f"] = kept.sb("norm_f", [P, D])
        c["dots"] = kept.sb("dots", [P, RING])
        c["coef"] = kept.sb("coef", [P, RING])
        c["side_sm"] = kept.sb("side_sm", [P, N_BESIDE])
        beside = Nothing()
        for n, (lo, hi) in enumerate(GROUPS):
            g = Group("abc"[n] + "_", lo, hi)
            c["free"] = kept.at
            if n:
                ring = Region(c["arena"], kept.at)
                c["ring"] = ring.sb("ring", [P, RING, 2 * D])
                c["free"] = ring.at
            for build in BUILDS:
                if build is attend_sample and not g.sampled:
                    continue
                beside.stage(build)
                stage(nc, build, io, c, g, beside)
            if n:
                beside.sems.end()
            if not g.sampled:
                c["free"] = kept.at
                handed = g.hi - 1 if GROUPS[n + 1][1] == NT else None
                stage(nc, fronts, io, c, g, handed)
                tiles = range(g.lo, g.hi if handed is None else handed)
                beside = Side(nc, c, io, tiles, GROUPS[n + 1][1] == NT)
        stage(nc, experts, io, c, GROUPS[-1][0] - 1)


BUILDS = (project, attend_prompt, attend_sample, hgrn, hgrn_out, merge)
SHARES = {False: {project: 32, attend_prompt: 26, hgrn: 18, hgrn_out: 2, merge: 22},
          True: {project: 18, attend_prompt: 31, attend_sample: 15, hgrn: 20, hgrn_out: 3, merge: 13}}


def lay_out(inputs):
    import numpy as np

    a = {k: np.asarray(v) for k, v in inputs.items()}
    w_in = a["w_in"][0]
    cols = lambda lo, n: w_in[:, lo:lo + n]
    turned = np.concatenate([cols(0, 1024), cols(1536, 1024), cols(3584, 2048)], axis=1)
    by_rows = np.concatenate([cols(1024, 512), cols(2560, 1024)], axis=1)

    def chunks(w, n):
        k = w.shape[0] // P
        return w.reshape(k, P, w.shape[1] // n, n).transpose(2, 1, 0, 3)

    out = {
        "x": np.concatenate([a["x_prompt"].reshape(SEQ, D), a["x_sample"].reshape(NS, D)]),
        "norm1": a["norm1_w"].reshape(KD, P).T,
        "lam_w": np.concatenate([a["lambda_q1"], a["lambda_q2"], a["lambda_k1"], a["lambda_k2"]]).reshape(1, 4 * DH),
        "lb_w": a["lb_param"].reshape(2, H, P).transpose(2, 0, 1),
        "subln": a["subln_w"].reshape(P, 1),
        "gnorm": a["gnorm_w"].reshape(P, 1),
        "pages": a["page_table"].reshape(1, NS * PAGES),
        "w_t": chunks(turned, P),
        "w_n": chunks(by_rows, 512),
        "cache_k": a["cache_k"].reshape(-1, 512),
        "cache_v": a["cache_v"].reshape(-1, 512),
        "state": a["state_hgrn"][0].transpose(2, 0, 1, 3),
        "wa": chunks(a["w_branch_a"][0], P),
        "wb": chunks(a["w_branch_b"][0], P),
        "w_out": chunks(a["w_out"][0], D)[0],
        "w_query": chunks(a["w_query"][0], D)[0],
        "keys": a["sub_keys"][0].transpose(1, 3, 0, 2).reshape(P, HP, NK),
        "norm2": a["norm2_w"].reshape(1, D),
        "norm_f": a["norm_f_w"].reshape(1, D),
        "experts": np.concatenate([a["expert_u"][0], a["expert_v"][0]], axis=1),
    }
    return {k: np.ascontiguousarray(v) for k, v in out.items()}


OUTS = {
    "y": [T, D], "k_out": [T, 512], "v_out": [T, 512],
    "state_prompt": [H, P, DV], "state_sample": [P, NS, H, DV],
}


def kernel(**inputs):
    import numpy as np
    import concourse.bacc as bacc
    from concourse.bass_utils import run_bass_kernel_spmd

    nc = bacc.Bacc("TRN2", target_bir_lowering=False, num_devices=1)
    laid = lay_out(inputs)
    arrays = {f"in_{n}": a for n, a in laid.items()}
    io = {n: nc.dram_tensor(f"in_{n}", a.shape, mybir.dt.from_np(a.dtype), kind="ExternalInput").ap()
          for n, a in laid.items()}
    for n, shape in OUTS.items():
        io[n] = nc.dram_tensor(n, shape, F32, kind="ExternalOutput").ap()
    program(nc, io)
    r = run_bass_kernel_spmd(nc, [arrays], core_ids=[0]).results[0]
    y, k, v = (np.asarray(r[n]) for n in ("y", "k_out", "v_out"))
    return (y[:SEQ].reshape(1, SEQ, D), y[SEQ:].reshape(NS, 1, D),
            k[:SEQ].reshape(1, 1, SEQ, H, 2, DH), v[:SEQ].reshape(1, 1, SEQ, H, DV),
            np.asarray(r["state_prompt"]).reshape(1, 1, H, P, DV),
            k[SEQ:].reshape(1, NS, 1, H, 2, DH), v[SEQ:].reshape(1, NS, 1, H, DV),
            np.asarray(r["state_sample"]).transpose(1, 2, 0, 3).reshape(1, NS, H, P, DV))
```
